# Optimizing a Trainium2 kernel written in Bass

```python
import math
import jax, jax.numpy as jnp
from jax import lax
import numpy as np

D_MODEL = 1024
BATCH = 1
SEQ = 1024
DEPTH = 1

D_RNN = D_MODEL
RNN_BLOCKS = 8
RNN_BLOCK_W = D_RNN // RNN_BLOCKS
CONV_RNN = 4
RG_LRU_C = 8.0
DIFF_HEADS = 4
DIFF_HEAD_DIM = 64
DIFF_QK = DIFF_HEADS * 2 * DIFF_HEAD_DIM
DIFF_WIDTH = DIFF_HEADS * 2 * DIFF_HEAD_DIM
FOX_HEADS = 8
FOX_HEAD_DIM = 64
FOX_WIDTH = FOX_HEADS * FOX_HEAD_DIM
N_BUCKETS = 32
MAX_EXACT = N_BUCKETS // 2
MAX_DISTANCE = 128
Q_BLOCK = 128
D_FF = ((8 * D_MODEL // 3 + 127) // 128) * 128
CONV_FFN = 3
N_BRANCH = 3
EPS = 1e-6

IN_WIDTHS = (D_RNN, D_RNN, DIFF_QK, DIFF_QK, DIFF_WIDTH, FOX_WIDTH, FOX_WIDTH, FOX_WIDTH, FOX_HEADS, N_BRANCH * D_MODEL)
N_IN = int(sum(IN_WIDTHS))
IN_SPLITS = tuple(int(v) for v in np.cumsum(IN_WIDTHS)[:-1])


def rmsnorm(x, g):
    xf = x.astype(jnp.float32)
    y = xf * lax.rsqrt(jnp.mean(xf * xf, axis=-1, keepdims=True) + EPS)
    return (y * g.astype(jnp.float32)).astype(x.dtype)

def causal_dwconv(x, w, b):
    k = w.shape[0]
    s = x.shape[1]
    xp = jnp.pad(x, ((0, 0), (k - 1, 0), (0, 0)))
    y = b + xp[:, 0:s] * w[0]
    for j in range(1, k):
        y = y + xp[:, j:j + s] * w[j]
    return y

def _to_blocks(t):
    b, s = t.shape[:2]
    return jnp.moveaxis(t.reshape(b, s // Q_BLOCK, Q_BLOCK, *t.shape[2:]), 1, 0)

def _from_blocks(t):
    nb, b = t.shape[:2]
    t = jnp.moveaxis(t, 0, 1)
    return t.reshape(b, nb * Q_BLOCK, *t.shape[3:])

def t5_bucket(dist):
    n = jnp.maximum(dist, 0)
    nf = jnp.maximum(n, 1).astype(jnp.float32)
    large = MAX_EXACT + (jnp.log(nf / MAX_EXACT) / math.log(MAX_DISTANCE / MAX_EXACT)
                         * (N_BUCKETS - MAX_EXACT)).astype(jnp.int32)
    large = jnp.minimum(large, N_BUCKETS - 1)
    return jnp.where(n < MAX_EXACT, n, large)

def rg_lru(x, w_r, b_r, w_i, b_i, a_param):
    bsz, s, c = x.shape
    xb = x.reshape(bsz, s, RNN_BLOCKS, RNN_BLOCK_W)
    r = jax.nn.sigmoid(jnp.einsum('bsnc,ncd->bsnd', xb, w_r).reshape(bsz, s, c) + b_r)
    i = jax.nn.sigmoid(jnp.einsum('bsnc,ncd->bsnd', xb, w_i).reshape(bsz, s, c) + b_i)
    log_a = (-RG_LRU_C * r.astype(jnp.float32)) * jax.nn.softplus(-a_param.astype(jnp.float32))
    a = jnp.exp(log_a)
    u = jnp.sqrt(-jnp.expm1(2.0 * log_a)) * (i * x).astype(jnp.float32)

    def combine(left, right):
        a1, b1 = left
        a2, b2 = right
        return a1 * a2, a2 * b1 + b2

    _, h = lax.associative_scan(combine, (a, u), axis=1)
    return h.astype(x.dtype)

def diff_attention(q, k, v, lam, rel_table):
    s_len = q.shape[1]
    scale = DIFF_HEAD_DIM ** -0.5
    k_pos = jnp.arange(s_len)

    def one_block(args):
        qb, blk = args
        q_pos = blk * Q_BLOCK + jnp.arange(Q_BLOCK)
        dist = q_pos[:, None] - k_pos[None, :]
        bias = jnp.moveaxis(rel_table[t5_bucket(dist)], -1, 0)
        sc = jnp.einsum('bqhcd,bkhcd->bchqk', qb, k).astype(jnp.float32) * scale + bias.astype(jnp.float32)
        sc = jnp.where(dist >= 0, sc, -jnp.inf)
        p = jax.nn.softmax(sc, axis=-1)
        w = p[:, 0] - lam * p[:, 1]
        return jnp.einsum('bhqk,bkhd->bqhd', w.astype(v.dtype), v)

    out = lax.map(one_block, (_to_blocks(q), jnp.arange(s_len // Q_BLOCK)))
    return _from_blocks(out)

def forgetting_attention(q, k, v, log_f):
    s_len = q.shape[1]
    scale = FOX_HEAD_DIM ** -0.5
    k_pos = jnp.arange(s_len)
    c = jnp.cumsum(log_f.astype(jnp.float32), axis=1)
    ck = jnp.moveaxis(c, -1, 1)

    def one_block(args):
        qb, cq, blk = args
        q_pos = blk * Q_BLOCK + jnp.arange(Q_BLOCK)
        dist = q_pos[:, None] - k_pos[None, :]
        decay = jnp.moveaxis(cq, -1, 1)[..., None] - ck[:, :, None, :]
        sc = jnp.einsum('bqhd,bkhd->bhqk', qb, k).astype(jnp.float32) * scale + decay
        sc = jnp.where(dist >= 0, sc, -jnp.inf)
        p = jax.nn.softmax(sc, axis=-1)
        return jnp.einsum('bhqk,bkhd->bqhd', p.astype(v.dtype), v)

    out = lax.map(one_block, (_to_blocks(q), _to_blocks(c), jnp.arange(s_len // Q_BLOCK)))
    return _from_blocks(out)

def first_inputs(seed: int = 0) -> dict:
    key = jax.random.key(seed)
    ks = jax.random.split(key, 32)
    L = DEPTH

    def nrm(k, shape, scale):
        return jax.random.normal(k, shape, jnp.float32) * scale

    a_target = jax.random.uniform(ks[9], (L, D_RNN), jnp.float32, 0.9, 0.999)
    sig = a_target ** (1.0 / RG_LRU_C)
    return {
        "x": nrm(ks[0], (BATCH, SEQ, D_MODEL), 1.0),
        "norm1_g": 1.0 + nrm(ks[1], (L, D_MODEL), 0.02),
        "w_in": nrm(ks[2], (L, D_MODEL, N_IN), D_MODEL ** -0.5),
        "rnn_conv_w": nrm(ks[3], (L, CONV_RNN, D_RNN), CONV_RNN ** -0.5),
        "rnn_conv_b": nrm(ks[4], (L, D_RNN), 0.02),
        "rg_w_r": nrm(ks[5], (L, RNN_BLOCKS, RNN_BLOCK_W, RNN_BLOCK_W), RNN_BLOCK_W ** -0.5),
        "rg_b_r": nrm(ks[6], (L, D_RNN), 0.02),
        "rg_w_i": nrm(ks[7], (L, RNN_BLOCKS, RNN_BLOCK_W, RNN_BLOCK_W), RNN_BLOCK_W ** -0.5),
        "rg_b_i": nrm(ks[8], (L, D_RNN), 0.02),
        "rg_a": jnp.log(sig) - jnp.log1p(-sig),
        "diff_lq1": nrm(ks[10], (L, DIFF_HEAD_DIM), 0.1),
        "diff_lk1": nrm(ks[11], (L, DIFF_HEAD_DIM), 0.1),
        "diff_lq2": nrm(ks[12], (L, DIFF_HEAD_DIM), 0.1),
        "diff_lk2": nrm(ks[13], (L, DIFF_HEAD_DIM), 0.1),
        "diff_subln_g": 1.0 + nrm(ks[14], (L, 2 * DIFF_HEAD_DIM), 0.02),
        "rel_bias": nrm(ks[15], (N_BUCKETS, DIFF_HEADS), 0.5),
        "fox_b_f": 3.0 + nrm(ks[16], (L, FOX_HEADS), 0.5),
        "gate_b": nrm(ks[17], (L, N_BRANCH, D_MODEL), 0.02),
        "w_br_rnn": nrm(ks[18], (L, D_RNN, D_MODEL), D_RNN ** -0.5),
        "w_br_diff": nrm(ks[19], (L, DIFF_WIDTH, D_MODEL), DIFF_WIDTH ** -0.5),
        "w_br_fox": nrm(ks[20], (L, FOX_WIDTH, D_MODEL), FOX_WIDTH ** -0.5),
        "w_out": nrm(ks[21], (L, D_MODEL, D_MODEL), D_MODEL ** -0.5),
        "norm2_g": 1.0 + nrm(ks[22], (L, D_MODEL), 0.02),
        "ffn_up": nrm(ks[23], (L, D_MODEL, 2 * D_FF), D_MODEL ** -0.5),
        "ffn_conv_w": nrm(ks[24], (L, CONV_FFN, 2 * D_FF), CONV_FFN ** -0.5),
        "ffn_conv_b": nrm(ks[25], (L, 2 * D_FF), 0.02),
        "ffn_down": nrm(ks[26], (L, D_FF, D_MODEL), D_FF ** -0.5),
        "final_g": 1.0 + nrm(ks[27], (D_MODEL,), 0.02),
    }

def first_block(x, norm1_g, w_in, rnn_conv_w, rnn_conv_b, rg_w_r, rg_b_r, rg_w_i, rg_b_i, rg_a,
              diff_lq1, diff_lk1, diff_lq2, diff_lk2, diff_subln_g, rel_bias, fox_b_f, gate_b,
              w_br_rnn, w_br_diff, w_br_fox, w_out, norm2_g, ffn_up, ffn_conv_w, ffn_conv_b,
              ffn_down, final_g):
    bsz, s_len, _ = x.shape
    for l in range(DEPTH):
        h = rmsnorm(x, norm1_g[l])
        proj = h @ w_in[l]
        (x_rnn, g_rnn, dq, dk, dv, fq, fk, fv, f_logit, gates) = jnp.split(proj, IN_SPLITS, axis=-1)

        x_rnn = causal_dwconv(x_rnn, rnn_conv_w[l], rnn_conv_b[l])
        y_rnn = jax.nn.gelu(g_rnn) * rg_lru(x_rnn, rg_w_r[l], rg_b_r[l], rg_w_i[l], rg_b_i[l], rg_a[l])

        lam_init = 0.8 - 0.6 * math.exp(-0.3 * l)
        lam = (jnp.exp(jnp.sum(diff_lq1[l] * diff_lk1[l]).astype(jnp.float32))
               - jnp.exp(jnp.sum(diff_lq2[l] * diff_lk2[l]).astype(jnp.float32)) + lam_init)
        o_diff = diff_attention(dq.reshape(bsz, s_len, DIFF_HEADS, 2, DIFF_HEAD_DIM),
                                dk.reshape(bsz, s_len, DIFF_HEADS, 2, DIFF_HEAD_DIM),
                                dv.reshape(bsz, s_len, DIFF_HEADS, 2 * DIFF_HEAD_DIM), lam, rel_bias)
        y_diff = (rmsnorm(o_diff, diff_subln_g[l]) * (1.0 - lam_init)).reshape(bsz, s_len, DIFF_WIDTH)

        log_f = jax.nn.log_sigmoid((f_logit + fox_b_f[l]).astype(jnp.float32))
        o_fox = forgetting_attention(fq.reshape(bsz, s_len, FOX_HEADS, FOX_HEAD_DIM),
                                     fk.reshape(bsz, s_len, FOX_HEADS, FOX_HEAD_DIM),
                                     fv.reshape(bsz, s_len, FOX_HEADS, FOX_HEAD_DIM), log_f)
        y_fox = o_fox.reshape(bsz, s_len, FOX_WIDTH)

        g = jax.nn.sigmoid(gates.reshape(bsz, s_len, N_BRANCH, D_MODEL) + gate_b[l])
        m = (g[:, :, 0] * (y_rnn @ w_br_rnn[l])
             + g[:, :, 1] * (y_diff @ w_br_diff[l])
             + g[:, :, 2] * (y_fox @ w_br_fox[l]))
        x = x + m @ w_out[l]

        h = rmsnorm(x, norm2_g[l])
        u = causal_dwconv(h @ ffn_up[l], ffn_conv_w[l], ffn_conv_b[l])
        u_gate, u_val = jnp.split(u, 2, axis=-1)
        x = x + (jax.nn.gelu(u_gate) * u_val) @ ffn_down[l]
    return rmsnorm(x, final_g)


MIX_WIDTH = 2 * D_MODEL
SSD_WIDTH = MIX_WIDTH // 2
SSD_HEAD_DIM = 64
SSD_HEADS = SSD_WIDTH // SSD_HEAD_DIM
SSD_GROUPS = 2
SSD_HEADS_PER_GROUP = SSD_HEADS // SSD_GROUPS
SSD_STATE = 128
SSD_CONV = 4
SSD_CHUNK = 128
SSD_CONV_DIM = SSD_WIDTH + 2 * SSD_GROUPS * SSD_STATE
HGRN_WIDTH = MIX_WIDTH // 4
HGRN_HEAD_DIM = 128
HGRN_HEADS = HGRN_WIDTH // HGRN_HEAD_DIM
HGRN_CHUNK = 64
S5_WIDTH = MIX_WIDTH - SSD_WIDTH - HGRN_WIDTH
S5_GROUP_SIZE = 16
S5_GROUPS = S5_WIDTH // S5_GROUP_SIZE
S5_STATE = 64
S5_MIN_NEG = 1e-4

IN_COLS = SSD_WIDTH + SSD_CONV_DIM + SSD_HEADS + 4 * HGRN_WIDTH + 2 * S5_WIDTH


def _in_proj_splits():
    widths = [SSD_WIDTH, SSD_CONV_DIM, SSD_HEADS, HGRN_WIDTH, HGRN_WIDTH,
              HGRN_WIDTH, HGRN_WIDTH, S5_WIDTH, S5_WIDTH]
    pts, acc = [], 0
    for w in widths[:-1]:
        acc += w
        pts.append(acc)
    return pts

def rms_norm(x, w):
    xf = x.astype(jnp.float32)
    y = xf * lax.rsqrt(jnp.mean(xf * xf, axis=-1, keepdims=True) + EPS)
    return (y * w.astype(jnp.float32)).astype(x.dtype)

def grouped_rms_norm(x, w, n_groups):
    shp = x.shape
    xf = x.astype(jnp.float32).reshape(shp[:-1] + (n_groups, shp[-1] // n_groups))
    y = xf * lax.rsqrt(jnp.mean(xf * xf, axis=-1, keepdims=True) + EPS)
    return (y.reshape(shp) * w.astype(jnp.float32)).astype(x.dtype)

def causal_depthwise_conv(x, w, b):
    out = lax.conv_general_dilated(
        x, w[:, None, :].astype(x.dtype), window_strides=(1,),
        padding=[(SSD_CONV - 1, 0)], dimension_numbers=("NWC", "WIO", "NWC"),
        feature_group_count=x.shape[-1])
    return out + b.astype(x.dtype)

def ssd_mixer(z, xbc, dt_raw, conv_w, conv_b, dt_bias, a_log, d_skip, norm_w):
    bsz, seqlen, _ = xbc.shape
    nc = seqlen // SSD_CHUNK
    G, R, P, N, T = SSD_GROUPS, SSD_HEADS_PER_GROUP, SSD_HEAD_DIM, SSD_STATE, SSD_CHUNK
    xbc = jax.nn.silu(causal_depthwise_conv(xbc, conv_w, conv_b))
    xs, b_in, c_in = jnp.split(xbc, [SSD_WIDTH, SSD_WIDTH + G * N], axis=-1)
    xs = xs.reshape(bsz, nc, T, G, R, P)
    b_in = b_in.reshape(bsz, nc, T, G, N)
    c_in = c_in.reshape(bsz, nc, T, G, N)
    dt = jax.nn.softplus(dt_raw.astype(jnp.float32) + dt_bias.astype(jnp.float32))
    dt = dt.reshape(bsz, nc, T, G, R)
    a = -jnp.exp(a_log.astype(jnp.float32)).reshape(G, R)
    a_cum = jnp.cumsum(dt * a, axis=2)
    mask = jnp.tril(jnp.ones((T, T), dtype=bool))[:, :, None, None]
    seg = a_cum[:, :, :, None] - a_cum[:, :, None, :]
    decay = jnp.exp(jnp.where(mask, seg, -jnp.inf))
    x_dt = xs * dt[..., None]
    scores = jnp.einsum("bclgn,bcsgn->bclsg", c_in, b_in)
    y_diag = jnp.einsum("bclsg,bclsgr,bcsgrp->bclgrp", scores, decay, x_dt)
    decay_to_end = jnp.exp(a_cum[:, :, -1:] - a_cum)
    chunk_states = jnp.einsum("bclgn,bclgr,bclgrp->bcgrpn", b_in, decay_to_end, x_dt)
    chunk_decay = jnp.exp(a_cum[:, :, -1])

    def step(h, inp):
        dec, st = inp
        return dec[..., None, None] * h + st, h

    h0 = jnp.zeros((bsz, G, R, P, N), chunk_states.dtype)
    _, prev = lax.scan(step, h0, (jnp.moveaxis(chunk_decay, 1, 0),
                                  jnp.moveaxis(chunk_states, 1, 0)))
    prev = jnp.moveaxis(prev, 0, 1)
    y_off = jnp.einsum("bclgn,bcgrpn,bclgr->bclgrp", c_in, prev, jnp.exp(a_cum))
    y = y_diag + y_off + d_skip.reshape(G, R)[:, :, None] * xs
    y = y.reshape(bsz, seqlen, SSD_WIDTH)
    return grouped_rms_norm(y * jax.nn.silu(z), norm_w, SSD_GROUPS)

def hgrn2_mixer(q, f_raw, i_in, g, lb, norm_w):
    bsz, seqlen, _ = q.shape
    nc = seqlen // HGRN_CHUNK
    H, Dh, T = HGRN_HEADS, HGRN_HEAD_DIM, HGRN_CHUNK
    q = jax.nn.silu(q)
    lbf = lb.astype(jnp.float32)
    log_f = jnp.logaddexp(jnp.log(lbf), jnp.log1p(-lbf) + jax.nn.log_sigmoid(f_raw.astype(jnp.float32)))
    k = -jnp.expm1(log_f)

    def to_chunks(t):
        return t.reshape(bsz, nc, T, H, Dh).transpose(1, 0, 3, 2, 4)

    mask = jnp.tril(jnp.ones((T, T), dtype=bool))[:, :, None]

    def step(state, inp):
        qc, kc, vc, lfc = inp
        cum = jnp.cumsum(lfc, axis=2)
        decay = jnp.exp(jnp.where(mask, cum[:, :, :, None, :] - cum[:, :, None, :, :], -jnp.inf))
        attn = jnp.einsum("bhlk,bhsk,bhlsk->bhls", qc, kc, decay)
        o = (jnp.einsum("bhls,bhsv->bhlv", attn, vc)
             + jnp.einsum("bhlk,bhkv->bhlv", qc * jnp.exp(cum), state))
        last = cum[:, :, -1:, :]
        state = (jnp.exp(last[:, :, 0, :])[..., None] * state
                 + jnp.einsum("bhsk,bhsv->bhkv", kc * jnp.exp(last - cum), vc))
        return state, o

    state0 = jnp.zeros((bsz, H, Dh, Dh), jnp.float32)
    _, o = lax.scan(step, state0, (to_chunks(q), to_chunks(k), to_chunks(i_in), to_chunks(log_f)))
    o = o.transpose(1, 0, 3, 2, 4).reshape(bsz, seqlen, HGRN_WIDTH)
    return grouped_rms_norm(o, norm_w, HGRN_HEADS) * jax.nn.silu(g)

def s5_mixer(u, gate, lam_re, lam_im, log_step, b_re, b_im, c_re, c_im, d_skip, glu_w, glu_b, norm_w):
    bsz, seqlen, _ = u.shape
    G, P, Hg = S5_GROUPS, S5_STATE, S5_GROUP_SIZE
    uf = u.astype(jnp.float32)
    lr = jnp.minimum(lam_re.astype(jnp.float32), -S5_MIN_NEG)
    li = lam_im.astype(jnp.float32)
    step = jnp.exp(log_step.astype(jnp.float32))[:, None]
    mag = jnp.exp(lr * step)
    ang = li * step
    ab_re, ab_im = mag * jnp.cos(ang), mag * jnp.sin(ang)
    den = lr * lr + li * li
    num_re, num_im = ab_re - 1.0, ab_im
    co_re = (num_re * lr + num_im * li) / den
    co_im = (num_im * lr - num_re * li) / den
    bb_re = co_re[..., None] * b_re - co_im[..., None] * b_im
    bb_im = co_re[..., None] * b_im + co_im[..., None] * b_re
    ug = uf.reshape(bsz, seqlen, G, Hg)
    bu_re = jnp.einsum("blgh,gph->lbgp", ug, bb_re)
    bu_im = jnp.einsum("blgh,gph->lbgp", ug, bb_im)
    a_re = jnp.broadcast_to(ab_re, (seqlen, 1, G, P))
    a_im = jnp.broadcast_to(ab_im, (seqlen, 1, G, P))

    def combine(e_i, e_j):
        ar_i, ai_i, br_i, bi_i = e_i
        ar_j, ai_j, br_j, bi_j = e_j
        return (ar_j * ar_i - ai_j * ai_i,
                ar_j * ai_i + ai_j * ar_i,
                ar_j * br_i - ai_j * bi_i + br_j,
                ar_j * bi_i + ai_j * br_i + bi_j)

    _, _, s_re, s_im = lax.associative_scan(combine, (a_re, a_im, bu_re, bu_im), axis=0)
    y = jnp.einsum("lbgp,ghp->blgh", s_re, c_re) - jnp.einsum("lbgp,ghp->blgh", s_im, c_im)
    y = y.reshape(bsz, seqlen, S5_WIDTH) + d_skip * uf
    y = jax.nn.gelu(y)
    hg = y @ glu_w + glu_b
    val, gt = jnp.split(hg, 2, axis=-1)
    y = val * jax.nn.sigmoid(gt) * jax.nn.silu(gate)
    return rms_norm(y, norm_w)

def second_inputs(seed: int = 0) -> dict:
    key = jax.random.key(seed)
    ks = jax.random.split(key, 24)
    f32 = jnp.float32
    nrm = lambda k, shp, s: s * jax.random.normal(k, shp, f32)
    dt0 = jnp.exp(jax.random.uniform(ks[6], (DEPTH, SSD_HEADS), f32, math.log(1e-3), math.log(1e-1)))
    lam_im0 = math.pi * jnp.arange(S5_STATE, dtype=f32)
    return {
        "x": jax.random.normal(ks[0], (BATCH, SEQ, D_MODEL), f32),
        "pre_norm_w": 1.0 + nrm(ks[1], (DEPTH, D_MODEL), 0.02),
        "post_norm_w": 1.0 + nrm(ks[2], (DEPTH, D_MODEL), 0.02),
        "w_in": nrm(ks[3], (DEPTH, D_MODEL, IN_COLS), D_MODEL ** -0.5),
        "w_out": nrm(ks[4], (DEPTH, MIX_WIDTH, D_MODEL), MIX_WIDTH ** -0.5),
        "ssd_conv_w": nrm(ks[5], (DEPTH, SSD_CONV, SSD_CONV_DIM), SSD_CONV ** -0.5),
        "ssd_conv_b": nrm(ks[7], (DEPTH, SSD_CONV_DIM), 0.02),
        "ssd_dt_bias": dt0 + jnp.log(-jnp.expm1(-dt0)),
        "ssd_a_log": jnp.log(jax.random.uniform(ks[8], (DEPTH, SSD_HEADS), f32, 1.0, 16.0)),
        "ssd_d": 1.0 + nrm(ks[9], (DEPTH, SSD_HEADS), 0.02),
        "ssd_norm_w": 1.0 + nrm(ks[10], (DEPTH, SSD_WIDTH), 0.02),
        "hgrn_lower_bounds": nrm(ks[11], (DEPTH, HGRN_WIDTH), 0.1),
        "hgrn_norm_w": 1.0 + nrm(ks[12], (DEPTH, HGRN_WIDTH), 0.02),
        "s5_lambda_re": -0.5 + nrm(ks[13], (DEPTH, S5_GROUPS, S5_STATE), 0.01),
        "s5_lambda_im": lam_im0 + nrm(ks[14], (DEPTH, S5_GROUPS, S5_STATE), 0.01),
        "s5_log_step": jax.random.uniform(ks[15], (DEPTH, S5_GROUPS), f32, math.log(1e-3), math.log(1e-1)),
        "s5_b_re": nrm(ks[16], (DEPTH, S5_GROUPS, S5_STATE, S5_GROUP_SIZE), (2 * S5_GROUP_SIZE) ** -0.5),
        "s5_b_im": nrm(ks[17], (DEPTH, S5_GROUPS, S5_STATE, S5_GROUP_SIZE), (2 * S5_GROUP_SIZE) ** -0.5),
        "s5_c_re": nrm(ks[18], (DEPTH, S5_GROUPS, S5_GROUP_SIZE, S5_STATE), S5_STATE ** -0.5),
        "s5_c_im": nrm(ks[19], (DEPTH, S5_GROUPS, S5_GROUP_SIZE, S5_STATE), S5_STATE ** -0.5),
        "s5_d": jax.random.normal(ks[20], (DEPTH, S5_WIDTH), f32),
        "s5_glu_w": nrm(ks[21], (DEPTH, S5_WIDTH, 2 * S5_WIDTH), S5_WIDTH ** -0.5),
        "s5_glu_b": nrm(ks[22], (DEPTH, 2 * S5_WIDTH), 0.02),
        "s5_norm_w": 1.0 + nrm(ks[23], (DEPTH, S5_WIDTH), 0.02),
    }

def second_block(x, pre_norm_w, post_norm_w, w_in, w_out, ssd_conv_w, ssd_conv_b, ssd_dt_bias,
              ssd_a_log, ssd_d, ssd_norm_w, hgrn_lower_bounds, hgrn_norm_w, s5_lambda_re,
              s5_lambda_im, s5_log_step, s5_b_re, s5_b_im, s5_c_re, s5_c_im, s5_d, s5_glu_w,
              s5_glu_b, s5_norm_w):
    lb_all = jnp.cumsum(jax.nn.softmax(hgrn_lower_bounds.astype(jnp.float32), axis=0), axis=0)
    lb_all = lb_all - lb_all[0:1]
    splits = _in_proj_splits()
    for l in range(DEPTH):
        h = rms_norm(x, pre_norm_w[l])
        proj = h @ w_in[l]
        z, xbc, dt_raw, q, f_raw, i_in, g, u, s5_gate = jnp.split(proj, splits, axis=-1)
        y_ssd = ssd_mixer(z, xbc, dt_raw, ssd_conv_w[l], ssd_conv_b[l], ssd_dt_bias[l],
                          ssd_a_log[l], ssd_d[l], ssd_norm_w[l])
        y_hgrn = hgrn2_mixer(q, f_raw, i_in, g, lb_all[l], hgrn_norm_w[l])
        y_s5 = s5_mixer(u, s5_gate, s5_lambda_re[l], s5_lambda_im[l], s5_log_step[l],
                        s5_b_re[l], s5_b_im[l], s5_c_re[l], s5_c_im[l], s5_d[l],
                        s5_glu_w[l], s5_glu_b[l], s5_norm_w[l])
        mix = jnp.concatenate([y_ssd, y_hgrn, y_s5], axis=-1).astype(x.dtype)
        x = x + rms_norm(mix @ w_out[l], post_norm_w[l])
    return x


_first_inputs = second_inputs


def second_inputs(seed=0):
    import zlib

    import numpy as np

    out = dict(_first_inputs(seed))
    spreads = {}
    factors = {'post_norm_w': 31.424,
     'ssd_conv_b': 3.769,
     'ssd_d': 153.159,
     'ssd_norm_w': 129.666,
     'hgrn_norm_w': 200.0,
     's5_lambda_re': 200.0,
     's5_glu_b': 4.563,
     's5_norm_w': 180.005,
     's5_lambda_im': 21.584,
     's5_log_step': 23.04,
     's5_b_re': 30.104,
     's5_b_im': 30.168,
     's5_c_re': 30.064,
     's5_c_im': 30.288,
     'ssd_dt_bias': 6.452,
     'ssd_a_log': 5.952}
    for name, (base, spread) in spreads.items():
        noise = np.random.default_rng([zlib.crc32(name.encode()), seed]).standard_normal(out[name].shape)
        drawn = base * np.exp(spread * noise) if base else spread * noise
        out[name] = __import__('jax').numpy.asarray(drawn.astype(out[name].dtype))
    for name, factor in factors.items():
        out[name] = (out[name] * factor).astype(out[name].dtype)
    return out


_narrow_inputs = second_inputs


def second_inputs(seed=0):
    out = dict(_narrow_inputs(seed))
    wider = {'post_norm_w': 3.13,
     'ssd_dt_bias': 12.0,
     'ssd_a_log': 12.0,
     'ssd_d': 4.81,
     'ssd_norm_w': 5.16,
     'hgrn_norm_w': 7.7,
     's5_norm_w': 5.16}
    for name, times in wider.items():
        mean = out[name].mean()
        out[name] = (mean + times * (out[name] - mean)).astype(out[name].dtype)
    return out


def setup_inputs(seed=0):
    out = dict(first_inputs(seed))
    for name, value in second_inputs(seed + 1).items():
        if name != "x":
            out[name + "_2"] = value
    return out


def reference(
    x, norm1_g, w_in, rnn_conv_w, rnn_conv_b, rg_w_r, rg_b_r, rg_w_i, rg_b_i, rg_a, diff_lq1,
    diff_lk1, diff_lq2, diff_lk2, diff_subln_g, rel_bias, fox_b_f, gate_b, w_br_rnn, w_br_diff,
    w_br_fox, w_out, norm2_g, ffn_up, ffn_conv_w, ffn_conv_b, ffn_down, final_g, pre_norm_w_2,
    post_norm_w_2, w_in_2, w_out_2, ssd_conv_w_2, ssd_conv_b_2, ssd_dt_bias_2, ssd_a_log_2,
    ssd_d_2, ssd_norm_w_2, hgrn_lower_bounds_2, hgrn_norm_w_2, s5_lambda_re_2, s5_lambda_im_2,
    s5_log_step_2, s5_b_re_2, s5_b_im_2, s5_c_re_2, s5_c_im_2, s5_d_2, s5_glu_w_2, s5_glu_b_2,
    s5_norm_w_2,
):
    x = first_block(
        x, norm1_g, w_in, rnn_conv_w, rnn_conv_b, rg_w_r, rg_b_r, rg_w_i, rg_b_i, rg_a,
        diff_lq1, diff_lk1, diff_lq2, diff_lk2, diff_subln_g, rel_bias, fox_b_f, gate_b,
        w_br_rnn, w_br_diff, w_br_fox, w_out, norm2_g, ffn_up, ffn_conv_w, ffn_conv_b, ffn_down,
        final_g,
    )
    return second_block(
        x, pre_norm_w_2, post_norm_w_2, w_in_2, w_out_2, ssd_conv_w_2, ssd_conv_b_2,
        ssd_dt_bias_2, ssd_a_log_2, ssd_d_2, ssd_norm_w_2, hgrn_lower_bounds_2, hgrn_norm_w_2,
        s5_lambda_re_2, s5_lambda_im_2, s5_log_step_2, s5_b_re_2, s5_b_im_2, s5_c_re_2,
        s5_c_im_2, s5_d_2, s5_glu_w_2, s5_glu_b_2, s5_norm_w_2,
    )


_drawn_inputs = setup_inputs


def setup_inputs(seed=0):
    import zlib

    import numpy as np

    out = dict(_drawn_inputs(seed))
    spreads = {}
    factors = {'rg_b_r': 64.0,
     'rg_b_i': 55.795,
     'diff_lq1': 8.0,
     'diff_subln_g': 4.408,
     'gate_b': 8.0,
     'norm2_g': 4.648,
     'ffn_conv_b': 4.464,
     'ssd_d_2': 2.671}
    for name, (base, spread) in spreads.items():
        noise = np.random.default_rng([zlib.crc32(name.encode()), seed]).standard_normal(out[name].shape)
        drawn = base * np.exp(spread * noise) if base else spread * noise
        out[name] = __import__('jax').numpy.asarray(drawn.astype(out[name].dtype))
    for name, factor in factors.items():
        out[name] = (out[name] * factor).astype(out[name].dtype)
    return out
```

```python
from contextlib import ExitStack, contextmanager

import numpy as np
import concourse.bass as bass
from concourse import mybir

F32 = mybir.dt.float32
F32R = mybir.dt.float32r
I32 = mybir.dt.int32
ALU = mybir.AluOpType
ACT = mybir.ActivationFunctionType
AX = mybir.AxisListType

P = 128
SEQ = 1024
D = 1024
NB = SEQ // P
KD = D // P
HALF = 512
EPS = 1e-6
NEG = -3.0e38


class Core:

    def __init__(self, nc, io):
        self.nc, self.io = nc, io


class Sems:

    def __init__(self, pool):
        self.pool, self.names = pool, {}

    def __call__(self, name):
        if name not in self.names:
            self.names[name] = self.pool[len(self.names)]
        return self.names[name]


@contextmanager
def stage(core):
    nc = core.nc
    sem = Sems(core.pool)
    with ExitStack() as ctx:
        yield ctx, sem
    used = sorted(s.num for s in sem.names.values())
    if used:
        nc.gpsimd.sem_clear(range(used[0], used[-1] + 1))
    nc.all_engine_barrier()


def sbuf(core, ctx, name, shape, dtype=F32):
    core.serial += 1
    tensor = ctx.enter_context(core.nc.sbuf_tensor(f"{name}_{core.serial}", shape, dtype))
    assert core.nc.sbuf_base <= core.limit, name
    return tensor


def psum(core, ctx, name, shape, dtype=F32):
    core.serial += 1
    return ctx.enter_context(core.nc.psum_tensor(f"{name}_{core.serial}", shape, dtype))


class WeightTiles:

    def __init__(self, core, ctx, sem, nk, width=P, name="w", slots=2):
        self.sem, self.nk, self.width, self.name, self.slots = sem, nk, width, name, slots
        self.raw = [sbuf(core, ctx, f"{name}_raw{s}", [P, nk, width]) for s in range(slots)]
        self.high = [sbuf(core, ctx, f"{name}_high{s}", [P, nk, width], F32R) for s in range(slots)]
        self.low = [sbuf(core, ctx, f"{name}_low{s}", [P, nk, width], F32R) for s in range(slots)]

    def s(self, what, slot=""):
        return self.sem(f"{self.name}_{what}{slot}")

    def open_pool(self, pool):
        for slot in range(self.slots):
            pool.sem_inc(self.s("raw_free", slot), 1)

    def open_pe(self, pe):
        for slot in range(self.slots):
            pe.sem_inc(self.s("used", slot), 1)

    def load(self, sp, slot, turn, src, nk=None):
        nk = nk or self.nk
        sp.wait_ge(self.s("raw_free", slot), turn + 1)
        sp.sem_inc(self.s("asked", slot), 1)
        sp.dma_start(self.raw[slot][:, 0:nk, :], src.rearrange("(k p) n -> p k n", p=P)).then_inc(self.s("loaded", slot), 16)

    def split_high(self, act, slot, turn, nk=None):
        nk = nk or self.nk
        act.wait_ge(self.s("loaded", slot), (turn + 1) * 16)
        act.wait_ge(self.s("used", slot), turn + 1)
        act.activation(self.high[slot][:, 0:nk, :], self.raw[slot][:, 0:nk, :], ACT.Copy).then_inc(self.s("high", slot), 1)

    def split_low(self, pool, slot, turn, nk=None):
        nk = nk or self.nk
        pool.wait_ge(self.s("high", slot), turn + 1)
        pool.tensor_tensor(self.low[slot][:, 0:nk, :], self.raw[slot][:, 0:nk, :], self.high[slot][:, 0:nk, :].bitcast(F32),
                           ALU.subtract).then_inc(self.s("low", slot), 1)
        pool.wait_ge(self.s("low", slot), turn + 1)
        pool.sem_inc(self.s("raw_free", slot), 1)

    def wait(self, pe, slot, turn):
        pe.wait_ge(self.s("low", slot), turn + 1)

    def multiply(self, pe, slot, out, high, low, nk=None, halves=False):
        nk = nk or self.nk
        for h in range(SEQ // HALF):
            cols = slice(h * HALF, (h + 1) * HALF)
            n = 0
            for k in range(nk):
                for w, x in ((self.high, high), (self.high, low), (self.low, high)):
                    last = pe.matmul(out[:, h, :] if not halves else out[h], w[slot][:, k, :], x[:, k, cols], start=(n == 0), stop=(n == 3 * nk - 1))
                    n += 1
        last.then_inc(self.s("used", slot), 1)


def stage_norm_to_channels(core, src_tile, gain_vec, src_dram=None):
    nc = core.nc
    AH, AL, ident = core.AH, core.AL, core.ident
    with stage(core) as (ctx, sem):
        gain = sbuf(core, ctx, "gain", [P, D])
        squares = sbuf(core, ctx, "squares", [P, 2, D])
        scaled = sbuf(core, ctx, "scaled", [P, 2, D])
        total = sbuf(core, ctx, "total", [P, NB])
        root = sbuf(core, ctx, "root", [P, NB])
        rstd = sbuf(core, ctx, "rstd", [P, NB])
        turned = psum(core, ctx, "turned", [P, 2, KD, P])
        with nc.Block() as block:

            @block.sync
            def _(sp):
                sp.dma_start(gain[:, :], gain_vec.partition_broadcast(P)).then_inc(sem("gain_loaded"), 16)
                if src_dram is not None:
                    sp.dma_start(src_tile[:, :, :], src_dram.rearrange("(b p) n -> p b n", p=P)).then_inc(sem("x_loaded"), 16)

            @block.scalar
            def _(act):
                if src_dram is not None:
                    act.wait_ge(sem("x_loaded"), 16)
                for b in range(NB):
                    act.activation(squares[:, b % 2, :], src_tile[:, b, :], ACT.Square, accum_out=total[:, b:b + 1]).then_inc(sem("squared"), 1)
                    act.wait_ge(sem("squared"), b + 1)
                act.activation(root[:, :], total[:, :], ACT.Sqrt, scale=1.0 / D, bias=core.eps[:, 0:1]).then_inc(sem("root"), 1)
                with act.Fori(0, NB // 2) as pair:
                    for s in range(2):
                        b = pair * 2 + s
                        act.wait_ge(sem("turned"), b + 1)
                        act.activation(AH[:, :, bass.ds(b * P, P)], turned[:, s, :, :], ACT.Copy).then_inc(sem("high"), 1)

            @block.tensor
            def _(pe):
                with pe.Fori(0, NB // 2) as pair:
                    for s in range(2):
                        b = pair * 2 + s
                        pe.wait_ge(sem("scaled"), b + 1)
                        pe.wait_ge(sem("turned_free"), b + 1)
                        for k in range(KD):
                            last = pe.transpose(turned[:, s, k, :], scaled[:, s, k * P:(k + 1) * P], ident[:, :])
                        last.then_inc(sem("turned"), 1)

            @block.vector
            def _(dve):
                dve.sem_inc(sem("turned_free"), 2)
                dve.wait_ge(sem("root"), 1)
                dve.reciprocal(rstd[:, :], root[:, :]).then_inc(sem("rstd"), 1)
                dve.wait_ge(sem("rstd"), 1)
                dve.wait_ge(sem("gain_loaded"), 16)

                def scale(b, s):
                    dve.scalar_tensor_tensor(out=scaled[:, s, :], in0=src_tile[:, b, :], scalar=rstd[:, b:b + 1],
                                             in1=gain[:, :], op0=ALU.mult, op1=ALU.mult).then_inc(sem("scaled"), 1)
                for s in range(2):
                    scale(s, s)
                with dve.Fori(0, NB // 2 - 1) as pair:
                    for s in range(2):
                        b = pair * 2 + s
                        dve.wait_ge(sem("high"), b + 1)
                        dve.tensor_tensor(AL[:, :, bass.ds(b * P, P)], turned[:, s, :, :], AH[:, :, bass.ds(b * P, P)].bitcast(F32),
                                          ALU.subtract).then_inc(sem("turned_free"), 1)
                        nxt = b + 2
                        dve.scalar_tensor_tensor(out=scaled[:, s, :], in0=src_tile[:, bass.ds(nxt, 1), :].squeeze(1),
                                                 scalar=rstd[:, bass.ds(nxt, 1)],
                                                 in1=gain[:, :], op0=ALU.mult, op1=ALU.mult).then_inc(sem("scaled"), 1)
                for s in range(2):
                    b = NB - 2 + s
                    dve.wait_ge(sem("high"), b + 1)
                    dve.tensor_tensor(AL[:, :, b * P:(b + 1) * P], turned[:, s, :, :], AH[:, :, b * P:(b + 1) * P].bitcast(F32),
                                      ALU.subtract).then_inc(sem("turned_free"), 1)


def setup(core):
    nc = core.nc
    with stage(core) as (ctx, sem):
        with nc.Block() as block:

            @block.gpsimd
            def _(pool):
                pool.memset(core.ident[:, :], 0.0).then_inc(sem("cleared"), 1)
                pool.memset(core.ones[:, :], 1.0)
                pool.memset(core.eps[:, :], EPS)
                pool.wait_ge(sem("cleared"), 1)
                pool.affine_select(out=core.ident[:, :], in_=core.ident[:, :], compare_op=ALU.not_equal, fill=1.0,
                                   base=0, pattern=[[-1, P]], channel_multiplier=1)


def make_core(nc, io, ctx):
    core = Core(nc, io)
    core.serial = 0
    core.limit = nc.sbuf_top
    core.pool = [ctx.enter_context(nc.semaphore(f"stage_sem{i}")) for i in range(120)]
    core.ident = sbuf(core, ctx, "ident", [P, P])
    core.ones = sbuf(core, ctx, "ones", [P, P])
    core.eps = sbuf(core, ctx, "eps", [P, 1])
    core.act_at = nc.sbuf_base
    core.AH = sbuf(core, ctx, "act_high", [P, KD, SEQ], F32R)
    core.AL = sbuf(core, ctx, "act_low", [P, KD, SEQ], F32R)
    return core


def per_channel(vector, chunks=None):
    return vector.rearrange("(k p) -> p k", p=P)


def over_loop(engine, count, body):
    with engine.Fori(0, count - 1) as n:
        body(n, True)
    body(count - 1, False)


class Softplus:

    def __init__(self, core, ctx, sem, name, shape):
        self.t, self.w, self.d, self.e = (sbuf(core, ctx, f"{name}_{x}", shape) for x in "twde")
        self.sem, self.name = sem, name

    def s(self, what):
        return self.sem(f"{self.name}_{what}")

    def on_act(self, act, z, turn=0):
        t, w = self.t, self.w
        act.activation(t[:, :], z, ACT.Abs).then_inc(self.s("abs"), 1)
        act.wait_ge(self.s("abs"), turn + 1)
        act.activation(t[:, :], t[:, :], ACT.Exp, scale=-1.0).then_inc(self.s("t"), 1)
        act.wait_ge(self.s("w"), turn + 1)
        act.activation(self.e[:, :], w[:, :], ACT.Ln).then_inc(self.s("ln"), 1)

    def on_dve(self, dve, z, out, turn=0):
        t, w, d, e = (x[:, :] for x in (self.t, self.w, self.d, self.e))
        s = self.s
        dve.wait_ge(s("t"), turn + 1)
        dve.tensor_scalar(w, t, 1.0, None, ALU.add).then_inc(s("w"), 1)
        dve.wait_ge(s("w"), turn + 1)
        dve.tensor_scalar(d, w, 1.0, None, ALU.subtract).then_inc(s("d"), 1)
        dve.wait_ge(s("ln"), turn + 1)
        dve.wait_ge(s("d"), turn + 1)
        dve.tensor_scalar(w, d, 0.0, None, ALU.is_equal).then_inc(s("same"), 1)
        dve.wait_ge(s("same"), turn + 1)
        dve.tensor_tensor(e, e, w, ALU.add).then_inc(s("num"), 1)
        dve.tensor_tensor(d, d, w, ALU.add).then_inc(s("den"), 1)
        dve.wait_ge(s("den"), turn + 1)
        dve.reciprocal(w, d).then_inc(s("rec"), 1)
        dve.wait_ge(s("num"), turn + 1)
        dve.tensor_tensor(e, e, t, ALU.mult).then_inc(s("numt"), 1)
        dve.wait_ge(s("rec"), turn + 1)
        dve.wait_ge(s("numt"), turn + 1)
        dve.tensor_tensor(e, e, w, ALU.mult).then_inc(s("log1p"), 1)
        dve.wait_ge(s("log1p"), turn + 1)
        dve.scalar_tensor_tensor(out=out, in0=z, scalar=0.0, in1=e, op0=ALU.max, op1=ALU.add).then_inc(s("out"), 1)


def stage_rnn(core):
    nc, io = core.nc, core.io
    w_in = io["w_in"][0]
    AH, AL, YH, YL = core.AH, core.AL, core.YH, core.YL
    with stage(core) as (ctx, sem):
        W = WeightTiles(core, ctx, sem, KD)
        taps = sbuf(core, ctx, "taps", [P, 4, KD])
        bias = sbuf(core, ctx, "bias", [P, 4, KD])
        minus_a = sbuf(core, ctx, "minus_a", [P, KD])
        soft = sbuf(core, ctx, "soft", [P, KD])
        rate = sbuf(core, ctx, "rate", [P, 2, KD])
        wr = sbuf(core, ctx, "wr", [P, P])
        wi = sbuf(core, ctx, "wi", [P, P])
        xc, G, R, I, A, Q, Hs = (sbuf(core, ctx, n, [P, SEQ]) for n in ("xc", "gelu", "r", "i", "a", "q", "h"))
        SP_ = Softplus(core, ctx, sem, "sp", [P, KD])
        pX, pG, pR, pI = (psum(core, ctx, n, [P, 2, HALF]) for n in ("px", "pg", "pr", "pi"))
        flat = lambda t: t[:, :, :].rearrange("p a b -> p (a b)")
        with nc.Block() as block:

            @block.sync
            def _(sp):
                for j in range(4):
                    sp.dma_start(taps[:, j, :], per_channel(io["rnn_conv_w"][0, j])).then_inc(sem("small"), 16)
                for j, name in enumerate(("rnn_conv_b", "rg_b_r", "rg_b_i", "rg_a")):
                    sp.dma_start(bias[:, j, :], per_channel(io[name][0])).then_inc(sem("small"), 16)
                with sp.Fori(0, KD) as n:
                    for slot, at in ((0, 0), (1, D)):
                        W.load(sp, slot, n, w_in[:, bass.ds(n * P + at, P)])
                    sp.wait_ge(sem("gates_free"), n + 1)
                    sp.dma_start(wr[:, :], io["rg_w_r"][0].rearrange("n c d -> (n c) d")[bass.ds(n * P, P), :]).then_inc(sem("wr"), 16)
                    sp.dma_start(wi[:, :], io["rg_w_i"][0].rearrange("n c d -> (n c) d")[bass.ds(n * P, P), :]).then_inc(sem("wi"), 16)

            @block.gpsimd
            def _(pool):
                W.open_pool(pool)
                with pool.Fori(0, KD) as n:
                    for slot in range(2):
                        W.split_low(pool, slot, n)

            @block.tensor
            def _(pe):
                W.open_pe(pe)
                pe.sem_inc(sem("gates_free"), 1)
                with pe.Fori(0, KD) as n:
                    W.wait(pe, 0, n)
                    pe.wait_ge(sem("px_free"), n + 1)
                    W.multiply(pe, 0, pX, AH, AL)
                    W.wait(pe, 1, n)
                    pe.wait_ge(sem("pg_free"), n + 1)
                    W.multiply(pe, 1, pG, AH, AL)
                    pe.wait_ge(sem("conv"), n + 1)
                    pe.wait_ge(sem("pri_free"), n + 1)
                    pe.wait_ge(sem("wr"), (n + 1) * 16)
                    pe.wait_ge(sem("wi"), (n + 1) * 16)
                    for p, w in ((pR, wr), (pI, wi)):
                        for h in range(2):
                            last = pe.matmul(p[:, h, :], w[:, :], xc[:, h * HALF:(h + 1) * HALF], start=True, stop=True)
                    last.then_inc(sem("gates_free"), 1)

            @block.scalar
            def _(act):
                act.sem_inc(sem("pg_free"), 1)
                act.sem_inc(sem("pri_free"), 1)
                for slot in range(2):
                    W.split_high(act, slot, 0)
                act.wait_ge(sem("minus_a"), 1)
                SP_.on_act(act, minus_a[:, :])
                act.wait_ge(sem("rate"), 2)

                def chunk(n, more):
                    act.wait_ge(W.s("used", 0), n + 2)
                    act.wait_ge(sem("xc_free"), n + 1)
                    act.activation(xc[:, :], flat(pX), ACT.Identity, scale=taps[:, 3, bass.ds(n, 1)],
                                   bias=bias[:, 0, bass.ds(n, 1)]).then_inc(sem("tap3"), 1)
                    if more:
                        W.split_high(act, 0, n + 1)
                    act.wait_ge(W.s("used", 1), n + 2)
                    act.wait_ge(sem("yl"), n + 1)
                    act.activation(G[:, :], flat(pG), ACT.Gelu_apprx_tanh).then_inc(sem("pg_free"), 1)
                    if more:
                        W.split_high(act, 1, n + 1)
                    act.wait_ge(sem("gates_free"), n + 2)
                    act.activation(R[:, :], flat(pR), ACT.Sigmoid, bias=bias[:, 1, bass.ds(n, 1)]).then_inc(sem("r"), 1)
                    act.activation(I[:, :], flat(pI), ACT.Sigmoid, bias=bias[:, 2, bass.ds(n, 1)]).then_inc(sem("pri_free"), 1)
                    act.wait_ge(sem("r"), n + 1)
                    act.activation(A[:, :], R[:, :], ACT.Exp, scale=rate[:, 0, bass.ds(n, 1)]).then_inc(sem("a"), 1)
                    act.activation(R[:, :], R[:, :], ACT.Tanh, scale=rate[:, 1, bass.ds(n, 1)]).then_inc(sem("tanh"), 1)
                    act.wait_ge(sem("one_minus_a2"), n + 1)
                    act.activation(Q[:, :], Q[:, :], ACT.Sqrt).then_inc(sem("root"), 1)
                    act.wait_ge(sem("y"), n + 1)
                    act.activation(YH[:, bass.ds(n, 1), :].squeeze(1), G[:, :], ACT.Copy).then_inc(sem("yh"), 1)
                over_loop(act, KD, chunk)

            @block.vector
            def _(dve):
                dve.sem_inc(sem("px_free"), 1)
                dve.sem_inc(sem("xc_free"), 1)
                dve.sem_inc(sem("yl"), 1)
                dve.wait_ge(sem("small"), 128)
                dve.tensor_scalar(minus_a[:, :], bias[:, 3, :], -1.0, None, ALU.mult).then_inc(sem("minus_a"), 1)
                dve.wait_ge(sem("minus_a"), 1)
                SP_.on_dve(dve, minus_a[:, :], soft[:, :])
                dve.wait_ge(SP_.s("out"), 1)
                dve.tensor_scalar(rate[:, 0, :], soft[:, :], -8.0, None, ALU.mult).then_inc(sem("rate"), 1)
                dve.tensor_scalar(rate[:, 1, :], soft[:, :], 8.0, None, ALU.mult).then_inc(sem("rate"), 1)
                with dve.Fori(0, KD) as n:
                    x = flat(pX)
                    dve.wait_ge(sem("tap3"), n + 1)
                    for back in (1, 2, 3):
                        ins = dve.scalar_tensor_tensor(out=xc[:, back:], in0=x[:, :SEQ - back], scalar=taps[:, 3 - back, bass.ds(n, 1)],
                                                       in1=xc[:, back:], op0=ALU.mult, op1=ALU.add)
                        if back < 3:
                            ins.then_inc(sem("taps"), 1)
                            dve.wait_ge(sem("taps"), n * 2 + back)
                    ins.then_inc(sem("conv"), 1)
                    dve.wait_ge(sem("conv"), n + 1)
                    dve.sem_inc(sem("px_free"), 1)
                    dve.wait_ge(sem("pri_free"), n + 2)
                    dve.tensor_tensor(I[:, :], I[:, :], xc[:, :], ALU.mult).then_inc(sem("ix"), 1)
                    dve.wait_ge(sem("a"), n + 1)
                    dve.tensor_tensor(Q[:, :], A[:, :], A[:, :], ALU.mult).then_inc(sem("a2"), 1)
                    dve.wait_ge(sem("a2"), n + 1)
                    dve.wait_ge(sem("tanh"), n + 1)
                    dve.scalar_tensor_tensor(out=Q[:, :], in0=Q[:, :], scalar=1.0, in1=R[:, :], op0=ALU.add, op1=ALU.mult).then_inc(sem("one_minus_a2"), 1)
                    dve.wait_ge(sem("root"), n + 1)
                    dve.wait_ge(sem("ix"), n + 1)
                    dve.tensor_tensor(Q[:, :], Q[:, :], I[:, :], ALU.mult).then_inc(sem("xc_free"), 1)
                    dve.wait_ge(sem("xc_free"), n + 2)
                    dve.tensor_tensor_scan(Hs[:, :], A[:, :], Q[:, :], 0.0, ALU.mult, ALU.add).then_inc(sem("scan"), 1)
                    dve.wait_ge(sem("scan"), n + 1)
                    dve.wait_ge(sem("pg_free"), n + 2)
                    dve.tensor_tensor(G[:, :], G[:, :], Hs[:, :], ALU.mult).then_inc(sem("y"), 1)
                    dve.wait_ge(sem("yh"), n + 1)
                    dve.tensor_tensor(YL[:, bass.ds(n, 1), :].squeeze(1), G[:, :], YH[:, bass.ds(n, 1), :].squeeze(1).bitcast(F32),
                                      ALU.subtract).then_inc(sem("yl"), 1)


GATES_AT = 2 * D + 6 * HALF + 8
FOX_F_AT = 2 * D + 6 * HALF


def stage_branches(core, parts, part_in=None, part_out=None):
    nc, io = core.nc, core.io
    w_in = io["w_in"][0]
    AH, AL, YH, YL = core.AH, core.AL, core.YH, core.YL
    NP = len(parts)
    with stage(core) as (ctx, sem):
        W = WeightTiles(core, ctx, sem, KD)
        gate_b = sbuf(core, ctx, "gate_b", [P, NP, KD])
        gate = [sbuf(core, ctx, f"gate{j}", [P, SEQ]) for j in range(NP)]
        other = sbuf(core, ctx, "other", [P, SEQ])
        pG = [psum(core, ctx, f"pg{j}", [P, 2, HALF]) for j in range(NP)]
        pY = [psum(core, ctx, f"py{j}", [P, 2, HALF]) for j in range(NP)]
        flat = lambda t: t[:, :, :].rearrange("p a b -> p (a b)")
        with nc.Block() as block:

            @block.sync
            def _(sp):
                for j, (g, _, _, _) in enumerate(parts):
                    sp.dma_start(gate_b[:, j, :], per_channel(io["gate_b"][0, g])).then_inc(sem("gate_b"), 16)

                def load(n):
                    for j, (g, w, nk, _) in enumerate(parts):
                        W.load(sp, 0, n * NP + j, w_in[:, bass.ds(n * P + GATES_AT + g * D, P)])
                        W.load(sp, 1, n * NP + j, w[:, bass.ds(n * P, P)], nk)
                    if part_in is not None:
                        sp.wait_ge(sem("other_free"), n + 1)
                        sp.dma_start(other[:, :], part_in.rearrange("n p s -> (n p) s")[bass.ds(n * P, P), :]).then_inc(sem("other"), 16)

                def store(n):
                    if part_out is not None:
                        sp.wait_ge(sem("sum"), n + 1)
                        sp.sem_inc(sem("store_asked"), 1)
                        sp.dma_start(part_out.rearrange("n p s -> (n p) s")[bass.ds(n * P, P), :], gate[0][:, :]).then_inc(sem("m_stored"), 16)

                load(0)
                with sp.Fori(1, KD) as n:
                    load(n)
                    store(n - 1)
                store(KD - 1)
                if part_out is not None:
                    sp.wait_ge(sem("m_stored"), KD * 16)

            @block.gpsimd
            def _(pool):
                W.open_pool(pool)
                with pool.Fori(0, KD) as n:
                    for j, (_, _, nk, _) in enumerate(parts):
                        W.split_low(pool, 0, n * NP + j)
                        W.split_low(pool, 1, n * NP + j, nk)

            @block.tensor
            def _(pe):
                W.open_pe(pe)
                with pe.Fori(0, KD) as n:
                    for j, (_, _, nk, y0) in enumerate(parts):
                        W.wait(pe, 0, n * NP + j)
                        pe.wait_ge(sem(f"pg_free{j}"), n + 1)
                        W.multiply(pe, 0, pG[j], AH, AL)
                        W.wait(pe, 1, n * NP + j)
                        pe.wait_ge(sem(f"py_free{j}"), n + 1)
                        W.multiply(pe, 1, pY[j], YH[:, y0:y0 + nk, :], YL[:, y0:y0 + nk, :], nk)

            @block.scalar
            def _(act):
                act.wait_ge(sem("gate_b"), 16 * NP)
                for j in range(NP):
                    act.sem_inc(sem(f"pg_free{j}"), 1)
                W.split_high(act, 0, 0)
                W.split_high(act, 1, 0, parts[0][2])

                def chunk(n, more):
                    for j in range(NP):
                        turn = n * NP + j
                        act.wait_ge(W.s("used", 0), turn + 2)
                        act.wait_ge(sem(f"gate_free{j}"), n + 1)
                        act.activation(gate[j][:, :], flat(pG[j]), ACT.Sigmoid, bias=gate_b[:, j, bass.ds(n, 1)]).then_inc(sem(f"pg_free{j}"), 1)
                        if more or j < NP - 1:
                            W.split_high(act, 0, turn + 1)
                            W.split_high(act, 1, turn + 1, parts[(j + 1) % NP][2])
                over_loop(act, KD, chunk)

            @block.vector
            def _(dve):
                for j in range(NP):
                    dve.sem_inc(sem(f"py_free{j}"), 1)
                    dve.sem_inc(sem(f"gate_free{j}"), 1)
                dve.sem_inc(sem("other_free"), 1)
                with dve.Fori(0, KD) as n:
                    for j in range(NP):
                        dve.wait_ge(sem(f"pg_free{j}"), n + 2)
                        dve.wait_ge(W.s("used", 1), n * NP + j + 2)
                        dve.tensor_tensor(gate[j][:, :], gate[j][:, :], flat(pY[j]), ALU.mult).then_inc(sem(f"py_free{j}"), 1)
                        dve.wait_ge(sem(f"py_free{j}"), n + 2)
                    if part_out is not None:
                        dve.tensor_tensor(gate[0][:, :], gate[0][:, :], gate[1][:, :], ALU.add).then_inc(sem("sum"), 1)
                        dve.wait_ge(sem("sum"), n + 1)
                        dve.wait_ge(sem("m_stored"), (n + 1) * 16)
                    else:
                        dve.wait_ge(sem("other"), (n + 1) * 16)
                        dve.tensor_tensor(core.M[:, bass.ds(n, 1), :].squeeze(1), gate[0][:, :], other[:, :], ALU.add).then_inc(sem("sum"), 1)
                        dve.wait_ge(sem("sum"), n + 1)
                    for j in range(NP):
                        dve.sem_inc(sem(f"gate_free{j}"), 1)
                    dve.sem_inc(sem("other_free"), 1)


def stage_rows(core, XH, XL, nk, w, acc, whole=None, load_acc=None, add=True):
    nc = core.nc
    G = 4
    NG = nk // G
    with stage(core) as (ctx, sem):
        W = WeightTiles(core, ctx, sem, G, HALF)
        out = psum(core, ctx, "rows", [P, NB, HALF])
        tiles = [(half, kg) for half in range(2) for kg in range(NG)]
        with nc.Block() as block:

            @block.sync
            def _(sp):
                if load_acc is not None:
                    sp.dma_start(acc[:, :, :], load_acc.rearrange("(b p) n -> p b n", p=P)).then_inc(sem("acc_loaded"), 16)
                for t, (half, kg) in enumerate(tiles):
                    W.load(sp, t % 2, t // 2, w[kg * G * P:(kg + 1) * G * P, half * HALF:(half + 1) * HALF])

            @block.gpsimd
            def _(pool):
                W.open_pool(pool)
                for t in range(len(tiles)):
                    W.split_low(pool, t % 2, t // 2)

            @block.scalar
            def _(act):
                if whole is not None:
                    for k in range(nk):
                        act.activation(XH[:, k, :], whole[:, k, :], ACT.Copy).then_inc(sem("x_high"), 1)
                for t in range(len(tiles)):
                    W.split_high(act, t % 2, t // 2)

            @block.tensor
            def _(pe):
                W.open_pe(pe)
                for t, (half, kg) in enumerate(tiles):
                    W.wait(pe, t % 2, t // 2)
                    for b in range(NB):
                        if half and kg == 0:
                            pe.wait_ge(sem("added"), b + 1)
                        steps = slice(b * P, (b + 1) * P)
                        for k in range(G):
                            kk = kg * G + k
                            if whole is not None and b == 0 and half == 0:
                                pe.wait_ge(sem("x_low"), kk + 1)
                            for i, (x, v) in enumerate(((XH, W.high), (XL, W.high), (XH, W.low))):
                                last = pe.matmul(out[:, b, :], x[:, kk, steps], v[t % 2][:, k, :],
                                                 start=(kk == 0 and i == 0), stop=(kk == nk - 1 and i == 2))
                        if kg == NG - 1 and b < NB - 1:
                            last.then_inc(sem("out"), 1)
                    last.then_inc(W.s("used", t % 2), 1)

            @block.vector
            def _(dve):
                if whole is not None:
                    for k in range(nk):
                        dve.wait_ge(sem("x_high"), k + 1)
                        dve.tensor_tensor(XL[:, k, :], whole[:, k, :], XH[:, k, :].bitcast(F32), ALU.subtract).then_inc(sem("x_low"), 1)
                if load_acc is not None:
                    dve.wait_ge(sem("acc_loaded"), 16)
                for half in range(2):
                    cols = slice(half * HALF, (half + 1) * HALF)
                    for b in range(NB):
                        t = half * NG + NG - 1
                        if b < NB - 1:
                            dve.wait_ge(sem("out"), half * (NB - 1) + b + 1)
                        else:
                            dve.wait_ge(W.s("used", t % 2), t // 2 + 2)
                        if add:
                            dve.tensor_tensor(acc[:, b, cols], acc[:, b, cols], out[:, b, :], ALU.add).then_inc(sem("added"), 1)
                        else:
                            dve.tensor_copy(acc[:, b, cols], out[:, b, :]).then_inc(sem("added"), 1)


BUCKETS, MAX_DIST = 32, 128
LINE = SEQ + P


def bucket_edges():
    half = BUCKETS // 2
    n = np.arange(1, SEQ + 1, dtype=np.float64)
    large = half + np.floor(np.log(n / half) / np.log(MAX_DIST / half) * (BUCKETS - half) + 1e-9)
    of = np.concatenate([[0], np.where(n < half, n, np.minimum(large, BUCKETS - 1))])
    first = [int(np.argmax(of == b)) for b in range(BUCKETS)]
    return np.array([[a, b] for a, b in zip(first, first[1:] + [SEQ])], np.float32)


def stage_attention_tables(core):
    nc, io = core.nc, core.io
    AH, AL = core.AH, core.AL
    NH = 4
    with stage(core) as (ctx, sem):
        W = WeightTiles(core, ctx, sem, KD, slots=1)
        dist = sbuf(core, ctx, "dist", [BUCKETS, LINE])
        hot = sbuf(core, ctx, "hot", [BUCKETS, LINE])
        edges = sbuf(core, ctx, "edges", [BUCKETS, 2])
        rel = sbuf(core, ctx, "rel", [BUCKETS, NH])
        rel_wide = sbuf(core, ctx, "rel_wide", [BUCKETS, NH, P])
        line = sbuf(core, ctx, "line", [P, 2, LINE])
        bf = sbuf(core, ctx, "bf", [8, 1])
        z, t, f, c = (sbuf(core, ctx, n, [8, SEQ]) for n in ("z", "t", "f", "c"))
        pf = psum(core, ctx, "pf", [P, 2, HALF])
        pl = psum(core, ctx, "pl", [P, 3, HALF])
        with nc.Block() as block:

            @block.sync
            def _(sp):
                W.load(sp, 0, 0, io["w_in"][0][:, FOX_F_AT:FOX_F_AT + P])
                sp.dma_start(edges[:, :], io["bucket_edges"]).then_inc(sem("edges"), 16)
                sp.dma_start(rel[:, :], io["rel_bias"]).then_inc(sem("rel"), 16)
                sp.dma_start(bf[:, :], io["fox_b_f"].rearrange("a n -> n a")).then_inc(sem("bf"), 16)
                for h in range(NH):
                    sp.wait_ge(sem("line"), h + 2)
                    sp.dma_start(core.lines[h], line[:, h % 2, :]).then_inc(sem("line_stored" if h % 2 == 0 else "line_stored1"), 16)
                sp.wait_ge(sem("c"), 1)
                sp.dma_start(core.neg_c, c[:, :]).then_inc(sem("c_stored"), 16)
                sp.wait_ge(sem("c_stored"), 16)
                sp.wait_ge(sem("line_stored"), 32)
                sp.wait_ge(sem("line_stored1"), 32)

            @block.gpsimd
            def _(pool):
                W.open_pool(pool)
                pool.iota(dist[:, :], pattern=[[-1, LINE]], base=SEQ - 1, channel_multiplier=0,
                          allow_small_or_imprecise_dtypes=True).then_inc(sem("dist"), 1)
                W.split_low(pool, 0, 0)

            @block.scalar
            def _(act):
                W.split_high(act, 0, 0)
                act.wait_ge(sem("z"), 1)
                act.activation(t[:, :], z[:, :], ACT.Abs).then_inc(sem("abs"), 1)
                act.wait_ge(sem("abs"), 1)
                act.activation(t[:, :], t[:, :], ACT.Exp, scale=-1.0).then_inc(sem("exp"), 1)
                act.wait_ge(sem("exp"), 1)
                act.activation(t[:, :], t[:, :], ACT.Ln, bias=1.0).then_inc(sem("ln"), 1)

            @block.tensor
            def _(pe):
                W.open_pe(pe)
                pe.wait_ge(sem("hot"), 1)
                pe.wait_ge(sem("rel_wide"), 1)
                for h in range(NH):
                    pe.wait_ge(sem("line"), h + 1)
                    for j in range(3):
                        cols = slice(j * HALF, min((j + 1) * HALF, LINE))
                        last = pe.matmul(pl[:, j, 0:cols.stop - cols.start], rel_wide[:, h, :], hot[:, cols], start=True, stop=True)
                    last.then_inc(sem("pl"), 1)
                W.wait(pe, 0, 0)
                W.multiply(pe, 0, pf, AH, AL)

            @block.vector
            def _(dve):
                dve.wait_ge(sem("edges"), 16)
                dve.wait_ge(sem("dist"), 1)
                dve.tensor_scalar(hot[:, :], dist[:, :], edges[:, 0:1], None, ALU.is_ge).then_inc(sem("above"), 1)
                dve.wait_ge(sem("above"), 1)
                dve.scalar_tensor_tensor(out=hot[:, :], in0=dist[:, :], scalar=edges[:, 1:2], in1=hot[:, :],
                                         op0=ALU.is_lt, op1=ALU.mult).then_inc(sem("hot"), 1)
                dve.wait_ge(sem("rel"), 16)
                dve.tensor_copy(rel_wide[:, :, :], rel[:, :].unsqueeze(2).to_broadcast([BUCKETS, NH, P])).then_inc(sem("rel_wide"), 1)
                dve.sem_inc(sem("line"), 1)
                for h in range(NH):
                    dve.wait_ge(sem("pl"), h + 1)
                    if h >= 2:
                        dve.wait_ge(sem(("line_stored", "line_stored1")[h % 2]), 16)
                    dve.tensor_copy(line[:, h % 2, 0:SEQ], pl[:, :, :].rearrange("p a b -> p (a b)")[:, 0:SEQ]).then_inc(sem("line_low"), 1)
                    dve.wait_ge(sem("line_low"), h + 1)
                    dve.memset(line[:, h % 2, SEQ:LINE], NEG).then_inc(sem("line"), 1)
                dve.wait_ge(sem("bf"), 16)
                dve.wait_ge(W.s("used", 0), 2)
                dve.tensor_scalar(z[:, :], pf[0:8, :, :].rearrange("p a b -> p (a b)"), bf[:, 0:1], None, ALU.add).then_inc(sem("z"), 1)
                dve.wait_ge(sem("z"), 1)
                dve.memset(f[:, :], 1.0).then_inc(sem("f"), 1)
                dve.tensor_scalar(c[:, :], z[:, :], 0.0, None, ALU.min).then_inc(sem("min"), 1)
                dve.wait_ge(sem("ln"), 1)
                dve.wait_ge(sem("min"), 1)
                dve.tensor_tensor(z[:, :], t[:, :], c[:, :], ALU.subtract).then_inc(sem("nlf"), 1)
                dve.wait_ge(sem("nlf"), 1)
                dve.wait_ge(sem("f"), 1)
                dve.tensor_tensor_scan(c[:, :], f[:, :], z[:, :], 0.0, ALU.mult, ALU.add).then_inc(sem("c"), 1)


def stage_attention(core, kind, q_at, k_at, v_at, y0):
    nc, io = core.nc, core.io
    w_in = io["w_in"][0]
    AH, AL, YH, YL, ident = core.AH, core.AL, core.YH, core.YL, core.ident
    NH = 4
    U = 2 * NB
    diff = kind == "diff"
    with stage(core) as (ctx, sem):
        W = WeightTiles(core, ctx, sem, KD)
        Q = [sbuf(core, ctx, f"q{c}", [P, SEQ]) for c in range(2)]
        K = sbuf(core, ctx, "k", [P, SEQ])
        V = sbuf(core, ctx, "v", [P, NB, P])
        bias = sbuf(core, ctx, "bias", [P, 1 if diff else 2, SEQ])
        S = sbuf(core, ctx, "scores", [P, 2, SEQ])
        PR = sbuf(core, ctx, "probs", [P, 2, SEQ])
        PT = sbuf(core, ctx, "probs_t", [P, 2, SEQ])
        O = sbuf(core, ctx, "o", [P, NB, P]) if diff else None
        OS = sbuf(core, ctx, "o_scaled", [P, NB, P])
        VT = OS[:, :, :].rearrange("p b t -> p (b t)")
        mx = sbuf(core, ctx, "mx", [P, U])
        nmx = sbuf(core, ctx, "nmx", [P, U])
        total = sbuf(core, ctx, "total", [P, U])
        part = sbuf(core, ctx, "part", [P, U])
        mask = sbuf(core, ctx, "mask", [P, P])
        gain = sbuf(core, ctx, "gain", [P, 1])
        lq = sbuf(core, ctx, "lq", [P, 4, 64])
        lam = sbuf(core, ctx, "lam", [P, 4])
        blank = sbuf(core, ctx, "blank", [1, 2 * U])
        norm = sbuf(core, ctx, "norm", [P, 3, NB])
        pS = [psum(core, ctx, f"ps{c}", [P, 2, HALF]) for c in range(2)]
        pT = [psum(core, ctx, f"pt{c}", [P, 4, P]) for c in range(2)]
        pO = [psum(core, ctx, f"po{c}", [P, 4, P]) for c in range(2)]
        flat = lambda t: t[:, :, :].rearrange("p a b -> p (a b)")
        groups = [(u, g, min(4, u // 2 + 1 - g)) for u in range(U) for g in range(0, u // 2 + 1, 4)]
        GN = len(groups)
        last_group = {u: n for n, (u, _, _) in enumerate(groups)}

        with nc.Block() as block:

            @block.sync
            def _(sp):
                if diff:
                    for j, name in enumerate(("diff_lq1", "diff_lk1", "diff_lq2", "diff_lk2")):
                        sp.dma_start(lq[:, j, :], io[name][0].partition_broadcast(P)).then_inc(sem("lq"), 16)
                    sp.dma_start(gain[:, :], io["diff_subln_g"].rearrange("a n -> n a")).then_inc(sem("gain"), 16)
                with sp.Fori(0, NH) as h:
                    for slot, turn, at in ((0, h * 2, q_at), (1, h, k_at), (0, h * 2 + 1, v_at)):
                        W.load(sp, slot, turn, w_in[:, bass.ds(h * P + at, P)])
                    sp.wait_ge(sem("bias_free"), h + 1)
                    if diff:
                        src = core.lines.rearrange("h p y -> h (p y)")[bass.ds(h, 1), P - 1:P - 1 + P * (LINE - 1)]
                        sp.dma_start(bias[:, 0, :], src.rearrange("a (p y) -> (a p) y", p=P)[:, 0:SEQ]).then_inc(sem("bias"), 16)
                    else:
                        src = core.neg_c.rearrange("(h c) s -> h (c s)", c=2)[bass.ds(h, 1), :]
                        sp.dma_start(bias[:, :, :].rearrange("p c s -> p (c s)"), src.squeeze(0).partition_broadcast(P)).then_inc(sem("bias"), 16)

            @block.gpsimd
            def _(pool):
                W.open_pool(pool)
                if not diff:
                    pool.memset(mask[:, :], 0.0).then_inc(sem("mask0"), 1)
                    pool.wait_ge(sem("mask0"), 1)
                    pool.affine_select(out=mask[:, :], in_=mask[:, :], compare_op=ALU.is_ge, fill=NEG, base=0,
                                       pattern=[[-1, P]], channel_multiplier=1).then_inc(sem("mask"), 1)
                    pool.wait_ge(sem("mask"), 1)
                for c in range(2):
                    pool.memset(Q[c][64 * (1 - c):64 * (2 - c), :], 0.0).then_inc(sem("q_zero"), 1)
                    pool.wait_ge(sem("q_zero"), c + 1)
                with pool.Fori(0, NH) as h:
                    W.split_low(pool, 0, h * 2)
                    W.split_low(pool, 1, h)
                    W.split_low(pool, 0, h * 2 + 1)

            @block.tensor
            def _(pe):
                W.open_pe(pe)
                pe.wait_ge(sem("q_zero"), 2)
                if not diff:
                    pe.wait_ge(sem("mask"), 1)
                def project_q(h):
                    W.wait(pe, 0, h * 2)
                    pe.wait_ge(sem("reduced"), h * U + U)
                    W.multiply(pe, 0, pS[0][:, :, :], AH, AL)

                def pair(h, more):
                    W.wait(pe, 1, h)
                    W.multiply(pe, 1, pS[1][:, :, :], AH, AL)

                    def scores(u):
                        b, c = u // 2, u % 2
                        n = (b + 1) * P
                        if u >= 2:
                            pe.wait_ge(sem("reduced"), h * U + u - 1 + U)
                        for a in range(0, n, HALF):
                            e = min(a + HALF, n)
                            masked = not diff and e == n
                            last = pe.matmul(pS[c][:, a // HALF, 0:e - a], Q[c][:, b * P:(b + 1) * P], K[:, a:e], start=True, stop=not masked)
                            if masked:
                                at = b * P - a
                                last = pe.matmul(pS[c][:, a // HALF, at:at + P], ident[:, :], mask[:, :], start=False, stop=True)
                        last.then_inc(sem("scores"), 1)

                    def turn(u):
                        for n, (uu, g, count) in enumerate(groups):
                            if uu != u:
                                continue
                            pe.wait_ge(sem("probs"), h * U + u + 1)
                            if n < 2:
                                pe.wait_ge(sem("v"), h * 2 + n + 1)
                            else:
                                pe.wait_ge(sem("probs_t"), h * GN + n - 1)
                            for j in range(count):
                                last = pe.transpose(pT[n % 2][:, j, :], PR[:, u % 2, (g + j) * P:(g + j + 1) * P], ident[:, :])
                            last.then_inc(sem("pt"), 1)

                    def values(u):
                        b, c = u // 2, u % 2
                        pe.wait_ge(sem("probs_t"), h * GN + last_group[u] + 1)
                        pe.wait_ge(sem("o_taken"), h * U + u + 1)
                        cols = slice(0, P) if diff else slice(c * 64, (c + 1) * 64)
                        for j in range(b + 1):
                            last = pe.matmul(pO[c][:, 0, 0:cols.stop - cols.start], PT[:, c, j * P:(j + 1) * P], V[:, j, cols],
                                             start=(j == 0), stop=(j == b))
                        last.then_inc(sem("o"), 1)

                    pe.wait_ge(sem("q"), h * 2 + 2)
                    pe.wait_ge(sem("k"), h + 1)
                    scores(0)
                    scores(1)
                    W.wait(pe, 0, h * 2 + 1)
                    W.multiply(pe, 0, [pS[0][:, 1, :], pS[1][:, 1, :]], AH, AL, halves=True)
                    pe.wait_ge(sem("vt"), h * 2 + 2)
                    for g in range(2):
                        pe.wait_ge(sem("yl"), h * 2 + 1)
                        for b in range(4):
                            blk = g * 4 + b
                            last = pe.transpose(pT[g][:, b, :], OS[:, blk, :], ident[:, :])
                        last.then_inc(sem("pt"), 1)
                    for u in range(U):
                        turn(u)
                        if u + 2 < U:
                            scores(u + 2)
                        values(u)
                    if more:
                        project_q(h + 1)
                    for g in range(2):
                        pe.wait_ge(sem("o_scaled"), h + 1)
                        pe.wait_ge(sem("probs_t"), h * GN + GN - 1 + g)
                        for b in range(4):
                            last = pe.transpose(pT[(GN + g) % 2][:, b, :], OS[:, g * 4 + b, :], ident[:, :])
                        last.then_inc(sem("pt"), 1)
                project_q(0)
                over_loop(pe, NH, pair)

            @block.scalar
            def _(act):
                if diff:
                    act.wait_ge(sem("lam_sums"), 2)
                    act.activation(lam[:, 2:4], lam[:, 0:2], ACT.Exp).then_inc(sem("lam_exp"), 1)
                W.split_high(act, 0, 0)
                W.split_high(act, 1, 0)

                def pair(h, more):
                    act.wait_ge(W.s("used", 0), h * 2 + 2)
                    W.split_high(act, 0, h * 2 + 1)
                    act.wait_ge(sem("scores"), h * U + U)
                    for c in range(2):
                        rows = slice(64 * c, 64 * (c + 1))
                        act.activation(Q[c][rows, :], flat(pS[0])[rows, :], ACT.Copy, scale=0.125).then_inc(sem("q"), 1)
                    act.wait_ge(W.s("used", 1), h + 2)
                    act.activation(K[:, :], flat(pS[1]), ACT.Copy).then_inc(sem("k"), 1)
                    if more:
                        W.split_high(act, 1, h + 1)
                    for u in range(U):
                        if u == 2:
                            act.wait_ge(W.s("used", 0), h * 2 + 3)
                            for half in range(2):
                                act.activation(VT[:, half * HALF:(half + 1) * HALF], pS[half][:, 1, :], ACT.Copy).then_inc(sem("vt"), 1)
                            if more:
                                W.split_high(act, 0, h * 2 + 2)
                        n = (u // 2 + 1) * P
                        act.wait_ge(sem("nmx"), h * U + u + 1)
                        act.wait_ge(sem("pt"), 4 + h * (GN + 4) + (last_group[u - 2] + 3 if u >= 2 else 0))
                        act.activation(PR[:, u % 2, 0:n], S[:, u % 2, 0:n], ACT.Exp, bias=nmx[:, u:u + 1],
                                       accum_out=total[:, u:u + 1]).then_inc(sem("probs"), 1)
                        if u >= 1:
                            evacuate(h, u - 1)
                    evacuate(h, U - 1)
                    if diff:
                        act.wait_ge(sem("mean"), h + 1)
                        act.activation(norm[:, 1, :], norm[:, 0, :], ACT.Sqrt, scale=1.0 / P, bias=core.eps[:, 0:1]).then_inc(sem("norm_root"), 1)
                    for g in range(2):
                        act.wait_ge(sem("pt"), 4 + h * (GN + 4) + 2 + GN + g + 1)
                        act.activation(YH[:, bass.ds(h + y0, 1), g * HALF:(g + 1) * HALF].squeeze(1), flat(pT[(GN + g) % 2]), ACT.Copy,
                                       scale=gain[:, 0:1] if diff else 1.0).then_inc(sem("yh"), 1)

                def evacuate(h, u):
                    for n, (uu, g, count) in enumerate(groups):
                        if uu != u or n % 2 == 0:
                            continue
                        act.wait_ge(sem("pt"), 4 + h * (GN + 4) + 2 + n + 1)
                        act.wait_ge(sem("probs_t"), h * GN + n)
                        if u >= 2:
                            act.wait_ge(sem("o"), h * U + u - 1)
                        act.activation(PT[:, u % 2, g * P:(g + count) * P], flat(pT[n % 2])[:, 0:count * P], ACT.Copy).then_inc(sem("probs_t"), 1)

                act.wait_ge(sem("opened"), 1)
                if diff:
                    act.wait_ge(sem("gain_scaled"), 1)
                over_loop(act, NH, pair)

            @block.vector
            def _(dve):
                dve.sem_inc(sem("bias_free"), 1)
                dve.sem_inc(sem("reduced"), U)
                dve.sem_inc(sem("yl"), 1)
                dve.sem_inc(sem("o_taken"), 2)
                dve.sem_inc(sem("scores"), U)
                dve.sem_inc(sem("pt"), 4)
                dve.sem_inc(sem("opened"), 1)
                if diff:
                    dve.wait_ge(sem("lq"), 64)
                    for j in range(2):
                        dve.tensor_tensor_reduce(lq[:, 2 * j, :], lq[:, 2 * j, :], lq[:, 2 * j + 1, :], 1.0, 0.0, ALU.mult, ALU.add,
                                                 lam[:, j:j + 1]).then_inc(sem("lam_sums"), 1)
                    dve.wait_ge(sem("lam_exp"), 1)
                    dve.tensor_tensor(lam[:, 0:1], lam[:, 3:4], lam[:, 2:3], ALU.subtract).then_inc(sem("lam"), 1)
                    dve.wait_ge(sem("lam"), 1)
                    dve.tensor_scalar(lam[:, 0:1], lam[:, 0:1], -LAM_INIT, None, ALU.add).then_inc(sem("lam"), 1)
                    dve.wait_ge(sem("gain"), 16)
                    dve.tensor_scalar(gain[:, :], gain[:, :], 1.0 - LAM_INIT, None, ALU.mult).then_inc(sem("gain_scaled"), 1)
                    dve.wait_ge(sem("lam"), 2)
                    dve.wait_ge(sem("gain_scaled"), 1)
                with dve.Fori(0, NH) as h:
                    dve.wait_ge(sem("bias"), (h + 1) * 16)

                    def reduce(u):
                        b, c = u // 2, u % 2
                        n = (b + 1) * P
                        dve.wait_ge(sem("scores"), h * U + U + u + 1)
                        if u >= 2:
                            dve.wait_ge(sem("probs"), h * U + u - 1)
                        dve.memset(blank[:, u:u + 1], 0.0)
                        table = bias[:, 0, SEQ - n:SEQ] if diff else bias[:, c, 0:n]
                        dve.tensor_tensor_reduce(S[:, c, 0:n], flat(pS[c])[:, 0:n], table, 1.0, NEG, ALU.add, ALU.max,
                                                 mx[:, u:u + 1]).then_inc(sem("reduced"), 1)
                        dve.wait_ge(sem("reduced"), h * U + U + u + 1)
                        dve.tensor_scalar(nmx[:, u:u + 1], mx[:, u:u + 1], -1.0, None, ALU.mult).then_inc(sem("nmx"), 1)

                    def evacuate(u):
                        for n, (uu, g, count) in enumerate(groups):
                            if uu != u or n % 2:
                                continue
                            dve.wait_ge(sem("pt"), 4 + h * (GN + 4) + 2 + n + 1)
                            if n:
                                dve.wait_ge(sem("probs_t"), h * GN + n)
                            if u >= 2:
                                dve.wait_ge(sem("o"), h * U + u - 1)
                            dve.tensor_copy(PT[:, u % 2, g * P:(g + count) * P], flat(pT[n % 2])[:, 0:count * P]).then_inc(sem("probs_t"), 1)

                    def take(u):
                        b, c = u // 2, u % 2
                        dve.wait_ge(sem("probs"), h * U + u + 1)
                        dve.reciprocal(part[:, u:u + 1], total[:, u:u + 1]).then_inc(sem("part"), 1)
                        dve.wait_ge(sem("part"), h * U + u + 1)
                        if diff and c == 1:
                            dve.tensor_scalar(part[:, u:u + 1], part[:, u:u + 1], lam[:, 0:1], None, ALU.mult).then_inc(sem("part_lam"), 1)
                            dve.wait_ge(sem("part_lam"), h * NB + b + 1)
                        dve.wait_ge(sem("o"), h * U + u + 1)
                        if diff:
                            if c == 0:
                                dve.tensor_scalar(O[:, b, :], pO[0][:, 0, :], part[:, u:u + 1], None, ALU.mult).then_inc(sem("o_taken"), 1)
                            else:
                                dve.wait_ge(sem("o_taken"), h * U + u + 2)
                                dve.scalar_tensor_tensor(out=O[:, b, :], in0=pO[1][:, 0, :], scalar=part[:, u:u + 1], in1=O[:, b, :],
                                                         op0=ALU.mult, op1=ALU.add).then_inc(sem("o_taken"), 1)
                                dve.wait_ge(sem("o_taken"), h * U + u + 3)
                                dve.memset(blank[:, U + u:U + u + 1], 0.0)
                                dve.tensor_tensor_reduce(OS[:, b, :], O[:, b, :], O[:, b, :], 1.0, 0.0, ALU.mult, ALU.add,
                                                         norm[:, 0, b:b + 1]).then_inc(sem("square"), 1)
                        else:
                            dve.tensor_scalar(OS[:, b, c * 64:(c + 1) * 64], pO[c][:, 0, 0:64], part[:, u:u + 1], None, ALU.mult).then_inc(sem("o_taken"), 1)

                    reduce(0)
                    reduce(1)
                    for g in range(2):
                        dve.wait_ge(sem("pt"), 4 + h * (GN + 4) + g + 1)
                        dve.tensor_copy(V[:, g * 4:(g + 1) * 4, :], pT[g][:, :, :]).then_inc(sem("v"), 1)
                    for u in range(U):
                        evacuate(u)
                        if u + 2 < U:
                            reduce(u + 2)
                        take(u)
                    dve.sem_inc(sem("bias_free"), 1)
                    if diff:
                        dve.wait_ge(sem("square"), (h + 1) * NB)
                        dve.sem_inc(sem("mean"), 1)
                        dve.wait_ge(sem("norm_root"), h + 1)
                        dve.reciprocal(norm[:, 2, :], norm[:, 1, :]).then_inc(sem("rstd"), 1)
                        dve.wait_ge(sem("rstd"), h + 1)
                        dve.tensor_tensor(OS[:, :, :], O[:, :, :], norm[:, 2, :].unsqueeze(2).to_broadcast([P, NB, P]), ALU.mult).then_inc(sem("o_scaled"), 1)
                    else:
                        dve.wait_ge(sem("o_taken"), h * U + U + 2)
                        dve.sem_inc(sem("o_scaled"), 1)
                    for g in range(2):
                        dve.wait_ge(sem("yh"), h * 2 + g + 1)
                        y = YL[:, bass.ds(h + y0, 1), g * HALF:(g + 1) * HALF].squeeze(1)
                        yh = YH[:, bass.ds(h + y0, 1), g * HALF:(g + 1) * HALF].squeeze(1).bitcast(F32)
                        if diff:
                            dve.scalar_tensor_tensor(out=y, in0=flat(pT[(GN + g) % 2]), scalar=gain[:, 0:1], in1=yh,
                                                     op0=ALU.mult, op1=ALU.subtract).then_inc(sem("yl"), 1)
                        else:
                            dve.tensor_tensor(y, flat(pT[(GN + g) % 2]), yh, ALU.subtract).then_inc(sem("yl"), 1)


LAM_INIT = 0.8 - 0.6 * 1.0


D_FF = 2816
FCH = D_FF // P


def stage_ffn(core, X):
    nc, io = core.nc, core.io
    AH, AL = core.AH, core.AL
    up, down = io["ffn_up"][0], io["ffn_down"][0]
    G = 2
    NG = FCH // G
    with stage(core) as (ctx, sem):
        W = WeightTiles(core, ctx, sem, KD)
        V = WeightTiles(core, ctx, sem, G, D, name="v", slots=1)
        taps = sbuf(core, ctx, "taps", [P, 3, 2 * FCH])
        bias = sbuf(core, ctx, "bias", [P, 2 * FCH])
        UG = sbuf(core, ctx, "u_gate", [P, SEQ])
        UV = sbuf(core, ctx, "u_val", [P, SEQ])
        FH = sbuf(core, ctx, "f_high", [P, G, SEQ], F32R)
        FL = sbuf(core, ctx, "f_low", [P, G, SEQ], F32R)
        pU = [psum(core, ctx, f"pu{s}", [P, 2, HALF]) for s in range(2)]
        pD = psum(core, ctx, "pd", [P, 4, HALF])
        flat = lambda t: t[:, :, :].rearrange("p a b -> p (a b)")
        with nc.Block() as block:

            @block.sync
            def _(sp):
                for j in range(3):
                    sp.dma_start(taps[:, j, :], per_channel(io["ffn_conv_w"][0, j])).then_inc(sem("small"), 16)
                sp.dma_start(bias[:, :], per_channel(io["ffn_conv_b"][0])).then_inc(sem("small"), 16)
                with sp.Fori(0, NG) as i:
                    for j in range(G):
                        W.load(sp, 0, i * G + j, up[:, bass.ds((i * G + j) * P, P)])
                        W.load(sp, 1, i * G + j, up[:, bass.ds((i * G + j + FCH) * P, P)])
                        if j == 0:
                            V.load(sp, 0, i, down[bass.ds(i * (G * P), G * P), :])

            @block.gpsimd
            def _(pool):
                W.open_pool(pool)
                V.open_pool(pool)
                with pool.Fori(0, NG) as i:
                    for j in range(G):
                        W.split_low(pool, 0, i * G + j)
                        W.split_low(pool, 1, i * G + j)
                    V.split_low(pool, 0, i)

            @block.tensor
            def _(pe):
                W.open_pe(pe)
                V.open_pe(pe)

                def project(i, j, slot):
                    W.wait(pe, slot, i * G + j)
                    pe.wait_ge(sem(f"pu_free{slot}"), i * G + j + 1)
                    W.multiply(pe, slot, pU[slot], AH, AL)

                def output(i):
                    V.wait(pe, 0, i)
                    pe.wait_ge(sem("f_low"), i * G + G)
                    for q in range(2 * NB):
                        b, half = q // 2, q % 2
                        pe.wait_ge(sem("added"), i * 2 * NB + q + 1)
                        n = 0
                        for k in range(G):
                            for x, w in ((FH, V.high), (FL, V.high), (FH, V.low)):
                                last = pe.matmul(pD[:, q % 4, :], x[:, k, b * P:(b + 1) * P], w[0][:, k, half * HALF:(half + 1) * HALF],
                                                 start=(n == 0), stop=(n == 3 * G - 1))
                                n += 1
                        if q < 2 * NB - 1:
                            last.then_inc(sem("pd"), 1)
                    last.then_inc(V.s("used", 0), 1)

                def group(i, first):
                    project(i, 0, 0)
                    if not first:
                        output(i - 1)
                    project(i, 0, 1)
                    project(i, 1, 0)
                    project(i, 1, 1)

                group(0, True)
                with pe.Fori(1, NG) as i:
                    group(i, False)
                output(NG - 1)

            @block.scalar
            def _(act):
                act.wait_ge(sem("small"), 64)
                W.split_high(act, 0, 0)
                W.split_high(act, 1, 0)

                def group(i, more):
                    for j in range(G):
                        turn = i * G + j
                        for slot, U in ((0, UG), (1, UV)):
                            n = i * G + j + slot * FCH
                            act.wait_ge(W.s("used", slot), turn + 2)
                            act.wait_ge(sem(f"u_free{slot}"), turn + 1)
                            act.activation(U[:, :], flat(pU[slot]), ACT.Identity, scale=taps[:, 2, bass.ds(n, 1)],
                                           bias=bias[:, bass.ds(n, 1)]).then_inc(sem(f"tap2_{slot}"), 1)
                            if more or j < G - 1:
                                W.split_high(act, slot, turn + 1)
                            if slot == 0:
                                act.wait_ge(sem("pu_free0"), turn + 2)
                                act.activation(UG[:, :], UG[:, :], ACT.Gelu_apprx_tanh).then_inc(sem("gelu"), 1)
                        act.wait_ge(sem("product"), turn + 1)
                        act.wait_ge(V.s("used", 0), i + 1)
                        act.activation(FH[:, j, :], UV[:, :], ACT.Copy).then_inc(sem("f_high"), 1)
                        if j == 0:
                            V.split_high(act, 0, i)
                over_loop(act, NG, group)

            @block.vector
            def _(dve):
                for slot in range(2):
                    dve.sem_inc(sem(f"pu_free{slot}"), 1)
                    dve.sem_inc(sem(f"u_free{slot}"), 1)
                dve.sem_inc(sem("added"), 4)

                def add(i):
                    for q in range(2 * NB):
                        b, half = q // 2, q % 2
                        if q < 2 * NB - 1:
                            dve.wait_ge(sem("pd"), i * (2 * NB - 1) + q + 1)
                        else:
                            dve.wait_ge(V.s("used", 0), i + 2)
                        cols = slice(half * HALF, (half + 1) * HALF)
                        dve.tensor_tensor(X[:, b, cols], X[:, b, cols], pD[:, q % 4, :], ALU.add).then_inc(sem("added"), 1)

                def hidden(i, j, slot):
                    turn = i * G + j
                    U = (UG, UV)[slot]
                    n = i * G + j + slot * FCH
                    x = flat(pU[slot])
                    dve.wait_ge(sem(f"tap2_{slot}"), turn + 1)
                    dve.scalar_tensor_tensor(out=U[:, 1:], in0=x[:, :SEQ - 1], scalar=taps[:, 1, bass.ds(n, 1)], in1=U[:, 1:],
                                             op0=ALU.mult, op1=ALU.add).then_inc(sem(f"tap1_{slot}"), 1)
                    dve.wait_ge(sem(f"tap1_{slot}"), turn + 1)
                    dve.scalar_tensor_tensor(out=U[:, 2:], in0=x[:, :SEQ - 2], scalar=taps[:, 0, bass.ds(n, 1)], in1=U[:, 2:],
                                             op0=ALU.mult, op1=ALU.add).then_inc(sem(f"pu_free{slot}"), 1)
                    if slot == 1:
                        dve.wait_ge(sem("gelu"), turn + 1)
                        dve.wait_ge(sem("pu_free1"), turn + 2)
                        dve.tensor_tensor(UV[:, :], UV[:, :], UG[:, :], ALU.mult).then_inc(sem("product"), 1)
                        dve.wait_ge(sem("product"), turn + 1)
                        dve.sem_inc(sem("u_free0"), 1)
                        dve.wait_ge(sem("f_high"), turn + 1)
                        dve.tensor_tensor(FL[:, j, :], UV[:, :], FH[:, j, :].bitcast(F32), ALU.subtract).then_inc(sem("f_low"), 1)
                        dve.wait_ge(sem("f_low"), turn + 1)
                        dve.sem_inc(sem("u_free1"), 1)

                def group(i, first):
                    hidden(i, 0, 0)
                    if not first:
                        add(i - 1)
                    hidden(i, 0, 1)
                    hidden(i, 1, 0)
                    hidden(i, 1, 1)

                group(0, True)
                with dve.Fori(1, NG) as i:
                    group(i, False)
                add(NG - 1)


def stage_norm_time(core, X, gain, keep=None, residual=None, out=None):
    nc = core.nc
    with stage(core) as (ctx, sem):
        g = sbuf(core, ctx, "gain", [P, D])
        squares = sbuf(core, ctx, "squares", [P, 2, D])
        other = sbuf(core, ctx, "other", [P, NB, D]) if residual is not None else None
        stats = sbuf(core, ctx, "stats", [P, 3, NB])
        with nc.Block() as block:

            @block.sync
            def _(sp):
                sp.dma_start(g[:, :], gain.partition_broadcast(P)).then_inc(sem("gain"), 16)
                if residual is not None:
                    sp.dma_start(other[:, :, :], residual.rearrange("(b p) n -> p b n", p=P)).then_inc(sem("residual"), 16)
                dst = keep if keep is not None else out
                if dst is not None:
                    for b in range(NB):
                        sp.wait_ge(sem("done"), b + 1)
                        sp.dma_start(dst[b * P:(b + 1) * P, :], X[:, b, :]).then_inc(sem("stored"), 16)
                    sp.wait_ge(sem("stored"), 16 * NB)

            @block.scalar
            def _(act):
                for b in range(NB):
                    act.activation(squares[:, b % 2, :], X[:, b, :], ACT.Square, accum_out=stats[:, 0, b:b + 1]).then_inc(sem("squared"), 1)
                    act.wait_ge(sem("squared"), b + 1)
                act.activation(stats[:, 1, :], stats[:, 0, :], ACT.Sqrt, scale=1.0 / D, bias=core.eps[:, 0:1]).then_inc(sem("root"), 1)

            @block.vector
            def _(dve):
                dve.wait_ge(sem("root"), 1)
                dve.reciprocal(stats[:, 2, :], stats[:, 1, :]).then_inc(sem("rstd"), 1)
                dve.wait_ge(sem("rstd"), 1)
                dve.wait_ge(sem("gain"), 16)
                if residual is not None:
                    dve.wait_ge(sem("residual"), 16)
                for b in range(NB):
                    dve.scalar_tensor_tensor(out=X[:, b, :], in0=X[:, b, :], scalar=stats[:, 2, b:b + 1], in1=g[:, :],
                                             op0=ALU.mult, op1=ALU.mult).then_inc(sem("done" if residual is None else "scaled"), 1)
                    if residual is not None:
                        dve.wait_ge(sem("scaled"), b + 1)
                        dve.tensor_tensor(X[:, b, :], X[:, b, :], other[:, b, :], ALU.add).then_inc(sem("done"), 1)


def first_block(core):
    io, nc = core.io, core.nc
    with ExitStack() as ctx:
        x0 = sbuf(core, ctx, "x0", [P, NB, D])
        stage_norm_to_channels(core, x0, io["norm1_g"][0], io["x"][0])
    M = nc.alloc_sbuf_tensor_at("m_top", [P, KD, SEQ], F32, offset=nc.sbuf_top - 4 * KD * SEQ)
    core.M = M
    with ExitStack() as ctx:
        core.YH = sbuf(core, ctx, "y_high", [P, KD, SEQ], F32R)
        core.YL = sbuf(core, ctx, "y_low", [P, KD, SEQ], F32R)
        stage_attention_tables(core)
        stage_attention(core, "diff", 2 * D, 2 * D + HALF, 2 * D + 2 * HALF, 0)
        stage_attention(core, "fox", 2 * D + 3 * HALF, 2 * D + 4 * HALF, 2 * D + 5 * HALF, 4)
        stage_branches(core, [(1, io["w_br_diff"][0], 4, 0), (2, io["w_br_fox"][0], 4, 4)], part_out=core.m_part)
        stage_rnn(core)
        stage_branches(core, [(0, io["w_br_rnn"][0], 8, 0)], part_in=core.m_part)
    with ExitStack() as ctx:
        X = sbuf(core, ctx, "x", [P, NB, D])
        stage_rows(core, core.AH, core.AL, KD, io["w_out"][0], X, whole=M, load_acc=io["x"][0])
        stage_norm_to_channels(core, X, io["norm2_g"][0])
        stage_ffn(core, X)
        stage_norm_time(core, X, io["final_g"], keep=core.x_mid)
        stage_norm_to_channels(core, X, io["pre_norm_w_2"][0])


Z_AT, XBC_AT, DT_AT = 0, 1024, 2560
Q_AT, F_AT, I_AT, G_AT = 2576, 3088, 3600, 4112
U_AT, S5G_AT = 4624, 5136
SSD_H = 16
GH = 8
SSD_CH = 12


class Overlay:

    def __init__(self, core, start, size):
        self.core, self.at, self.end = core, (start + 31) // 32 * 32, start + size

    def take(self, name, shape, dtype=F32):
        size = 4 * int(np.prod(shape[1:]))
        size = (size + 31) // 32 * 32
        assert self.at + size <= self.end, name
        self.core.serial += 1
        t = self.core.nc.alloc_sbuf_tensor_at(f"{name}_{self.core.serial}", shape, dtype, offset=self.at)
        self.at += size
        return t


def flat2(t):
    return t[:, :, :].rearrange("p a b -> p (a b)")


def stage_ssd_steps(core, dtN, acN):
    nc, io = core.nc, core.io
    with stage(core) as (ctx, sem):
        W = WeightTiles(core, ctx, sem, KD, slots=1)
        vec = sbuf(core, ctx, "vec", [SSD_H, 4])
        z, dt, ac, keep = (sbuf(core, ctx, n, [SSD_H, SEQ]) for n in ("z", "dt", "ac", "keep"))
        soft = Softplus(core, ctx, sem, "sp", [SSD_H, SEQ])
        pD = psum(core, ctx, "pd", [P, 2, HALF])
        pN = psum(core, ctx, "pn", [P, 2, NB, SSD_H])
        with nc.Block() as block:

            @block.sync
            def _(sp):
                W.load(sp, 0, 0, io["w_in_2"][0][:, DT_AT:DT_AT + P])
                sp.dma_start(vec[:, 0:1], io["ssd_dt_bias_2"].rearrange("a n -> n a")).then_inc(sem("vec"), 16)
                sp.dma_start(vec[:, 1:2], io["ssd_a_log_2"].rearrange("a n -> n a")).then_inc(sem("vec"), 16)
                sp.wait_ge(sem("ac"), 1)
                sp.dma_start(core.acum, ac[:, :]).then_inc(sem("stored"), 16)
                sp.wait_ge(sem("stored"), 16)

            @block.gpsimd
            def _(pool):
                W.open_pool(pool)
                pool.memset(keep[:, :], 1.0).then_inc(sem("keep0"), 1)
                pool.wait_ge(sem("keep0"), 1)
                pool.memset(keep[:, :].rearrange("p (c t) -> p c t", t=P)[:, :, 0:1], 0.0).then_inc(sem("keep"), 1)
                W.split_low(pool, 0, 0)

            @block.scalar
            def _(act):
                W.split_high(act, 0, 0)
                act.wait_ge(sem("vec"), 32)
                act.activation(vec[:, 2:3], vec[:, 1:2], ACT.Exp).then_inc(sem("ea"), 1)
                act.wait_ge(sem("z"), 1)
                soft.on_act(act, z[:, :])

            @block.tensor
            def _(pe):
                W.open_pe(pe)
                W.wait(pe, 0, 0)
                W.multiply(pe, 0, pD, core.AH, core.AL)
                pe.wait_ge(soft.s("out"), 1)
                pe.wait_ge(sem("ac"), 1)
                for j, src in enumerate((dt, ac)):
                    for c in range(NB):
                        last = pe.transpose(pN[:, j, c, :], src[:, c * P:(c + 1) * P], core.ident[0:SSD_H, 0:SSD_H])
                last.then_inc(sem("turned"), 1)

            @block.vector
            def _(dve):
                dve.wait_ge(sem("vec"), 32)
                dve.wait_ge(W.s("used", 0), 2)
                dve.tensor_scalar(z[:, :], pD[0:SSD_H, :, :].rearrange("p a b -> p (a b)"), vec[:, 0:1], None, ALU.add).then_inc(sem("z"), 1)
                dve.wait_ge(sem("z"), 1)
                soft.on_dve(dve, z[:, :], dt[:, :])
                dve.wait_ge(sem("ea"), 1)
                dve.wait_ge(soft.s("out"), 1)
                dve.tensor_scalar(z[:, :], dt[:, :], vec[:, 2:3], -1.0, ALU.mult, ALU.mult).then_inc(sem("dta"), 1)
                dve.wait_ge(sem("dta"), 1)
                dve.wait_ge(sem("keep"), 1)
                dve.tensor_tensor_scan(ac[:, :], keep[:, :], z[:, :], 0.0, ALU.mult, ALU.add).then_inc(sem("ac"), 1)
                dve.wait_ge(sem("turned"), 1)
                dve.tensor_copy(dtN[:, :, :], pN[:, 0, :, :]).then_inc(sem("n"), 1)
                dve.tensor_copy(acN[:, :, :], pN[:, 1, :, :]).then_inc(sem("n"), 1)


def stage_ssd_project(core, XBC, ZT):
    nc, io = core.nc, core.io
    w_in = io["w_in_2"][0]
    with stage(core) as (ctx, sem):
        W = WeightTiles(core, ctx, sem, KD)
        taps = sbuf(core, ctx, "taps", [P, 4, SSD_CH])
        bias = sbuf(core, ctx, "bias", [P, SSD_CH])
        pU = [psum(core, ctx, f"pu{s}", [P, 2, HALF]) for s in range(2)]
        TAIL = SSD_CH - KD

        with nc.Block() as block:

            @block.sync
            def _(sp):
                for j in range(4):
                    sp.dma_start(taps[:, j, :], per_channel(io["ssd_conv_w_2"][0, j])).then_inc(sem("small"), 16)
                sp.dma_start(bias[:, :], per_channel(io["ssd_conv_b_2"][0])).then_inc(sem("small"), 16)
                with sp.Fori(0, KD) as n:
                    W.load(sp, 0, n, w_in[:, bass.ds(n * P + XBC_AT, P)])
                    W.load(sp, 1, n, w_in[:, bass.ds(n * P + Z_AT, P)])
                for j in range(TAIL):
                    at = XBC_AT + (KD + j) * P
                    W.load(sp, j % 2, KD + j // 2, w_in[:, at:at + P])

            @block.gpsimd
            def _(pool):
                W.open_pool(pool)
                with pool.Fori(0, KD + TAIL // 2) as n:
                    W.split_low(pool, 0, n)
                    W.split_low(pool, 1, n)

            @block.tensor
            def _(pe):
                W.open_pe(pe)
                with pe.Fori(0, KD + TAIL // 2) as n:
                    for s in range(2):
                        W.wait(pe, s, n)
                        pe.wait_ge(sem(f"pu_free{s}"), n + 1)
                        W.multiply(pe, s, pU[s], core.AH, core.AL)

            @block.scalar
            def _(act):
                act.wait_ge(sem("small"), 80)
                W.split_high(act, 0, 0)
                W.split_high(act, 1, 0)

                def conv(s, turn, n, more):
                    tile = XBC[:, bass.ds(n, 1), :].squeeze(1)
                    act.wait_ge(W.s("used", s), turn + 2)
                    act.activation(tile, flat2(pU[s]), ACT.Identity, scale=taps[:, 3, bass.ds(n, 1)],
                                   bias=bias[:, bass.ds(n, 1)]).then_inc(sem("tap3"), 1)
                    if more:
                        W.split_high(act, s, turn + 1)

                def silu(n):
                    tile = XBC[:, bass.ds(n, 1), :].squeeze(1)
                    act.wait_ge(sem("conv"), n + 1)
                    act.sem_inc(sem("act_asked"), 1)
                    act.activation(tile, tile, ACT.Silu).then_inc(sem("silu"), 1)

                with act.Fori(0, KD) as n:
                    conv(0, n, n, True)
                    act.wait_ge(W.s("used", 1), n + 2)
                    act.activation(ZT[:, bass.ds(n, 1), :].squeeze(1), flat2(pU[1]), ACT.Silu).then_inc(sem("z"), 1)
                    W.split_high(act, 1, n + 1)
                    silu(n)
                for j in range(TAIL):
                    conv(j % 2, KD + j // 2, KD + j, j < TAIL - 2)
                    silu(KD + j)

            @block.vector
            def _(dve):
                dve.sem_inc(sem("pu_free0"), 1)
                dve.sem_inc(sem("pu_free1"), 1)

                def conv(s, n):
                    tile, x = XBC[:, bass.ds(n, 1), :].squeeze(1), flat2(pU[s])
                    dve.wait_ge(sem("tap3"), n + 1)
                    for back in (1, 2, 3):
                        ins = dve.scalar_tensor_tensor(out=tile[:, back:], in0=x[:, :SEQ - back], scalar=taps[:, 3 - back, bass.ds(n, 1)],
                                                       in1=tile[:, back:], op0=ALU.mult, op1=ALU.add)
                        if back < 3:
                            ins.then_inc(sem("taps"), 1)
                            dve.wait_ge(sem("taps"), n * 2 + back)
                    ins.then_inc(sem("conv"), 1)
                    dve.wait_ge(sem("conv"), n + 1)
                    dve.sem_inc(sem(f"pu_free{s}"), 1)

                with dve.Fori(0, KD) as n:
                    conv(0, n)
                    dve.wait_ge(sem("z"), n + 1)
                    dve.sem_inc(sem("pu_free1"), 1)
                for j in range(TAIL):
                    conv(j % 2, KD + j)


def stage_ssd_chunks(core, XBC, ZT, dtN, acN):
    nc, io = core.nc, core.io
    with stage(core) as (ctx, sem):
        lay = Overlay(core, core.act_at, 2 * 4 * KD * SEQ)
        two = range(2)
        acB = [lay.take(f"acum_rows{s}", [P, GH, P]) for s in two]
        E = [lay.take(f"decay{s}", [P, GH, P]) for s in two]
        XS = [lay.take(f"x_chunk{s}", [P, 4, P]) for s in two]
        BS = [lay.take(f"b_chunk{s}", [P, P]) for s in two]
        CS = [lay.take(f"c_chunk{s}", [P, P]) for s in two]
        XD = [lay.take(f"x_skip{s}", [P, 4, P]) for s in two]
        xdt = [lay.take(f"x_dt{s}", [P, GH, 64]) for s in two]
        xde = [lay.take(f"x_dt_end{s}", [P, GH, 64]) for s in two]
        BN = [lay.take(f"b_time{s}", [P, P]) for s in two]
        small = [lay.take(f"small{s}", [P, 4, GH]) for s in two]
        Y = [lay.take(f"y{s}", [P, GH, 64]) for s in two]
        T = [lay.take(f"y_skip{s}", [P, 4, P]) for s in two]
        ST = lay.take("state", [P, GH, 64])
        skip = lay.take("skip", [P, KD])
        pX = psum(core, ctx, "px", [P, 4, P])
        pB = psum(core, ctx, "pb", [P, P])
        pC = psum(core, ctx, "pc", [P, P])
        pYD = psum(core, ctx, "pyd", [P, GH, 64])
        pYO = psum(core, ctx, "pyo", [P, GH, 64])
        pS = psum(core, ctx, "pst", [P, GH, 64])
        pT = [psum(core, ctx, f"pty{s}", [P, 4, P]) for s in two]

        def loops(engine, prepare, finish=None, before=None):
            for g in range(2):
                if before is not None:
                    before(g)

                def at(body, pair, c):
                    if body is not None:
                        body(g, pair * 2 + c, pair * 2 + (c + g * NB), c % 2, pair + (c // 2 + g * (NB // 2)))

                at(prepare, 0, 0)
                with engine.Fori(0, NB // 2 - 1) as pair:
                    for c in two:
                        at(prepare, pair, c + 1)
                        at(finish, pair, c)
                at(prepare, NB // 2 - 1, 1)
                at(finish, NB // 2 - 1, 0)
                at(finish, NB // 2 - 1, 1)

        with nc.Block() as block:

            @block.sync
            def _(sp):
                for k in range(KD):
                    for j in range(2):
                        sp.dma_start(skip[j * 64:(j + 1) * 64, k:k + 1], io["ssd_d_2"][0, 2 * k + j:2 * k + j + 1].partition_broadcast(64)).then_inc(sem("skip"), 16)

                def prepare(g, c, it, s, turn):
                    sp.wait_ge(sem("seg"), it + 1)
                    sp.wait_ge(sem("small"), it + 1)
                    src = core.acum[g * GH:(g + 1) * GH, bass.ds(c * P, P)]
                    sp.sem_inc(sem("asked"), 1)
                    sp.dma_start(acB[s][:, :, :], src.partition_broadcast(P)).then_inc(sem(f"rows{s}"), 16)
                loops(sp, prepare)

            @block.gpsimd
            def _(pool):
                pool.wait_ge(sem("skip"), 16 * 2 * KD)
                fill = pool.to_reg(NEG)
                pool.sem_inc(sem("xd"), 2)

                def prepare(g, c, it, s, turn):
                    pool.wait_ge(sem("skipped"), it + 1)
                    pool.wait_ge(sem("xs"), it + 1)
                    pool.tensor_tensor(XD[s][:, :, :], XS[s][:, :, :], skip[:, g * 4:(g + 1) * 4].unsqueeze(2).to_broadcast([P, 4, P]),
                                       ALU.mult).then_inc(sem("xd"), 1)
                    pool.wait_ge(sem("seg"), it + 3)
                    pool.sem_inc(sem("pool_asked"), 1)
                    pool.affine_select(out=E[s][:, :, :], in_=E[s][:, :, :], compare_op=ALU.is_ge, fill=fill, base=0,
                                       pattern=[[0, GH], [1, P]], channel_multiplier=-1).then_inc(sem("masked"), 1)
                loops(pool, prepare)

            @block.scalar
            def _(act):
                act.sem_inc(sem("small"), 2)

                def prepare(g, c, it, s, turn):
                    steps = bass.ds(c * P, P)
                    act.wait_ge(sem("scores"), it + 1)
                    act.wait_ge(sem("xd"), it + 1)
                    act.sem_inc(sem("act_asked"), 1)
                    act.activation(XS[s][:, :, :], XBC[:, g * 4:(g + 1) * 4, steps], ACT.Copy).then_inc(sem("xs"), 1)
                    act.activation(BS[s][:, :], XBC[:, KD + g, steps], ACT.Copy).then_inc(sem("bs"), 1)
                    act.wait_ge(sem("pyo"), it + 1)
                    act.sem_inc(sem("act_asked"), 1)
                    act.activation(CS[s][:, :], XBC[:, KD + 2 + g, steps], ACT.Copy).then_inc(sem("cs"), 1)
                    act.wait_ge(sem(f"rows{s}"), turn * 16 + 16)
                    act.wait_ge(sem("state"), it + 1)
                    act.sem_inc(sem("act_asked"), 1)
                    act.activation(small[s][:, 2, :], acN[:, bass.ds(c, 1), g * GH:(g + 1) * GH].squeeze(1), ACT.Exp).then_inc(sem("ea"), 1)
                    act.activation(small[s][:, 3, :], acB[s][:, :, P - 1], ACT.Exp).then_inc(sem("small"), 1)
                    act.wait_ge(sem("to_end"), it + 1)
                    act.activation(small[s][:, 1, :], small[s][:, 0, :], ACT.Exp).then_inc(sem("dte"), 1)
                    act.wait_ge(sem("masked"), it + 1)
                    act.activation(E[s][:, :, :], E[s][:, :, :], ACT.Exp).then_inc(sem("decay"), 1)
                    act.wait_ge(sem("b_turned"), it + 1)
                    act.activation(BN[s][:, :], pB[:, :], ACT.Copy).then_inc(sem("bn"), 1)
                loops(act, prepare)

            @block.tensor
            def _(pe):
                ident = core.ident
                pe.sem_inc(sem("y_turned"), 2)
                pe.sem_inc(sem("ydiag"), 2)
                pe.sem_inc(sem("scores"), 2)
                pe.sem_inc(sem("pyo"), 2)

                def prepare(g, c, it, s, turn):
                    pe.wait_ge(sem("xs"), it + 1)
                    pe.wait_ge(sem("cs"), it + 1)
                    pe.wait_ge(sem("bs"), it + 1)
                    pe.wait_ge(sem("x_dt"), it + 1)
                    for j in range(4):
                        last = pe.transpose(pX[:, j, :], XS[s][:, j, :], ident[:, :])
                    last.then_inc(sem("x_turned"), 1)
                    pe.wait_ge(sem("bn"), it + 1)
                    pe.wait_ge(sem("mt"), it + 1)
                    pe.transpose(pB[:, :], BS[s][:, :], ident[:, :]).then_inc(sem("b_turned"), 1)
                    pe.matmul(pC[:, :], BS[s][:, :], CS[s][:, :], start=True, stop=True).then_inc(sem("scores"), 1)

                def finish(g, c, it, s, turn):
                    pe.wait_ge(sem("state"), it + 2)
                    pe.wait_ge(sem("y_off"), it + 1)
                    pe.matmul(pYO[:, :, :].rearrange("p a b -> p (a b)"), CS[s][:, :], ST[:, :, :].rearrange("p a b -> p (a b)"), start=True, stop=True).then_inc(sem("pyo"), 1)
                    pe.wait_ge(sem("bn"), it + 2)
                    pe.wait_ge(sem("x_dte"), it + 1)
                    pe.matmul(pS[:, :, :].rearrange("p a b -> p (a b)"), BN[s][:, :], xde[s][:, :, :].rearrange("p a b -> p (a b)"), start=True, stop=True).then_inc(sem("pst"), 1)
                    pe.wait_ge(sem("mt"), it + 2)
                    pe.wait_ge(sem("y"), it + 2)
                    for h in range(GH):
                        last = pe.matmul(pYD[:, h, :], E[s][:, h, :], xdt[s][:, h, :], start=True, stop=True)
                    last.then_inc(sem("ydiag"), 1)
                    pe.wait_ge(sem("y"), it + 3)
                    pe.wait_ge(sem("skipped"), it + 1)
                    yv = Y[s][:, :, :].rearrange("p (j a) b -> p j (a b)", j=4)
                    for j in range(4):
                        last = pe.transpose(pT[s][:, j, :], yv[:, j, :], ident[:, :])
                    last.then_inc(sem("y_turned"), 1)
                loops(pe, prepare, finish, lambda g: pe.wait_ge(sem("cleared"), g + 1))

            @block.vector
            def _(dve):
                for name, n in (("seg", 2), ("skipped", 2), ("state", 2), ("x_dt", 1), ("mt", 1), ("y_off", 1), ("y", 2)):
                    dve.sem_inc(sem(name), n)
                dve.sem_inc(sem("bn"), 1)
                wide = lambda t: t.unsqueeze(2).to_broadcast([P, GH, 64])

                def prepare(g, c, it, s, turn):
                    heads = slice(g * GH, (g + 1) * GH)
                    ac_c = acN[:, bass.ds(c, 1), heads].squeeze(1)
                    dve.wait_ge(sem(f"rows{s}"), turn * 16 + 16)
                    dve.wait_ge(sem("ydiag"), it + 1)
                    dve.tensor_tensor(small[s][:, 0, :], acB[s][:, :, P - 1], ac_c, ALU.subtract).then_inc(sem("to_end"), 1)
                    dve.tensor_tensor(E[s][:, :, :], acB[s][:, :, :], ac_c.unsqueeze(2).to_broadcast([P, GH, P]), ALU.subtract).then_inc(sem("seg"), 1)
                    dve.wait_ge(sem("x_turned"), it + 1)
                    dve.tensor_tensor(xdt[s][:, :, :], pX[:, :, :].rearrange("p a b -> p (a b)").rearrange("p (h d) -> p h d", d=64),
                                      wide(dtN[:, bass.ds(c, 1), heads].squeeze(1)), ALU.mult).then_inc(sem("x_dt"), 1)
                    dve.wait_ge(sem("x_dt"), it + 2)
                    dve.wait_ge(sem("dte"), it + 1)
                    dve.tensor_tensor(xde[s][:, :, :], xdt[s][:, :, :], wide(small[s][:, 1, :]), ALU.mult).then_inc(sem("x_dte"), 1)
                    dve.wait_ge(sem("decay"), it + 1)
                    dve.wait_ge(sem("scores"), it + 3)
                    dve.tensor_tensor(E[s][:, :, :], E[s][:, :, :], pC[:, :].unsqueeze(1).to_broadcast([P, GH, P]), ALU.mult).then_inc(sem("mt"), 1)

                def finish(g, c, it, s, turn):
                    steps = bass.ds(c * P, P)
                    dve.wait_ge(sem("ea"), it + 1)
                    dve.wait_ge(sem("pyo"), it + 3)
                    dve.tensor_tensor(Y[s][:, :, :], pYO[:, :, :], wide(small[s][:, 2, :]), ALU.mult).then_inc(sem("y_off"), 1)
                    dve.wait_ge(sem("small"), it + 3)
                    dve.tensor_tensor(ST[:, :, :], ST[:, :, :], wide(small[s][:, 3, :]), ALU.mult).then_inc(sem("decayed"), 1)
                    dve.wait_ge(sem("decayed"), it + 1)
                    dve.wait_ge(sem("pst"), it + 1)
                    dve.tensor_tensor(ST[:, :, :], ST[:, :, :], pS[:, :, :], ALU.add).then_inc(sem("state"), 1)
                    dve.wait_ge(sem("y_off"), it + 2)
                    dve.wait_ge(sem("ydiag"), it + 3)
                    dve.tensor_tensor(Y[s][:, :, :], Y[s][:, :, :], pYD[:, :, :], ALU.add).then_inc(sem("y"), 1)
                    dve.wait_ge(sem("y_turned"), it + 3)
                    dve.wait_ge(sem("xd"), it + 3)
                    dve.tensor_tensor(T[s][:, :, :], pT[s][:, :, :], XD[s][:, :, :], ALU.add).then_inc(sem("skipped"), 1)
                    dve.wait_ge(sem("skipped"), it + 3)
                    zt = ZT[:, g * 4:(g + 1) * 4, steps]
                    dve.tensor_tensor(zt, zt, T[s][:, :, :], ALU.mult).then_inc(sem("gated"), 1)

                def clear(g):
                    if g:
                        dve.wait_ge(sem("state"), NB * g + 2)
                        dve.wait_ge(sem("pyo"), NB * g + 2)
                    dve.memset(ST[:, :, :], 0.0).then_inc(sem("cleared"), 1)
                    dve.wait_ge(sem("cleared"), g + 1)
                loops(dve, prepare, finish, clear)


def stage_mix_rows(core, src, chunks, per_group, gain, high, low, w, acc, factor=None, add=True):
    nc = core.nc
    NG = chunks // per_group
    KT = 4
    NK = chunks // KT
    tiles = [(half, kt) for half in range(2) for kt in range(NK)]
    with stage(core) as (ctx, sem):
        W = WeightTiles(core, ctx, sem, KT, HALF)
        sq = [sbuf(core, ctx, f"sq{s}", [P, SEQ]) for s in range(2)]
        diag = sbuf(core, ctx, "diag", [P, NB, P])
        gains = sbuf(core, ctx, "gains", [P, chunks])
        stats = sbuf(core, ctx, "stats", [P, 3, NG, NB])
        out = psum(core, ctx, "rows", [P, NB, HALF])
        sums = out[:, NB - 1, 0:chunks * NB].rearrange("p (k b) -> p k b", b=NB)
        spread = [out[:, 2 * s:2 * s + 2, :] for s in range(2)]

        with nc.Block() as block:

            @block.sync
            def _(sp):
                sp.dma_start(gains[:, :], per_channel(gain)).then_inc(sem("gains"), 16)
                for t, (half, kt) in enumerate(tiles):
                    W.load(sp, t % 2, t // 2, w[kt * KT * P:(kt + 1) * KT * P, half * HALF:(half + 1) * HALF])

            @block.gpsimd
            def _(pool):
                W.open_pool(pool)
                for t in range(len(tiles)):
                    W.split_low(pool, t % 2, t // 2)

            @block.tensor
            def _(pe):
                W.open_pe(pe)
                for k in range(chunks):
                    pe.wait_ge(sem(f"squared{k % 2}"), k // 2 + 1)
                    for b in range(NB):
                        last = pe.matmul(sums[:, k, b:b + 1], sq[k % 2][:, b * P:(b + 1) * P], core.ones[:, 0:1], start=True, stop=True)
                    last.then_inc(sem("summed"), 1)
                for g in range(NG):
                    pe.wait_ge(sem("diag"), g + 1)
                    if g >= 2:
                        pe.wait_ge(sem("scaled"), (g - 1) * per_group)
                    for h in range(2):
                        last = pe.matmul(spread[g % 2][:, h, :], core.ones[:, :], flat2(diag)[:, h * HALF:(h + 1) * HALF], start=True, stop=True)
                    last.then_inc(sem("spread"), 1)
                pe.wait_ge(sem("scaled"), chunks)
                for t, (half, kt) in enumerate(tiles):
                    W.wait(pe, t % 2, t // 2)
                    for b in range(NB):
                        if half and kt == 0:
                            pe.wait_ge(sem("added"), b + 1)
                        for k in range(KT):
                            kk = kt * KT + k
                            if b == 0 and half == 0:
                                pe.wait_ge(sem("low"), kk + 1)
                            for i, (x, v) in enumerate(((high, W.high), (low, W.high), (high, W.low))):
                                last = pe.matmul(out[:, b, :], x[:, kk, b * P:(b + 1) * P], v[t % 2][:, k, :],
                                                 start=(kk == 0 and i == 0), stop=(kk == chunks - 1 and i == 2))
                        if kt == NK - 1 and b < NB - 1:
                            last.then_inc(sem("out"), 1)
                    last.then_inc(W.s("used", t % 2), 1)

            @block.scalar
            def _(act):
                for k in range(0, chunks, 2):
                    if k:
                        act.wait_ge(sem("summed"), k - 1)
                    act.activation(sq[0][:, :], src[:, k, :], ACT.Square).then_inc(sem("squared0"), 1)
                act.wait_ge(sem("total"), NG)
                act.activation(stats[:, 1, :, :], stats[:, 0, :, :], ACT.Sqrt, scale=1.0 / (per_group * P),
                               bias=core.eps[:, 0:1]).then_inc(sem("root"), 1)
                W.split_high(act, 0, 0)
                for k in range(chunks):
                    act.wait_ge(sem("result"), k + 1)
                    act.activation(high[:, k, :], src[:, k, :], ACT.Copy).then_inc(sem("high"), 1)
                for t in range(1, len(tiles)):
                    W.split_high(act, t % 2, t // 2)

            @block.vector
            def _(dve):
                for k in range(1, chunks, 2):
                    if k > 1:
                        dve.wait_ge(sem("summed"), k - 1)
                    dve.tensor_tensor(sq[1][:, :], src[:, k, :], src[:, k, :], ALU.mult).then_inc(sem("squared1"), 1)
                dve.wait_ge(sem("summed"), chunks)
                for g in range(NG):
                    dve.tensor_reduce(stats[:, 0, g, :], sums[:, g * per_group:(g + 1) * per_group, :].rearrange("p k b -> p b k"),
                                      AX.X, ALU.add).then_inc(sem("total"), 1)
                dve.wait_ge(sem("root"), 1)
                dve.reciprocal(stats[:, 2, :, :], stats[:, 1, :, :]).then_inc(sem("rstd"), 1)
                dve.wait_ge(sem("rstd"), 1)
                dve.wait_ge(sem("gains"), 16)

                def spread_out(g):
                    if g:
                        dve.wait_ge(sem("spread"), g)
                    dve.tensor_tensor(diag[:, :, :], core.ident[:, :].unsqueeze(1).to_broadcast([P, NB, P]),
                                      stats[:, 2, g, :].unsqueeze(2).to_broadcast([P, NB, P]), ALU.mult).then_inc(sem("diag"), 1)

                def split_low(k):
                    dve.wait_ge(sem("high"), k + 1)
                    dve.tensor_tensor(low[:, k, :], src[:, k, :], high[:, k, :].bitcast(F32), ALU.subtract).then_inc(sem("low"), 1)

                spread_out(0)
                for k in range(chunks):
                    g = k // per_group
                    if k % per_group == 0:
                        if g + 1 < NG:
                            spread_out(g + 1)
                        dve.wait_ge(sem("spread"), g + 1)
                    dve.scalar_tensor_tensor(out=src[:, k, :], in0=src[:, k, :], scalar=gains[:, k:k + 1], in1=flat2(spread[g % 2]),
                                             op0=ALU.mult, op1=ALU.mult).then_inc(sem("scaled"), 1)
                    dve.wait_ge(sem("scaled"), k + 1)
                    if factor is not None:
                        dve.tensor_tensor(src[:, k, :], src[:, k, :], factor[:, k, :], ALU.mult).then_inc(sem("result"), 1)
                    else:
                        dve.sem_inc(sem("result"), 1)
                    if k:
                        split_low(k - 1)
                split_low(chunks - 1)
                for half in range(2):
                    cols = slice(half * HALF, (half + 1) * HALF)
                    for b in range(NB):
                        t = half * NK + NK - 1
                        if b < NB - 1:
                            dve.wait_ge(sem("out"), half * (NB - 1) + b + 1)
                        else:
                            dve.wait_ge(W.s("used", t % 2), t // 2 + 2)
                        if add:
                            dve.tensor_tensor(acc[:, b, cols], acc[:, b, cols], out[:, b, :], ALU.add).then_inc(sem("added"), 1)
                        else:
                            dve.tensor_copy(acc[:, b, cols], out[:, b, :]).then_inc(sem("added"), 1)


HG_H = 4
LEVELS = 7


def level_masks():
    s, l = np.arange(P)[:, None], np.arange(P)[None, :]
    out = [s == l]
    for v in range(LEVELS):
        m = 1 << v
        out.append((s // (2 * m) == l // (2 * m)) & (s % (2 * m) < m) & (l % (2 * m) >= m))
    return np.ascontiguousarray(np.stack(out, 1).astype(np.int32))


def stage_hgrn(core, O, SG):
    nc, io = core.nc, core.io
    w_in = io["w_in_2"][0]
    with stage(core) as (ctx, sem):
        W = WeightTiles(core, ctx, sem, KD)
        Qt, Kt, CU, VT, A, TF = (sbuf(core, ctx, n, [P, SEQ]) for n in ("q", "k", "cum", "vt", "attn", "tf"))
        Dc = [sbuf(core, ctx, f"d{s}", [P, SEQ]) for s in range(2)]
        X = [sbuf(core, ctx, f"x{s}", [P, SEQ]) for s in range(2)]
        V = sbuf(core, ctx, "v", [P, NB, P])
        keep = sbuf(core, ctx, "keep", [P, SEQ])
        masks = sbuf(core, ctx, "masks", [P, LEVELS + 1, P], I32)
        blank = sbuf(core, ctx, "blank", [1, LEVELS + 1])
        el = sbuf(core, ctx, "el", [P, NB])
        pp = [psum(core, ctx, f"pp{s}", [P, 2, HALF]) for s in range(4)]
        KN, ST = Dc[0], TF
        blocks = lambda t: t[:, :].rearrange("p (c t) -> p c t", t=P)
        pblocks = lambda t: flat2(t).rearrange("p (c t) -> p c t", t=P)
        NL = LEVELS + 1

        def halves(t, v):
            m = 1 << v
            r = t[:, :].rearrange("p (n two m) -> p n two m", two=2, m=m)
            return r[:, :, 0, :], r[:, :, 1, :]

        def middle(v):
            m = 1 << v
            r = CU[:, :].rearrange("p (n two m) -> p n two m", two=2, m=m)
            return r[:, :, 0, m - 1:m].to_broadcast([P, SEQ // (2 * m), m])

        with nc.Block() as block:

            @block.sync
            def _(sp):
                sp.dma_start(masks[:, :, :], io["level_masks"]).then_inc(sem("masks"), 16)
                with sp.Fori(0, HG_H) as h:
                    for j, at in enumerate((F_AT, Q_AT, I_AT, G_AT)):
                        W.load(sp, j % 2, h * 2 + j // 2, w_in[:, bass.ds(h * P + at, P)])

            @block.gpsimd
            def _(pool):
                W.open_pool(pool)
                pool.memset(keep[:, :], 1.0).then_inc(sem("keep0"), 1)
                pool.wait_ge(sem("keep0"), 1)
                pool.memset(blocks(keep)[:, :, 0:1], 0.0).then_inc(sem("keep"), 1)
                pool.memset(A[:, :], 0.0).then_inc(sem("keep"), 1)
                with pool.Fori(0, HG_H) as h:
                    for j in range(4):
                        W.split_low(pool, j % 2, h * 2 + j // 2)
                    for v in range(LEVELS):
                        s = v % 2
                        pool.wait_ge(sem("level_exp"), h * LEVELS + v + 1)
                        pool.wait_ge(sem("level_done"), h * NL + v + 2)
                        pool.tensor_tensor(halves(X[s], v)[0], halves(Kt, v)[0], halves(Dc[s], v)[0], ALU.mult).then_inc(sem("left"), 1)

            @block.tensor
            def _(pe):
                W.open_pe(pe)
                pe.sem_inc(sem("level_done"), 2)
                ident = core.ident
                with pe.Fori(0, HG_H) as h:
                    for j in range(4):
                        s, turn = j % 2, h * 2 + j // 2
                        W.wait(pe, s, turn)
                        pe.wait_ge(sem("banks_free"), h + 1)
                        W.multiply(pe, s, pp[j], core.AH, core.AL)
                    pe.wait_ge(sem("vt"), h + 1)
                    pe.wait_ge(sem("lf"), h + 1)
                    pe.wait_ge(sem("k"), h + 1)
                    for c in range(NB):
                        last = pe.transpose(pblocks(pp[0])[:, c, :], blocks(VT)[:, c, :], ident[:, :])
                    last.then_inc(sem("v_turned"), 1)
                    pe.wait_ge(sem("q"), h + 1)
                    for c in range(NB):
                        last = pe.matmul(pblocks(pp[1])[:, c, :], blocks(Kt)[:, c, :], blocks(Qt)[:, c, :], start=True, stop=True)
                    last.then_inc(sem("level_done"), 1)
                    for v in range(LEVELS):
                        pe.wait_ge(sem("left"), h * LEVELS + v + 1)
                        pe.wait_ge(sem("right"), h * LEVELS + v + 1)
                        if v >= 1:
                            pe.wait_ge(sem("placed"), h * NL + v)
                        x = blocks(X[v % 2])
                        out = pblocks(pp[1 + (v + 1) % 2])
                        for c in range(NB):
                            last = pe.matmul(out[:, c, :], x[:, c, :], x[:, c, :], start=True, stop=True)
                        last.then_inc(sem("level_done"), 1)
                    pe.wait_ge(sem("k_end"), h + 1)
                    pe.wait_ge(sem("sg"), h + 1)
                    for c in range(NB):
                        last = pe.transpose(pblocks(pp[3])[:, c, :], blocks(X[0])[:, c, :], ident[:, :])
                    last.then_inc(sem("k_turned"), 1)
                    pe.wait_ge(sem("kn"), h + 1)
                    pe.wait_ge(sem("v"), h + 1)
                    for c in range(NB):
                        last = pe.matmul(pblocks(pp[0])[:, c, :], blocks(KN)[:, c, :], V[:, c, :], start=True, stop=True)
                    last.then_inc(sem("added"), 1)
                    pe.wait_ge(sem("placed"), h * NL + NL)
                    pe.wait_ge(sem("q_start"), h + 1)
                    for c in range(NB):
                        if c:
                            pe.wait_ge(sem("state"), h * (NB - 1) + c)
                        out = pblocks(pp[1])[:, c, :]
                        last = pe.matmul(out, V[:, c, :], blocks(A)[:, c, :], start=True, stop=(c == 0))
                        if c:
                            last = pe.matmul(out, blocks(ST)[:, c, :], blocks(X[1])[:, c, :], start=False, stop=True)
                    last.then_inc(sem("o"), 1)

            @block.scalar
            def _(act):
                W.split_high(act, 0, 0)
                W.split_high(act, 1, 0)

                def head(h, more):
                    act.wait_ge(W.s("used", 0), h * 2 + 2)
                    W.split_high(act, 0, h * 2 + 1)
                    act.activation(TF[:, :], flat2(pp[0]), ACT.Abs).then_inc(sem("abs"), 1)
                    act.wait_ge(sem("abs"), h + 1)
                    act.activation(TF[:, :], TF[:, :], ACT.Exp, scale=-1.0).then_inc(sem("exp_f"), 1)
                    act.wait_ge(sem("exp_f"), h + 1)
                    act.activation(TF[:, :], TF[:, :], ACT.Ln, bias=1.0).then_inc(sem("ln_f"), 1)
                    act.activation(Kt[:, :], flat2(pp[0]), ACT.Sigmoid, scale=-1.0).then_inc(sem("k"), 1)
                    act.wait_ge(W.s("used", 1), h * 2 + 2)
                    W.split_high(act, 1, h * 2 + 1)
                    act.activation(Qt[:, :], flat2(pp[1]), ACT.Silu).then_inc(sem("q"), 1)
                    act.wait_ge(W.s("used", 0), h * 2 + 3)
                    if more:
                        W.split_high(act, 0, h * 2 + 2)
                    act.activation(VT[:, :], flat2(pp[2]), ACT.Copy).then_inc(sem("vt"), 1)
                    act.wait_ge(W.s("used", 1), h * 2 + 3)
                    if more:
                        W.split_high(act, 1, h * 2 + 2)
                    act.activation(SG[:, bass.ds(h, 1), :].squeeze(1), flat2(pp[3]), ACT.Silu).then_inc(sem("sg"), 1)
                    act.wait_ge(sem("v_turned"), h + 1)
                    act.activation(flat2(V), flat2(pp[0]), ACT.Copy).then_inc(sem("v"), 1)
                    for v in range(LEVELS):
                        s = v % 2
                        act.wait_ge(sem("level_diff"), h * LEVELS + v + 1)
                        act.activation(Dc[s][:, :], Dc[s][:, :], ACT.Exp).then_inc(sem("level_exp"), 1)
                    act.wait_ge(sem("end_diff"), h + 1)
                    act.activation(Dc[1][:, :], Dc[1][:, :], ACT.Exp).then_inc(sem("end_exp"), 1)
                    act.wait_ge(sem("left"), h * LEVELS + LEVELS)
                    act.wait_ge(sem("right"), h * LEVELS + LEVELS)
                    act.activation(Dc[0][:, :], CU[:, :], ACT.Exp).then_inc(sem("exp_cum"), 1)
                    act.activation(el[:, :], blocks(CU)[:, :, P - 1], ACT.Exp).then_inc(sem("el"), 1)
                    act.wait_ge(sem("k_turned"), h + 1)
                    act.wait_ge(sem("q_start"), h + 1)
                    act.activation(KN[:, :], flat2(pp[3]), ACT.Copy).then_inc(sem("kn"), 1)
                    act.wait_ge(sem("o"), h + 1)
                    act.activation(O[:, bass.ds(h, 1), :].squeeze(1), flat2(pp[1]), ACT.Copy).then_inc(sem("o_out"), 1)
                over_loop(act, HG_H, head)

            @block.vector
            def _(dve):
                dve.sem_inc(sem("banks_free"), 1)
                dve.wait_ge(sem("keep"), 2)
                dve.wait_ge(sem("masks"), 16)
                with dve.Fori(0, HG_H) as h:
                    dve.wait_ge(sem("ln_f"), h + 1)
                    dve.wait_ge(sem("k"), h + 1)
                    dve.scalar_tensor_tensor(out=TF[:, :], in0=flat2(pp[0]), scalar=0.0, in1=TF[:, :], op0=ALU.min, op1=ALU.subtract).then_inc(sem("lf"), 1)
                    dve.wait_ge(sem("lf"), h + 1)
                    dve.tensor_tensor_scan(CU[:, :], keep[:, :], TF[:, :], 0.0, ALU.mult, ALU.add).then_inc(sem("cum"), 1)
                    dve.wait_ge(sem("cum"), h + 1)

                    def differences(v):
                        s = v % 2
                        if v >= 2:
                            dve.wait_ge(sem("left"), h * LEVELS + v - 1)
                            dve.wait_ge(sem("right"), h * LEVELS + v - 1)
                        l, r = halves(Dc[s], v)
                        cl, cr = halves(CU, v)
                        dve.tensor_tensor(l, middle(v), cl, ALU.subtract)
                        dve.tensor_tensor(r, cr, middle(v), ALU.subtract).then_inc(sem("level_diff"), 1)

                    def place(level):
                        dve.wait_ge(sem("level_done"), h * NL + level + 3)
                        dve.memset(blank[:, level:level + 1], 0.0)
                        m = masks[:, level, :].unsqueeze(1).to_broadcast([P, NB, P])
                        dve.copy_predicated(blocks(A), m, pblocks(pp[1 + level % 2])).then_inc(sem("placed"), 1)

                    differences(0)
                    differences(1)
                    place(0)
                    for v in range(LEVELS):
                        s = v % 2
                        dve.wait_ge(sem("level_exp"), h * LEVELS + v + 1)
                        dve.wait_ge(sem("q"), h + 1)
                        dve.wait_ge(sem("level_done"), h * NL + v + 2)
                        dve.tensor_tensor(halves(X[s], v)[1], halves(Qt, v)[1], halves(Dc[s], v)[1], ALU.mult).then_inc(sem("right"), 1)
                        if v + 2 < LEVELS:
                            differences(v + 2)
                        dve.wait_ge(sem("placed"), h * NL + v + 1)
                        place(v + 1)
                    dve.wait_ge(sem("left"), h * LEVELS + LEVELS)
                    dve.tensor_tensor(blocks(Dc[1]), blocks(CU)[:, :, P - 1:P].to_broadcast([P, NB, P]), blocks(CU), ALU.subtract).then_inc(sem("end_diff"), 1)
                    dve.wait_ge(sem("end_exp"), h + 1)
                    dve.tensor_tensor(X[0][:, :], Kt[:, :], Dc[1][:, :], ALU.mult).then_inc(sem("k_end"), 1)
                    dve.wait_ge(sem("exp_cum"), h + 1)
                    dve.tensor_tensor(X[1][:, :], Qt[:, :], Dc[0][:, :], ALU.mult).then_inc(sem("q_start"), 1)
                    dve.wait_ge(sem("added"), h + 1)
                    dve.wait_ge(sem("el"), h + 1)
                    st, add = blocks(ST), pblocks(pp[0])
                    for c in range(NB - 1):
                        if c == 0:
                            dve.tensor_copy(st[:, 1, :], add[:, 0, :]).then_inc(sem("state"), 1)
                        else:
                            dve.wait_ge(sem("state"), h * (NB - 1) + c)
                            dve.scalar_tensor_tensor(out=st[:, c + 1, :], in0=st[:, c, :], scalar=el[:, c:c + 1], in1=add[:, c, :],
                                                     op0=ALU.mult, op1=ALU.add).then_inc(sem("state"), 1)
                    dve.wait_ge(sem("state"), h * (NB - 1) + NB - 1)
                    dve.wait_ge(sem("o_out"), h + 1)
                    dve.sem_inc(sem("banks_free"), 1)


S5_CH = 4
S5_G = 32
S5_PAIRS = S5_G // 2
S5_P, S5_N = 64, 16
ST = 8
TWO_PI = 2 * np.pi
ROUND = 1.5 * 2.0 ** 23
FINE = 1.5 * 2.0 ** 7


def two_pi_parts():
    first = 6.28125
    second = float(np.floor((TWO_PI - first) * 2.0 ** 21) / 2.0 ** 21)
    return first, second, TWO_PI - first - second


class Chain:

    def __init__(self, engine, sem):
        self.engine, self.sem, self.count = engine, sem, 0

    def __call__(self, instruction):
        instruction.then_inc(self.sem, 1)
        self.count += 1
        self.engine.wait_ge(self.sem, self.count)


class S5Tables:

    def __init__(self, core, ctx):
        take = lambda name, shape: sbuf(core, ctx, name, [P] + shape)
        self.rot = take("rot", [2, S5_PAIRS, P])
        self.keep = take("keep", [S5_PAIRS, P])
        self.AB = take("ab", [2, S5_PAIRS, ST, S5_N])
        self.BB = take("bb", [2, S5_PAIRS, S5_N])
        self.CA = take("ca", [2, S5_PAIRS, ST + 2, S5_N])
        self.UT = take("ut", [S5_G, P])


def stage_s5_tables(core, T):
    nc, io = core.nc, core.io
    w_in = io["w_in_2"][0]
    with stage(core) as (ctx, sem):
        W = WeightTiles(core, ctx, sem, KD)
        lam = sbuf(core, ctx, "lam", [P, 3, S5_PAIRS])
        B = sbuf(core, ctx, "b", [P, 2, S5_PAIRS, S5_N])
        cn = sbuf(core, ctx, "c_rows", [P, 2, 4, 2, S5_P])
        C = sbuf(core, ctx, "c", [P, 2, S5_PAIRS, S5_N])
        v = sbuf(core, ctx, "values", [P, 12, S5_PAIRS])
        count = sbuf(core, ctx, "count", [P, P])
        pw = sbuf(core, ctx, "powers", [P, 6, ST + 1, S5_PAIRS])
        half_pi = sbuf(core, ctx, "half_pi", [P, 1])
        tmp = T.AB[:, :, :, :, :].rearrange("p i q j h -> p i (q j h)")
        scratch_c = sbuf(core, ctx, "scratch", [P, S5_PAIRS, S5_N])
        ub = [sbuf(core, ctx, f"u_blocks{s}", [P, ST, P]) for s in range(2)]
        pU = [psum(core, ctx, f"pu{s}", [P, 2, HALF]) for s in range(2)]
        pC = psum(core, ctx, "pc", [P, 2, 4, P])
        NQ = S5_PAIRS

        def fill(t, a):
            return a.unsqueeze(2).to_broadcast([P, NQ, t])

        with nc.Block() as block:

            @block.sync
            def _(sp):
                two = lambda name: io[name][0].rearrange("(q r) p -> r p q", r=2)
                for r in range(2):
                    half = slice(r * S5_P, (r + 1) * S5_P)
                    sp.dma_start(lam[half, 0, :], two("s5_lambda_re_2")[r]).then_inc(sem("lam"), 16)
                    sp.dma_start(lam[half, 1, :], two("s5_lambda_im_2")[r]).then_inc(sem("lam"), 16)
                    sp.dma_start(lam[half, 2, :], io["s5_log_step_2"][0].rearrange("(q r) -> r q", r=2)[r].partition_broadcast(S5_P)).then_inc(sem("lam"), 16)
                W.load(sp, 0, 0, w_in[:, U_AT:U_AT + P])
                for i, name in enumerate(("s5_b_re_2", "s5_b_im_2")):
                    for r in range(2):
                        sp.dma_start(B[r * S5_P:(r + 1) * S5_P, i, :, :], io[name][0].rearrange("(q r) p h -> r p q h", r=2)[r]).then_inc(sem("b"), 16)
                W.load(sp, 1, 0, w_in[:, U_AT + P:U_AT + 2 * P])
                for i, name in enumerate(("s5_c_re_2", "s5_c_im_2")):
                    for r in range(2):
                        sp.dma_start(cn[:, i, :, r, :], io[name][0].rearrange("(n g) h p -> (g h) n p", g=8)).then_inc(sem("c"), 16)
                for n in range(2, S5_CH):
                    W.load(sp, n % 2, n // 2, w_in[:, U_AT + n * P:U_AT + (n + 1) * P])
                for n in range(S5_CH):
                    sp.wait_ge(sem("u_blocks"), n + 1)
                    sp.dma_start(core.s5_u[n * P:(n + 1) * P, :, :], ub[n % 2][:, :, :]).then_inc(sem(f"u_stored{n % 2}"), 16)
                for s in range(2):
                    sp.wait_ge(sem(f"u_stored{s}"), 16 * S5_CH // 2)
                for j in range(ST):
                    sp.dma_start(T.UT[j * S5_N:(j + 1) * S5_N, :, :], core.s5_u[:, j, :].rearrange("(g h) b -> h g b", h=S5_N)).then_inc(sem("ut"), 16)
                sp.wait_ge(sem("ut"), 16 * ST)

            @block.gpsimd
            def _(pool):
                W.open_pool(pool)
                pool.memset(half_pi[:, :], np.pi / 2).then_inc(sem("half_pi"), 1)
                for n in range(S5_CH):
                    W.split_low(pool, n % 2, n // 2)

            @block.tensor
            def _(pe):
                W.open_pe(pe)
                pe.wait_ge(sem("c"), 64)
                for i in range(2):
                    for n in range(4):
                        last = pe.transpose(pC[:, i, n, :], cn[:, i, n, :, :].rearrange("x r p -> x (r p)"), core.ident[:, :])
                last.then_inc(sem("c_turned"), 1)
                for n in range(S5_CH):
                    W.wait(pe, n % 2, n // 2)
                    if n >= 2:
                        pe.wait_ge(sem("u_blocks"), n - 1)
                    W.multiply(pe, n % 2, pU[n % 2], core.AH, core.AL)

            @block.scalar
            def _(act):
                W.split_high(act, 0, 0)
                W.split_high(act, 1, 0)
                act.wait_ge(sem("lam"), 96)
                act.activation(v[:, 0, :], lam[:, 2, :], ACT.Exp).then_inc(sem("step"), 1)
                act.wait_ge(sem("half_pi"), 1)
                act.wait_ge(sem("log_powers"), 1)
                act.activation(pw[:, 1, :, :], pw[:, 0, :, :], ACT.Exp).then_inc(sem("mags"), 1)
                act.activation(v[:, 9, :], pw[:, 0, ST, :], ACT.Exp).then_inc(sem("mags"), 1)
                act.wait_ge(sem("turns"), 1)
                act.activation(pw[:, 3, :, :], pw[:, 2, :, :], ACT.Sin, scale=6.283185).then_inc(sem("sin"), 1)
                act.activation(pw[:, 4, :, :], pw[:, 2, :, :], ACT.Abs).then_inc(sem("abs"), 1)
                act.wait_ge(sem("abs"), 1)
                act.activation(pw[:, 4, :, :], pw[:, 4, :, :], ACT.Sin, scale=-6.283185, bias=half_pi[:, 0:1]).then_inc(sem("cos"), 1)

                def blocks(n):
                    act.wait_ge(W.s("used", n % 2), n // 2 + 2)
                    if n >= 2:
                        act.wait_ge(sem(f"u_stored{n % 2}"), 16 * (n // 2))
                    act.activation(ub[n % 2][:, :, :], flat2(pU[n % 2]).rearrange("p (b j) -> p j b", j=ST), ACT.Copy).then_inc(sem("u_blocks"), 1)
                    if n < 2:
                        W.split_high(act, n, 1)
                blocks(0)
                blocks(1)
                act.wait_ge(sem("big_turns"), 1)
                flat = lambda t: t.rearrange("p q b -> p (q b)")
                act.activation(flat(T.rot[:, 1, :, :]), tmp[:, 0, :], ACT.Sin, scale=6.283185).then_inc(sem("big_sin"), 1)
                act.activation(tmp[:, 1, :], tmp[:, 0, :], ACT.Abs).then_inc(sem("abs"), 1)
                act.wait_ge(sem("abs"), 2)
                act.activation(flat(T.rot[:, 0, :, :]), tmp[:, 1, :], ACT.Sin, scale=-6.283185, bias=half_pi[:, 0:1]).then_inc(sem("big_cos"), 1)
                blocks(2)
                blocks(3)

            @block.vector
            def _(dve):
                done = Chain(dve, sem("dve"))
                c1, c2, c3 = two_pi_parts()
                done(dve.tensor_tensor_scan(count[:, :], core.ones[:, :], core.ones[:, :], -1.0, ALU.mult, ALU.add))
                dve.wait_ge(sem("lam"), 96)
                lr, li = v[:, 1, :], lam[:, 1, :]
                done(dve.tensor_scalar(lr, lam[:, 0, :], -1e-4, None, ALU.min))
                dve.wait_ge(sem("step"), 1)
                step, ls, ang, k, f = (v[:, i, :] for i in (0, 2, 3, 4, 5))
                done(dve.tensor_tensor(ls, lr, step, ALU.mult))
                taus = count[:, 0:ST + 1].unsqueeze(2).to_broadcast([P, ST + 1, NQ])
                over_taus = lambda a: a.unsqueeze(1).to_broadcast([P, ST + 1, NQ])
                done(dve.tensor_tensor(pw[:, 0, :, :], taus, over_taus(ls), ALU.mult))
                dve.sem_inc(sem("log_powers"), 1)
                done(dve.tensor_tensor(ang, li, step, ALU.mult))
                done(dve.tensor_scalar(k, ang, 1.0 / TWO_PI, ROUND, ALU.mult, ALU.add))
                done(dve.tensor_scalar(k, k, ROUND, None, ALU.subtract))
                for c in (c1, c2, c3):
                    done(dve.scalar_tensor_tensor(out=ang, in0=k, scalar=-c, in1=ang, op0=ALU.mult, op1=ALU.add))
                done(dve.tensor_scalar(f, ang, 1.0 / TWO_PI, None, ALU.mult))

                def split(f, high, low):
                    done(dve.tensor_scalar(high, f, FINE, None, ALU.add))
                    done(dve.tensor_scalar(high, high, FINE, None, ALU.subtract))
                    done(dve.tensor_tensor(low, f, high, ALU.subtract))

                def turns(out, scratch, mult, high, low):
                    done(dve.tensor_tensor(out, mult, high, ALU.mult))
                    done(dve.tensor_scalar(scratch, out, ROUND, None, ALU.add))
                    done(dve.tensor_scalar(scratch, scratch, ROUND, None, ALU.subtract))
                    done(dve.tensor_tensor(out, out, scratch, ALU.subtract))
                    done(dve.tensor_tensor(scratch, mult, low, ALU.mult))
                    done(dve.tensor_tensor(out, out, scratch, ALU.add))
                    done(dve.tensor_scalar(out, out, 0.5, -0.5, ALU.min, ALU.max))

                high, low = v[:, 6, :], v[:, 7, :]
                split(f, high, low)
                turns(pw[:, 2, :, :], pw[:, 5, :, :], taus, over_taus(high), over_taus(low))
                dve.sem_inc(sem("turns"), 1)
                done(dve.tensor_scalar(f, f, float(ST), None, ALU.mult))
                done(dve.tensor_scalar(k, f, ROUND, None, ALU.add))
                done(dve.tensor_scalar(k, k, ROUND, None, ALU.subtract))
                done(dve.tensor_tensor(f, f, k, ALU.subtract))
                split(f, high, low)
                big = [tmp[:, i, :].rearrange("p (q b) -> p q b", b=P) for i in range(2)]
                turns(big[0], big[1], count[:, :].unsqueeze(1).to_broadcast([P, NQ, P]), fill(P, high), fill(P, low))
                dve.sem_inc(sem("big_turns"), 1)

                dve.wait_ge(sem("mags"), 2)
                done(dve.tensor_copy(T.keep[:, :, :], fill(P, v[:, 9, :])))
                done(dve.memset(T.keep[:, :, 0:1], 0.0))
                dve.wait_ge(sem("sin"), 1)
                dve.wait_ge(sem("cos"), 1)
                are, aim = pw[:, 2, :, :], pw[:, 3, :, :]
                done(dve.tensor_tensor(are, pw[:, 1, :, :], pw[:, 4, :, :], ALU.mult))
                done(dve.tensor_tensor(aim, pw[:, 1, :, :], aim, ALU.mult))
                nr, ni, den, t1, t2 = (v[:, i, :] for i in (6, 7, 8, 10, 11))
                cr, ci = v[:, 2, :], v[:, 3, :]
                done(dve.tensor_scalar(nr, pw[:, 2, 1, :], 1.0, None, ALU.subtract))
                done(dve.tensor_copy(ni, pw[:, 3, 1, :]))
                done(dve.tensor_tensor(t1, lr, lr, ALU.mult))
                done(dve.tensor_tensor(t2, li, li, ALU.mult))
                done(dve.tensor_tensor(t1, t1, t2, ALU.add))
                done(dve.reciprocal(den, t1))
                done(dve.tensor_tensor(t1, nr, lr, ALU.mult))
                done(dve.tensor_tensor(t2, ni, li, ALU.mult))
                done(dve.tensor_tensor(t1, t1, t2, ALU.add))
                done(dve.tensor_tensor(cr, t1, den, ALU.mult))
                done(dve.tensor_tensor(t1, ni, lr, ALU.mult))
                done(dve.tensor_tensor(t2, nr, li, ALU.mult))
                done(dve.tensor_tensor(t1, t1, t2, ALU.subtract))
                done(dve.tensor_tensor(ci, t1, den, ALU.mult))

                def times(out, sign, a1, b1, a2, b2, scratch):
                    done(dve.tensor_tensor(scratch, a1, b1, ALU.mult))
                    done(dve.tensor_tensor(out, a2, b2, ALU.mult))
                    done(dve.tensor_tensor(out, scratch, out, ALU.add if sign > 0 else ALU.subtract))

                dve.wait_ge(sem("b"), 64)
                small = scratch_c[:, :, :]
                times(T.BB[:, 0, :, :], -1, B[:, 0, :, :], fill(S5_N, cr), B[:, 1, :, :], fill(S5_N, ci), small)
                times(T.BB[:, 1, :, :], +1, B[:, 1, :, :], fill(S5_N, cr), B[:, 0, :, :], fill(S5_N, ci), small)
                dve.wait_ge(sem("c_turned"), 1)
                for i in range(2):
                    for r in range(2):
                        half = slice(r * S5_P, (r + 1) * S5_P)
                        src = pC[half, i, :, :].rearrange("p n (q r h) -> p (n q) r h", r=2, h=S5_N)[:, :, r, :]
                        done(dve.tensor_copy(C[half, i, :, :], src))
                for i in range(2):
                    done(dve.memset(T.CA[:, i, :, 0, :], 0.0))
                dve.wait_ge(sem("big_sin"), 1)
                dve.wait_ge(sem("big_cos"), 1)
                for tau in range(ST + 1):
                    ar, ai = fill(S5_N, pw[:, 2, tau, :]), fill(S5_N, pw[:, 3, tau, :])
                    sc = scratch_c[:, :, :]
                    times(T.CA[:, 0, :, tau + 1, :], -1, C[:, 0, :, :], ar, C[:, 1, :, :], ai, sc)
                    done(dve.tensor_tensor(sc, C[:, 0, :, :], ai, ALU.mult))
                    done(dve.tensor_tensor(T.CA[:, 1, :, tau + 1, :], C[:, 1, :, :], ar, ALU.mult))
                    done(dve.scalar_tensor_tensor(out=T.CA[:, 1, :, tau + 1, :], in0=sc, scalar=-1.0, in1=T.CA[:, 1, :, tau + 1, :],
                                                  op0=ALU.mult, op1=ALU.subtract))
                    if tau < ST:
                        j = ST - 1 - tau
                        times(T.AB[:, 0, :, j, :], -1, T.BB[:, 0, :, :], ar, T.BB[:, 1, :, :], ai, sc)
                        times(T.AB[:, 1, :, j, :], +1, T.BB[:, 1, :, :], ar, T.BB[:, 0, :, :], ai, sc)


def stage_s5_states(core, T):
    nc = core.nc
    NQ = S5_PAIRS
    with stage(core) as (ctx, sem):
        Z = sbuf(core, ctx, "z", [P, 2, NQ, P])
        R = T.AB[:, :, :, :, :].rearrange("p i q j h -> p i q (j h)")
        Y = Z[:, :, :, :].rearrange("p i q b -> p (i q) b")
        two = range(2)
        ab = [sbuf(core, ctx, f"ab{s}", [P, 2, P]) for s in two]
        abt = [sbuf(core, ctx, f"abt{s}", [P, 2, 2, P]) for s in two]
        t1 = [sbuf(core, ctx, f"tc{s}", [P, 2, P]) for s in two]
        t2 = [sbuf(core, ctx, f"ts{s}", [P, 2, P]) for s in two]
        be = [sbuf(core, ctx, f"b_even_odd{s}", [P, 2, 2, 2, ST, S5_N]) for s in two]
        cs = [sbuf(core, ctx, f"c_next{s}", [P, 2, 2, P]) for s in two]
        M = [sbuf(core, ctx, f"m{s}", [P, 2, P]) for s in two]
        SX = [sbuf(core, ctx, f"sx{s}", [P, 2, P]) for s in two]
        pT = [psum(core, ctx, f"pt{s}", [P, 4, P]) for s in two]
        pS = [psum(core, ctx, f"ps{s}", [P, 4, P]) for s in two]
        pM = [psum(core, ctx, f"pm{s}", [P, 4, P]) for s in two]
        pY = [psum(core, ctx, f"py{s}", [P, 4, P]) for s in two]

        def pairs(engine, body):
            with engine.Fori(0, NQ // 2) as i:
                for s in two:
                    body(i * 2 + s, s)

        def one(t, q):
            return t[:, :, bass.ds(q, 1), :].rearrange("p i q b -> p (i q) b")

        with nc.Block() as block:

            @block.gpsimd
            def _(pool):
                for s in two:
                    pool.memset(abt[s][:, :, :, :], 0.0).then_inc(sem("zero"), 1)
                    pool.memset(be[s][:, :, :, :, :, :], 0.0).then_inc(sem("zero"), 1)
                    pool.memset(cs[s][:, :, :, :], 0.0).then_inc(sem("zero"), 1)
                    pool.memset(M[s][:, :, :], 0.0).then_inc(sem("zero"), 1)
                    pool.memset(SX[s][:, :, 0:1], 0.0).then_inc(sem("zero"), 1)
                pool.wait_ge(sem("zero"), 10)

                def to_ab(q, s):
                    pool.wait_ge(sem("ab_turned"), q + 1)
                    pool.sem_inc(sem("pool_asked"), 1)
                    pool.tensor_copy(ab[s][:, :, :], T.AB[:, :, bass.ds(q, 1), :, :].rearrange("p i q j h -> p (i q) (j h)")).then_inc(sem("ab"), 1)
                pairs(pool, to_ab)
                pool.wait_ge(sem("ab"), NQ)

                def to_bc(q, s):
                    pool.wait_ge(sem("y"), q + 1)
                    pool.sem_inc(sem("pool_asked"), 1)
                    for r in two:
                        rows = slice(r * S5_P, (r + 1) * S5_P)
                        for i in two:
                            b = T.BB[rows, i, bass.ds(q, 1), :].to_broadcast([S5_P, ST // 2, S5_N])
                            for odd in two:
                                pool.tensor_copy(be[s][rows, r, i, odd, odd::2, :], b).then_inc(sem("be"), 1)
                        pool.tensor_copy(cs[s][rows, r, :, :], T.CA[rows, :, bass.ds(q, 1), 2:, :].rearrange("p i q j h -> p (i q) (j h)")).then_inc(sem("be"), 1)
                        pool.wait_ge(sem("be"), q * 10 + 5 * r + 5)
                pairs(pool, to_bc)

            @block.tensor
            def _(pe):
                pe.sem_inc(sem("ab_turned"), 2)
                pe.sem_inc(sem("y"), 2)

                def inputs(q, s):
                    pe.wait_ge(sem("ab"), q + 1)
                    for i in two:
                        last = pe.transpose(pT[s][:, i, :], ab[s][:, i, :], core.ident[:, :])
                    last.then_inc(sem("ab_turned"), 1)
                    pe.wait_ge(sem("abt"), 2 * q + 2)
                    pe.wait_ge(sem("z"), q + 1)
                    for i in two:
                        for r in two:
                            last = pe.matmul(pS[s][:, i, :], abt[s][:, i, r, :], T.UT[:, bass.ds(q * 2 + r, 1), :].squeeze(1),
                                             start=(r == 0), stop=(r == 1))
                    last.then_inc(sem("inputs"), 1)
                pairs(pe, inputs)

                def outputs(q, s):
                    pe.wait_ge(sem("be"), 10 * q + 10)
                    pe.wait_ge(sem("m"), q * 4 + 4)
                    for r in two:
                        n = 0
                        for i in two:
                            for odd in two:
                                last = pe.matmul(pM[s][:, r, :], be[s][:, r, i, odd, :, :].rearrange("p j h -> p (j h)"),
                                                 T.CA[:, i, bass.ds(q, 1), 1 - odd:ST + 1 - odd, :].rearrange("p q j h -> p (q j h)"),
                                                 start=(n == 0), stop=(n == 3))
                                n += 1
                    last.then_inc(sem("pm"), 1)
                    pe.wait_ge(sem("m"), q * 4 + 12)
                    pe.wait_ge(sem("sx"), q * 2 + 2)
                    pe.wait_ge(sem("y_kept"), q + 1)
                    for r in two:
                        pe.matmul(pY[s][:, r, :], M[s][:, r, :], T.UT[:, bass.ds(q * 2 + r, 1), :].squeeze(1), start=True, stop=False)
                        for i in two:
                            last = pe.matmul(pY[s][:, r, :], cs[s][:, r, i, :], SX[s][:, i, :], start=False, stop=(i == 1))
                    last.then_inc(sem("y"), 1)
                pairs(pe, outputs)

            @block.scalar
            def _(act):
                def turned(q, s):
                    act.wait_ge(sem("ab_turned"), q + 3)
                    act.wait_ge(sem("inputs_credit"), q + 1)
                    for r in two:
                        cols = slice(r * S5_P, (r + 1) * S5_P)
                        act.activation(abt[s][:, :, r, cols], pT[s][:, 0:2, cols], ACT.Copy).then_inc(sem("abt"), 1)
                act.wait_ge(sem("zero"), 10)
                pairs(act, turned)
                act.sem_inc(sem("m"), 8)

                def bands(q, s):
                    act.wait_ge(sem("pm"), q + 1)
                    act.wait_ge(sem("y"), q + 1)
                    for band in range(4):
                        at = band * 2 * S5_N
                        act.activation(M[s][at:at + 32, :, at:P], pM[s][at:at + 32, 0:2, 0:P - at], ACT.Copy).then_inc(sem("m"), 1)
                    act.wait_ge(sem("y"), q + 3)
                    act.wait_ge(sem("asked_y"), q + 1)
                    act.activation(Y[:, bass.ds(q * 2, 2), :], pY[s][:, 0:2, :], ACT.Copy).then_inc(sem("y_kept"), 1)
                    act.sem_inc(sem("asked_y"), 1)
                act.sem_inc(sem("asked_y"), 1)
                act.sem_inc(sem("y_kept"), 2)
                pairs(act, bands)

            @block.vector
            def _(dve):
                dve.sem_inc(sem("z"), 2)
                dve.sem_inc(sem("inputs_credit"), 2)

                def rotate(q, s):
                    cos, sin = (T.rot[:, i, bass.ds(q, 1), :].to_broadcast([P, 2, P]) for i in two)
                    dve.wait_ge(sem("inputs"), q + 1)
                    dve.sem_inc(sem("inputs_credit"), 1)
                    dve.tensor_tensor(t1[s][:, :, :], pS[s][:, 0:2, :], cos, ALU.mult).then_inc(sem("t1"), 1)
                    dve.tensor_tensor(t2[s][:, :, :], pS[s][:, 0:2, :], sin, ALU.mult).then_inc(sem("z"), 1)
                    dve.wait_ge(sem("t1"), q + 1)
                    dve.wait_ge(sem("z"), q + 3)
                    dve.tensor_tensor(Z[:, 0, bass.ds(q, 1), :].squeeze(1), t1[s][:, 0, :], t2[s][:, 1, :], ALU.add).then_inc(sem("zz"), 1)
                    dve.tensor_tensor(Z[:, 1, bass.ds(q, 1), :].squeeze(1), t1[s][:, 1, :], t2[s][:, 0, :], ALU.subtract).then_inc(sem("zz"), 1)
                    dve.wait_ge(sem("zz"), q * 2 + 2)
                pairs(dve, rotate)
                for i in two:
                    dve.tensor_tensor_scan(R[:, i, :, :].rearrange("p q b -> p (q b)"), T.keep[:, :, :].rearrange("p q b -> p (q b)"),
                                           Z[:, i, :, :].rearrange("p q b -> p (q b)"), 0.0, ALU.mult, ALU.add).then_inc(sem("scan"), 1)
                dve.wait_ge(sem("scan"), 2)
                dve.wait_ge(sem("zero"), 10)

                def back(q, s):
                    cos, sin = (T.rot[:, i, bass.ds(q, 1), :].to_broadcast([P, 2, P]) for i in two)
                    dve.tensor_tensor(t1[s][:, :, :], one(R, q), cos, ALU.mult).then_inc(sem("u1"), 1)
                    dve.tensor_tensor(t2[s][:, :, :], one(R, q), sin, ALU.mult).then_inc(sem("u2"), 1)
                    dve.wait_ge(sem("u1"), q + 1)
                    dve.wait_ge(sem("u2"), q + 1)
                    dve.wait_ge(sem("y"), q + 1)
                    dve.tensor_tensor(SX[s][:, 0, 1:], t1[s][:, 0, :P - 1], t2[s][:, 1, :P - 1], ALU.subtract).then_inc(sem("sx"), 1)
                    dve.tensor_tensor(SX[s][:, 1, 1:], t1[s][:, 1, :P - 1], t2[s][:, 0, :P - 1], ALU.add).then_inc(sem("sx"), 1)
                    dve.wait_ge(sem("sx"), q * 2 + 2)
                pairs(dve, back)

            @block.sync
            def _(sp):
                sp.wait_ge(sem("y_kept"), NQ + 2)
                for j in range(ST):
                    sp.dma_start(core.s5_y[:, j, :].rearrange("(g h) b -> h g b", h=S5_N), Y[j * S5_N:(j + 1) * S5_N, :, :]).then_inc(sem("stored"), 16)
                sp.wait_ge(sem("stored"), 16 * ST)


def stage_s5_glu(core, O):
    nc, io = core.nc, core.io
    w_in, glu = io["w_in_2"][0], io["s5_glu_w_2"][0]
    with stage(core) as (ctx, sem):
        W = WeightTiles(core, ctx, sem, KD, slots=3)
        yb = sbuf(core, ctx, "y_blocks", [P, S5_CH, SEQ])
        ub = sbuf(core, ctx, "u_blocks", [P, S5_CH, SEQ])
        H = sbuf(core, ctx, "y_high", [P, S5_CH, SEQ], F32R)
        L = sbuf(core, ctx, "y_low", [P, S5_CH, SEQ], F32R)
        skip = sbuf(core, ctx, "skip", [P, S5_CH])
        bias = sbuf(core, ctx, "bias", [P, 2 * S5_CH])
        sig = sbuf(core, ctx, "sig", [P, SEQ])
        gate = sbuf(core, ctx, "gate", [P, SEQ])
        pV, pS, pG = (psum(core, ctx, n, [P, 2, HALF]) for n in ("pv", "ps", "pg"))
        with nc.Block() as block:

            @block.sync
            def _(sp):
                def load(n):
                    W.load(sp, 2, n, w_in[:, S5G_AT + n * P:S5G_AT + (n + 1) * P])
                    W.load(sp, 0, n, glu[:, n * P:(n + 1) * P], S5_CH)
                    W.load(sp, 1, n, glu[:, (S5_CH + n) * P:(S5_CH + n + 1) * P], S5_CH)
                load(0)
                sp.dma_start(skip[:, :], per_channel(io["s5_d_2"][0])).then_inc(sem("small"), 16)
                sp.dma_start(bias[:, :], per_channel(io["s5_glu_b_2"][0])).then_inc(sem("small"), 16)
                for n in range(S5_CH):
                    sp.dma_start(yb[:, n, :], core.s5_y[n * P:(n + 1) * P, :, :].rearrange("p j b -> p (j b)")).then_inc(sem(f"y{n}"), 16)
                    sp.dma_start(ub[:, n, :], core.s5_u[n * P:(n + 1) * P, :, :].rearrange("p j b -> p (j b)")).then_inc(sem(f"y{n}"), 16)
                for n in range(1, S5_CH):
                    load(n)

            @block.gpsimd
            def _(pool):
                W.open_pool(pool)
                for n in range(S5_CH):
                    W.split_low(pool, 2, n)
                    W.split_low(pool, 0, n, S5_CH)
                    W.split_low(pool, 1, n, S5_CH)

            @block.tensor
            def _(pe):
                W.open_pe(pe)
                for n in range(S5_CH):
                    W.wait(pe, 2, n)
                    if n:
                        pe.wait_ge(sem("silu"), n)
                    W.multiply(pe, 2, pG, core.AH, core.AL)
                    if n == 0:
                        pe.wait_ge(sem("low"), S5_CH)
                    W.wait(pe, 0, n)
                    if n:
                        pe.wait_ge(sem("val"), n)
                    W.multiply(pe, 0, pV, H, L, S5_CH)
                    W.wait(pe, 1, n)
                    if n:
                        pe.wait_ge(sem("sig"), n)
                    W.multiply(pe, 1, pS, H, L, S5_CH)

            @block.scalar
            def _(act):
                W.split_high(act, 2, 0)
                W.split_high(act, 0, 0, S5_CH)
                W.split_high(act, 1, 0, S5_CH)
                for n in range(S5_CH):
                    act.wait_ge(sem("sum"), n + 1)
                    act.activation(ub[:, n, :], ub[:, n, :], ACT.Gelu_apprx_tanh).then_inc(sem("gelu"), 1)
                for n in range(S5_CH):
                    act.wait_ge(sem("gelu"), n + 1)
                    act.activation(H[:, n, :], ub[:, n, :], ACT.Copy).then_inc(sem("high"), 1)
                act.wait_ge(sem("small"), 32)
                for n in range(S5_CH):
                    act.wait_ge(W.s("used", 2), n + 2)
                    if n:
                        act.wait_ge(sem("out"), n)
                    act.activation(gate[:, :], flat2(pG), ACT.Silu).then_inc(sem("silu"), 1)
                    if n < S5_CH - 1:
                        W.split_high(act, 2, n + 1)
                        W.split_high(act, 0, n + 1, S5_CH)
                    act.wait_ge(W.s("used", 1), n + 2)
                    act.activation(sig[:, :], flat2(pS), ACT.Sigmoid, bias=bias[:, S5_CH + n:S5_CH + n + 1]).then_inc(sem("sig"), 1)
                    if n < S5_CH - 1:
                        W.split_high(act, 1, n + 1, S5_CH)

            @block.vector
            def _(dve):
                dve.wait_ge(sem("small"), 32)
                for n in range(S5_CH):
                    dve.wait_ge(sem(f"y{n}"), 32)
                    dve.scalar_tensor_tensor(out=yb[:, n, :], in0=ub[:, n, :], scalar=skip[:, n:n + 1], in1=yb[:, n, :],
                                             op0=ALU.mult, op1=ALU.add).then_inc(sem("plus"), 1)
                    dve.wait_ge(sem("plus"), n + 1)
                    dve.tensor_copy(ub[:, n, :].rearrange("p (b j) -> p j b", j=ST), yb[:, n, :].rearrange("p (j b) -> p j b", j=ST)).then_inc(sem("sum"), 1)
                for n in range(S5_CH):
                    dve.wait_ge(sem("high"), n + 1)
                    dve.tensor_tensor(L[:, n, :], ub[:, n, :], H[:, n, :].bitcast(F32), ALU.subtract).then_inc(sem("low"), 1)
                for n in range(S5_CH):
                    dve.wait_ge(sem("sig"), n + 1)
                    dve.scalar_tensor_tensor(out=O[:, n, :], in0=flat2(pV), scalar=bias[:, n:n + 1], in1=sig[:, :],
                                             op0=ALU.add, op1=ALU.mult).then_inc(sem("val"), 1)
                    dve.wait_ge(sem("val"), n + 1)
                    dve.tensor_tensor(O[:, n, :], O[:, n, :], gate[:, :], ALU.mult).then_inc(sem("out"), 1)


def second_block(core):
    io, nc = core.io, core.nc
    w_out = io["w_out_2"][0]
    SIZE = 4 * 4 * SEQ
    at = lambda name, n, dtype=F32: nc.alloc_sbuf_tensor_at(name, [P, 4, SEQ], dtype, offset=nc.sbuf_top - n * SIZE)
    O, OL, SG, OH = at("part_out", 1), at("part_low", 1, F32R), at("hgrn_gate", 2), at("part_high", 3, F32R)
    core.limit = nc.sbuf_top - SIZE
    with ExitStack() as ctx:
        T = S5Tables(core, ctx)
        stage_s5_tables(core, T)
        stage_s5_states(core, T)
    stage_s5_glu(core, O)
    X = sbuf(core, core.ctx, "mixed", [P, NB, D])
    core.limit = nc.sbuf_top - 3 * SIZE
    stage_mix_rows(core, O, S5_CH, S5_CH, io["s5_norm_w_2"][0], OH, OL, w_out[3 * HALF:4 * HALF, :], X, add=False)
    core.limit = nc.sbuf_top - 2 * SIZE
    stage_hgrn(core, O, SG)
    core.limit = nc.sbuf_top - 3 * SIZE
    stage_mix_rows(core, O, 4, 1, io["hgrn_norm_w_2"][0], OH, OL, w_out[2 * HALF:3 * HALF, :], X, factor=SG)
    core.limit = nc.sbuf_top
    with ExitStack() as ctx:
        ZT = sbuf(core, ctx, "z", [P, KD, SEQ])
        with ExitStack() as inner:
            dtN = sbuf(core, inner, "dt", [P, NB, SSD_H])
            acN = sbuf(core, inner, "acum", [P, NB, SSD_H])
            stage_ssd_steps(core, dtN, acN)
            XBC = sbuf(core, inner, "xbc", [P, SSD_CH, SEQ])
            stage_ssd_project(core, XBC, ZT)
            stage_ssd_chunks(core, XBC, ZT, dtN, acN)
        stage_mix_rows(core, ZT, KD, 4, io["ssd_norm_w_2"][0], core.AH, core.AL, w_out[0:D, :], X)
    stage_norm_time(core, X, io["post_norm_w_2"][0], residual=core.x_mid, out=io["out"])


def program(nc, io):
    with ExitStack() as ctx:
        ctx.enter_context(nc.allow_non_contiguous_dma(reason="small vectors and the S5 part's blocks"))
        core = make_core(nc, io, ctx)
        core.ctx = ctx
        scratch = lambda name, shape: nc.dram_tensor(name, shape, F32).ap()
        core.lines = scratch("lines", [4, P, LINE])
        core.neg_c = scratch("neg_c", [8, SEQ])
        core.m_part = scratch("m_part", [KD, P, SEQ])
        core.x_mid = scratch("x_mid", [SEQ, D])
        core.acum = scratch("acum_rows", [SSD_H, SEQ])
        core.s5_u = scratch("s5_u", [S5_CH * P, ST, P])
        core.s5_y = scratch("s5_y", [S5_CH * P, ST, P])
        setup(core)
        first_block(core)
        second_block(core)


def kernel(**inputs):
    import concourse.bacc as bacc
    from concourse.bass_utils import run_bass_kernel_spmd

    nc = bacc.Bacc("TRN2", target_bir_lowering=False, num_devices=1)
    data = dict(inputs, bucket_edges=bucket_edges(), level_masks=level_masks())
    arrays, io = {}, {}
    for name, value in data.items():
        value = np.ascontiguousarray(value)
        arrays[f"in_{name}"] = value
        io[name] = nc.dram_tensor(f"in_{name}", value.shape, mybir.dt.from_np(value.dtype), kind="ExternalInput").ap()
    io["out"] = nc.dram_tensor("out", (SEQ, D), F32, kind="ExternalOutput").ap()
    program(nc, io)
    result = run_bass_kernel_spmd(nc, [arrays], core_ids=[0])
    return result.results[0]["out"].reshape(1, SEQ, D)
```

```python
from contextlib import ExitStack, contextmanager

import numpy as np
import concourse.bass as bass
from concourse import mybir

F32 = mybir.dt.float32
F32R = mybir.dt.float32r
I32 = mybir.dt.int32
ALU = mybir.AluOpType
ACT = mybir.ActivationFunctionType
AX = mybir.AxisListType

P = 128
SEQ = 1024
D = 1024
NB = SEQ // P
KD = D // P
HALF = 512
EPS = 1e-6
NEG = -3.0e38


class Core:

    def __init__(self, nc, io):
        self.nc, self.io = nc, io


class Sems:

    def __init__(self, pool):
        self.pool, self.names = pool, {}

    def __call__(self, name):
        if name not in self.names:
            self.names[name] = self.pool[len(self.names)]
        return self.names[name]


@contextmanager
def stage(core):
    nc = core.nc
    sem = Sems(core.pool)
    with ExitStack() as ctx:
        yield ctx, sem
    used = sorted(s.num for s in sem.names.values())
    if used:
        nc.gpsimd.sem_clear(range(used[0], used[-1] + 1))
    nc.all_engine_barrier()


def sbuf(core, ctx, name, shape, dtype=F32):
    core.serial += 1
    tensor = ctx.enter_context(core.nc.sbuf_tensor(f"{name}_{core.serial}", shape, dtype))
    assert core.nc.sbuf_base <= core.limit, name
    return tensor


def psum(core, ctx, name, shape, dtype=F32):
    core.serial += 1
    return ctx.enter_context(core.nc.psum_tensor(f"{name}_{core.serial}", shape, dtype))


class WeightTiles:

    def __init__(self, core, ctx, sem, nk, width=P, name="w", slots=2, ready=True):
        self.sem, self.nk, self.width, self.name, self.slots, self.ready = sem, nk, width, name, slots, ready
        if name == "w":
            self.raw, self.high, self.low = ([tile_view(core.w_slots[part][s], nk, width) for s in range(slots)]
                                             for part in ("raw", "high", "low"))
        else:
            self.raw = [sbuf(core, ctx, f"{name}_raw{s}", [P, nk, width]) for s in range(slots)]
            self.high = [sbuf(core, ctx, f"{name}_high{s}", [P, nk, width], F32R) for s in range(slots)]
            self.low = [sbuf(core, ctx, f"{name}_low{s}", [P, nk, width], F32R) for s in range(slots)]

    def s(self, what, slot=""):
        return self.sem(f"{self.name}_{what}{slot}")

    def given(self, turn):
        return self.ready and isinstance(turn, int) and turn == 0

    def open_pool(self, pool):
        for slot in range(self.slots):
            pool.sem_inc(self.s("raw_free", slot), 1 + self.ready)
            if self.ready:
                pool.sem_inc(self.s("low", slot), 1)

    def open_pe(self, pe):
        for slot in range(self.slots):
            pe.sem_inc(self.s("used", slot), 1)

    def load(self, sp, slot, turn, src, nk=None):
        nk = nk or self.nk
        if self.given(turn):
            return
        sp.wait_ge(self.s("raw_free", slot), turn + 1)
        sp.sem_inc(self.s("asked", slot), 1)
        sp.dma_start(self.raw[slot][:, 0:nk, :], src.rearrange("(k p) n -> p k n", p=P)).then_inc(self.s("loaded", slot), 16)

    def split_high(self, act, slot, turn, nk=None):
        nk = nk or self.nk
        if self.given(turn):
            return
        act.wait_ge(self.s("loaded", slot), (turn + (1 - self.ready)) * 16)
        act.wait_ge(self.s("used", slot), turn + 1)
        act.activation(self.high[slot][:, 0:nk, :], self.raw[slot][:, 0:nk, :], ACT.Copy).then_inc(self.s("high", slot), 1)

    def split_low(self, pool, slot, turn, nk=None):
        nk = nk or self.nk
        if self.given(turn):
            return
        pool.wait_ge(self.s("high", slot), turn + (1 - self.ready))
        pool.tensor_tensor(self.low[slot][:, 0:nk, :], self.raw[slot][:, 0:nk, :], self.high[slot][:, 0:nk, :].bitcast(F32),
                           ALU.subtract).then_inc(self.s("low", slot), 1)
        pool.wait_ge(self.s("low", slot), turn + 1)
        pool.sem_inc(self.s("raw_free", slot), 1)

    def wait(self, pe, slot, turn):
        pe.wait_ge(self.s("low", slot), turn + 1)

    def multiply(self, pe, slot, out, high, low, nk=None, halves=False):
        nk = nk or self.nk
        for h in range(SEQ // HALF):
            cols = slice(h * HALF, (h + 1) * HALF)
            n = 0
            for k in range(nk):
                for w, x in ((self.high, high), (self.high, low), (self.low, high)):
                    last = pe.matmul(out[:, h, :] if not halves else out[h], w[slot][:, k, :], x[:, k, cols], start=(n == 0), stop=(n == 3 * nk - 1))
                    n += 1
        last.then_inc(self.s("used", slot), 1)


def tile_view(slot, nk, width):
    return slot[:, 0:nk * width].rearrange("p (k n) -> p k n", n=width)


class Ahead:

    def __init__(self, core, sem, tiles, W=None, turns=(0, 0)):
        self.sem, self.tiles, self.W, self.turns = sem, tiles, W, turns
        self.slots = core.w_slots

    def views(self, slot, src):
        nk, width = src.shape[0] // P, src.shape[1]
        return [tile_view(self.slots[part][slot], nk, width) for part in ("raw", "high", "low")]

    def load(self, sp):
        for slot, src in self.tiles:
            if self.turns[slot]:
                sp.wait_ge(self.W.s("raw_free", slot), self.turns[slot] + 1)
            raw = self.views(slot, src)[0]
            sp.dma_start(raw, src.rearrange("(k p) n -> p k n", p=P)).then_inc(self.sem(f"ahead_loaded{slot}"), 16)

    def split_high(self, act, *slots):
        for slot, src in self.tiles:
            if slots and slot not in slots:
                continue
            raw, high, _ = self.views(slot, src)
            act.wait_ge(self.sem(f"ahead_loaded{slot}"), 16)
            if self.turns[slot]:
                act.wait_ge(self.W.s("used", slot), self.turns[slot] + 1)
            act.activation(high, raw, ACT.Copy).then_inc(self.sem(f"ahead_high{slot}"), 1)

    def split_low(self, pool, *slots):
        for slot, src in self.tiles:
            if slots and slot not in slots:
                continue
            raw, high, low = self.views(slot, src)
            pool.wait_ge(self.sem(f"ahead_high{slot}"), 1)
            pool.tensor_tensor(low, raw, high.bitcast(F32), ALU.subtract)


def columns(w, *starts):
    return [(slot, w[:, at:at + P]) for slot, at in enumerate(starts)]


def stage_norm_to_channels(core, src_tile, gain_vec, src_dram=None, ahead=()):
    nc = core.nc
    AH, AL, ident = core.AH, core.AL, core.ident
    with stage(core) as (ctx, sem):
        A = Ahead(core, sem, ahead)
        gain = sbuf(core, ctx, "gain", [P, D])
        squares = sbuf(core, ctx, "squares", [P, 2, D])
        scaled = sbuf(core, ctx, "scaled", [P, 2, D])
        total = sbuf(core, ctx, "total", [P, NB])
        root = sbuf(core, ctx, "root", [P, NB])
        rstd = sbuf(core, ctx, "rstd", [P, NB])
        turned = psum(core, ctx, "turned", [P, 2, KD, P])
        with nc.Block() as block:

            @block.sync
            def _(sp):
                if src_dram is not None:
                    for b in range(NB):
                        sp.dma_start(src_tile[:, b, :], src_dram[b * P:(b + 1) * P, :]).then_inc(sem(f"x_loaded{b}"), 16)
                        if b == 0:
                            sp.dma_start(gain[:, :], gain_vec.partition_broadcast(P)).then_inc(sem("gain_loaded"), 16)
                else:
                    sp.dma_start(gain[:, :], gain_vec.partition_broadcast(P)).then_inc(sem("gain_loaded"), 16)
                A.load(sp)

            @block.gpsimd
            def _(pool):
                A.split_low(pool)

            @block.scalar
            def _(act):
                def square(b):
                    if src_dram is not None:
                        act.wait_ge(sem(f"x_loaded{b}"), 16)
                    act.activation(squares[:, b % 2, :], src_tile[:, b, :], ACT.Square, accum_out=total[:, b:b + 1]).then_inc(sem("squared"), 1)
                    act.wait_ge(sem("squared"), b + 1)
                    act.activation(root[:, b:b + 1], total[:, b:b + 1], ACT.Sqrt, scale=1.0 / D, bias=core.eps[:, 0:1]).then_inc(sem("root"), 1)

                square(0)
                square(1)
                for b in range(NB):
                    if b + 2 < NB:
                        square(b + 2)
                    act.wait_ge(sem("turned"), b + 1)
                    act.activation(AH[:, :, b * P:(b + 1) * P], turned[:, b % 2, :, :], ACT.Copy).then_inc(sem("high"), 1)
                    if b == 3:
                        A.split_high(act)

            @block.tensor
            def _(pe):
                with pe.Fori(0, NB // 2) as pair:
                    for s in range(2):
                        b = pair * 2 + s
                        pe.wait_ge(sem("scaled"), b + 1)
                        pe.wait_ge(sem("turned_free"), b + 1)
                        for k in range(KD):
                            last = pe.transpose(turned[:, s, k, :], scaled[:, s, k * P:(k + 1) * P], ident[:, :])
                        last.then_inc(sem("turned"), 1)

            @block.vector
            def _(dve):
                dve.sem_inc(sem("turned_free"), 2)
                dve.wait_ge(sem("gain_loaded"), 16)

                def scale(b):
                    dve.wait_ge(sem("root"), b + 1)
                    dve.reciprocal(rstd[:, b:b + 1], root[:, b:b + 1]).then_inc(sem("rstd"), 1)
                    dve.wait_ge(sem("rstd"), b + 1)
                    if b >= 2:
                        dve.wait_ge(sem("turned"), b - 1)
                    dve.scalar_tensor_tensor(out=scaled[:, b % 2, :], in0=src_tile[:, b, :], scalar=rstd[:, b:b + 1],
                                             in1=gain[:, :], op0=ALU.mult, op1=ALU.mult).then_inc(sem("scaled"), 1)

                scale(0)
                scale(1)
                for b in range(NB):
                    if b + 2 < NB:
                        scale(b + 2)
                    dve.wait_ge(sem("high"), b + 1)
                    dve.tensor_tensor(AL[:, :, b * P:(b + 1) * P], turned[:, b % 2, :, :], AH[:, :, b * P:(b + 1) * P].bitcast(F32),
                                      ALU.subtract).then_inc(sem("turned_free"), 1)


def setup(core):
    nc = core.nc
    with stage(core) as (ctx, sem):
        with nc.Block() as block:

            @block.gpsimd
            def _(pool):
                pool.memset(core.ident[:, :], 0.0).then_inc(sem("cleared"), 1)
                pool.memset(core.ones[:, :], 1.0)
                pool.memset(core.eps[:, :], EPS)
                pool.wait_ge(sem("cleared"), 1)
                pool.affine_select(out=core.ident[:, :], in_=core.ident[:, :], compare_op=ALU.not_equal, fill=1.0,
                                   base=0, pattern=[[-1, P]], channel_multiplier=1)


def make_core(nc, io, ctx):
    core = Core(nc, io)
    core.serial = 0
    core.limit = nc.sbuf_top
    core.pool = [ctx.enter_context(nc.semaphore(f"stage_sem{i}")) for i in range(120)]
    core.ident = sbuf(core, ctx, "ident", [P, P])
    core.ones = sbuf(core, ctx, "ones", [P, P])
    core.eps = sbuf(core, ctx, "eps", [P, 1])
    core.w_at = nc.sbuf_base
    core.w_slots = {part: [sbuf(core, ctx, f"w_{part}{s}", [P, D], dtype) for s in range(2)]
                    for part, dtype in (("raw", F32), ("high", F32R), ("low", F32R))}
    core.act_at = nc.sbuf_base
    core.AH = sbuf(core, ctx, "act_high", [P, KD, SEQ], F32R)
    core.AL = sbuf(core, ctx, "act_low", [P, KD, SEQ], F32R)
    return core


def per_channel(vector, chunks=None):
    return vector.rearrange("(k p) -> p k", p=P)


def over_loop(engine, count, body):
    with engine.Fori(0, count - 1) as n:
        body(n, True)
    body(count - 1, False)


def first_then_loop(engine, count, body):
    body(0)
    with engine.Fori(1, count) as n:
        body(n)


class Softplus:

    def __init__(self, core, ctx, sem, name, shape):
        self.t, self.w, self.d, self.e = (sbuf(core, ctx, f"{name}_{x}", shape) for x in "twde")
        self.sem, self.name = sem, name

    def s(self, what):
        return self.sem(f"{self.name}_{what}")

    def on_act(self, act, z, turn=0):
        t, w = self.t, self.w
        act.activation(t[:, :], z, ACT.Abs).then_inc(self.s("abs"), 1)
        act.wait_ge(self.s("abs"), turn + 1)
        act.activation(t[:, :], t[:, :], ACT.Exp, scale=-1.0).then_inc(self.s("t"), 1)
        act.wait_ge(self.s("w"), turn + 1)
        act.activation(self.e[:, :], w[:, :], ACT.Ln).then_inc(self.s("ln"), 1)

    def on_dve(self, dve, z, out, turn=0):
        t, w, d, e = (x[:, :] for x in (self.t, self.w, self.d, self.e))
        s = self.s
        dve.wait_ge(s("t"), turn + 1)
        dve.tensor_scalar(w, t, 1.0, None, ALU.add).then_inc(s("w"), 1)
        dve.wait_ge(s("w"), turn + 1)
        dve.tensor_scalar(d, w, 1.0, None, ALU.subtract).then_inc(s("d"), 1)
        dve.wait_ge(s("ln"), turn + 1)
        dve.wait_ge(s("d"), turn + 1)
        dve.tensor_scalar(w, d, 0.0, None, ALU.is_equal).then_inc(s("same"), 1)
        dve.wait_ge(s("same"), turn + 1)
        dve.tensor_tensor(e, e, w, ALU.add).then_inc(s("num"), 1)
        dve.tensor_tensor(d, d, w, ALU.add).then_inc(s("den"), 1)
        dve.wait_ge(s("den"), turn + 1)
        dve.reciprocal(w, d).then_inc(s("rec"), 1)
        dve.wait_ge(s("num"), turn + 1)
        dve.tensor_tensor(e, e, t, ALU.mult).then_inc(s("numt"), 1)
        dve.wait_ge(s("rec"), turn + 1)
        dve.wait_ge(s("numt"), turn + 1)
        dve.tensor_tensor(e, e, w, ALU.mult).then_inc(s("log1p"), 1)
        dve.wait_ge(s("log1p"), turn + 1)
        dve.scalar_tensor_tensor(out=out, in0=z, scalar=0.0, in1=e, op0=ALU.max, op1=ALU.add).then_inc(s("out"), 1)


def stage_rnn(core, ahead):
    nc, io = core.nc, core.io
    w_in = io["w_in"][0]
    AH, AL, YH, YL = core.AH, core.AL, core.YH, core.YL
    with stage(core) as (ctx, sem):
        W = WeightTiles(core, ctx, sem, KD)
        nxt = Ahead(core, sem, ahead, W, (KD, KD))
        taps = sbuf(core, ctx, "taps", [P, 4, KD])
        bias = sbuf(core, ctx, "bias", [P, 4, KD])
        minus_a = sbuf(core, ctx, "minus_a", [P, KD])
        soft = sbuf(core, ctx, "soft", [P, KD])
        rate = sbuf(core, ctx, "rate", [P, 2, KD])
        wr = sbuf(core, ctx, "wr", [P, P])
        wi = sbuf(core, ctx, "wi", [P, P])
        xc, G, R, I, A, Q, Hs = (sbuf(core, ctx, n, [P, SEQ]) for n in ("xc", "gelu", "r", "i", "a", "q", "h"))
        SP_ = Softplus(core, ctx, sem, "sp", [P, KD])
        pX, pG, pR, pI = (psum(core, ctx, n, [P, 2, HALF]) for n in ("px", "pg", "pr", "pi"))
        flat = lambda t: t[:, :, :].rearrange("p a b -> p (a b)")
        with nc.Block() as block:

            @block.sync
            def _(sp):
                for j in range(4):
                    sp.dma_start(taps[:, j, :], per_channel(io["rnn_conv_w"][0, j])).then_inc(sem("small"), 16)
                for j, name in enumerate(("rnn_conv_b", "rg_b_r", "rg_b_i", "rg_a")):
                    sp.dma_start(bias[:, j, :], per_channel(io[name][0])).then_inc(sem("small"), 16)
                def turn(n):
                    for slot, at in ((0, 0), (1, D)):
                        W.load(sp, slot, n, w_in[:, bass.ds(n * P + at, P)])
                    sp.wait_ge(sem("gates_free"), n + 1)
                    sp.dma_start(wr[:, :], io["rg_w_r"][0].rearrange("n c d -> (n c) d")[bass.ds(n * P, P), :]).then_inc(sem("wr"), 16)
                    sp.dma_start(wi[:, :], io["rg_w_i"][0].rearrange("n c d -> (n c) d")[bass.ds(n * P, P), :]).then_inc(sem("wi"), 16)
                first_then_loop(sp, KD, turn)
                nxt.load(sp)

            @block.gpsimd
            def _(pool):
                W.open_pool(pool)
                def turn(n):
                    for slot in range(2):
                        W.split_low(pool, slot, n)
                first_then_loop(pool, KD, turn)
                nxt.split_low(pool)

            @block.tensor
            def _(pe):
                W.open_pe(pe)
                pe.sem_inc(sem("gates_free"), 1)
                with pe.Fori(0, KD) as n:
                    W.wait(pe, 0, n)
                    pe.wait_ge(sem("px_free"), n + 1)
                    W.multiply(pe, 0, pX, AH, AL)
                    W.wait(pe, 1, n)
                    pe.wait_ge(sem("pg_free"), n + 1)
                    W.multiply(pe, 1, pG, AH, AL)
                    pe.wait_ge(sem("conv"), n + 1)
                    pe.wait_ge(sem("pri_free"), n + 1)
                    pe.wait_ge(sem("wr"), (n + 1) * 16)
                    pe.wait_ge(sem("wi"), (n + 1) * 16)
                    for p, w in ((pR, wr), (pI, wi)):
                        for h in range(2):
                            last = pe.matmul(p[:, h, :], w[:, :], xc[:, h * HALF:(h + 1) * HALF], start=True, stop=True)
                    last.then_inc(sem("gates_free"), 1)

            @block.scalar
            def _(act):
                act.sem_inc(sem("pg_free"), 1)
                act.sem_inc(sem("pri_free"), 1)
                act.wait_ge(sem("minus_a"), 1)
                SP_.on_act(act, minus_a[:, :])
                act.wait_ge(sem("rate"), 2)

                def chunk(n, more):
                    act.wait_ge(W.s("used", 0), n + 2)
                    act.wait_ge(sem("xc_free"), n + 1)
                    act.activation(xc[:, :], flat(pX), ACT.Identity, scale=taps[:, 3, bass.ds(n, 1)],
                                   bias=bias[:, 0, bass.ds(n, 1)]).then_inc(sem("tap3"), 1)
                    if more:
                        W.split_high(act, 0, n + 1)
                    else:
                        nxt.split_high(act, 0)
                    act.wait_ge(W.s("used", 1), n + 2)
                    act.wait_ge(sem("yl"), n + 1)
                    act.activation(G[:, :], flat(pG), ACT.Gelu_apprx_tanh).then_inc(sem("pg_free"), 1)
                    if more:
                        W.split_high(act, 1, n + 1)
                    else:
                        nxt.split_high(act, 1)
                    act.wait_ge(sem("gates_free"), n + 2)
                    act.activation(R[:, :], flat(pR), ACT.Sigmoid, bias=bias[:, 1, bass.ds(n, 1)]).then_inc(sem("r"), 1)
                    act.activation(I[:, :], flat(pI), ACT.Sigmoid, bias=bias[:, 2, bass.ds(n, 1)]).then_inc(sem("pri_free"), 1)
                    act.wait_ge(sem("r"), n + 1)
                    act.activation(A[:, :], R[:, :], ACT.Exp, scale=rate[:, 0, bass.ds(n, 1)]).then_inc(sem("a"), 1)
                    act.activation(R[:, :], R[:, :], ACT.Tanh, scale=rate[:, 1, bass.ds(n, 1)]).then_inc(sem("tanh"), 1)
                    act.wait_ge(sem("one_minus_a2"), n + 1)
                    act.activation(Q[:, :], Q[:, :], ACT.Sqrt).then_inc(sem("root"), 1)
                    act.wait_ge(sem("y"), n + 1)
                    act.activation(YH[:, bass.ds(n, 1), :].squeeze(1), G[:, :], ACT.Copy).then_inc(sem("yh"), 1)
                over_loop(act, KD, chunk)

            @block.vector
            def _(dve):
                dve.sem_inc(sem("px_free"), 1)
                dve.sem_inc(sem("xc_free"), 1)
                dve.sem_inc(sem("yl"), 1)
                dve.wait_ge(sem("small"), 128)
                dve.tensor_scalar(minus_a[:, :], bias[:, 3, :], -1.0, None, ALU.mult).then_inc(sem("minus_a"), 1)
                dve.wait_ge(sem("minus_a"), 1)
                SP_.on_dve(dve, minus_a[:, :], soft[:, :])
                dve.wait_ge(SP_.s("out"), 1)
                dve.tensor_scalar(rate[:, 0, :], soft[:, :], -8.0, None, ALU.mult).then_inc(sem("rate"), 1)
                dve.tensor_scalar(rate[:, 1, :], soft[:, :], 8.0, None, ALU.mult).then_inc(sem("rate"), 1)
                with dve.Fori(0, KD) as n:
                    x = flat(pX)
                    dve.wait_ge(sem("tap3"), n + 1)
                    for back in (1, 2, 3):
                        ins = dve.scalar_tensor_tensor(out=xc[:, back:], in0=x[:, :SEQ - back], scalar=taps[:, 3 - back, bass.ds(n, 1)],
                                                       in1=xc[:, back:], op0=ALU.mult, op1=ALU.add)
                        if back < 3:
                            ins.then_inc(sem("taps"), 1)
                            dve.wait_ge(sem("taps"), n * 2 + back)
                    ins.then_inc(sem("conv"), 1)
                    dve.wait_ge(sem("conv"), n + 1)
                    dve.sem_inc(sem("px_free"), 1)
                    dve.wait_ge(sem("pri_free"), n + 2)
                    dve.tensor_tensor(I[:, :], I[:, :], xc[:, :], ALU.mult).then_inc(sem("ix"), 1)
                    dve.wait_ge(sem("a"), n + 1)
                    dve.tensor_tensor(Q[:, :], A[:, :], A[:, :], ALU.mult).then_inc(sem("a2"), 1)
                    dve.wait_ge(sem("a2"), n + 1)
                    dve.wait_ge(sem("tanh"), n + 1)
                    dve.scalar_tensor_tensor(out=Q[:, :], in0=Q[:, :], scalar=1.0, in1=R[:, :], op0=ALU.add, op1=ALU.mult).then_inc(sem("one_minus_a2"), 1)
                    dve.wait_ge(sem("root"), n + 1)
                    dve.wait_ge(sem("ix"), n + 1)
                    dve.tensor_tensor(Q[:, :], Q[:, :], I[:, :], ALU.mult).then_inc(sem("xc_free"), 1)
                    dve.wait_ge(sem("xc_free"), n + 2)
                    dve.tensor_tensor_scan(Hs[:, :], A[:, :], Q[:, :], 0.0, ALU.mult, ALU.add).then_inc(sem("scan"), 1)
                    dve.wait_ge(sem("scan"), n + 1)
                    dve.wait_ge(sem("pg_free"), n + 2)
                    dve.tensor_tensor(G[:, :], G[:, :], Hs[:, :], ALU.mult).then_inc(sem("y"), 1)
                    dve.wait_ge(sem("yh"), n + 1)
                    dve.tensor_tensor(YL[:, bass.ds(n, 1), :].squeeze(1), G[:, :], YH[:, bass.ds(n, 1), :].squeeze(1).bitcast(F32),
                                      ALU.subtract).then_inc(sem("yl"), 1)


ROWS_K = 2
GATES_AT = 2 * D + 6 * HALF + 8
FOX_F_AT = 2 * D + 6 * HALF


def stage_branches(core, parts, ahead, part_in=None, part_out=None):
    nc, io = core.nc, core.io
    w_in = io["w_in"][0]
    AH, AL, YH, YL = core.AH, core.AL, core.YH, core.YL
    NP = len(parts)
    with stage(core) as (ctx, sem):
        W = WeightTiles(core, ctx, sem, KD)
        nxt = Ahead(core, sem, ahead, W, (KD * NP, KD * NP))
        gate_b = sbuf(core, ctx, "gate_b", [P, NP, KD])
        gate = [sbuf(core, ctx, f"gate{j}", [P, SEQ]) for j in range(NP)]
        other = sbuf(core, ctx, "other", [P, SEQ])
        pG = [psum(core, ctx, f"pg{j}", [P, 2, HALF]) for j in range(NP)]
        pY = [psum(core, ctx, f"py{j}", [P, 2, HALF]) for j in range(NP)]
        flat = lambda t: t[:, :, :].rearrange("p a b -> p (a b)")
        with nc.Block() as block:

            @block.sync
            def _(sp):
                for j, (g, _, _, _) in enumerate(parts):
                    sp.dma_start(gate_b[:, j, :], per_channel(io["gate_b"][0, g])).then_inc(sem("gate_b"), 16)

                def load(n):
                    for j, (g, w, nk, _) in enumerate(parts):
                        W.load(sp, 0, n * NP + j, w_in[:, bass.ds(n * P + GATES_AT + g * D, P)])
                        W.load(sp, 1, n * NP + j, w[:, bass.ds(n * P, P)], nk)
                    if part_in is not None:
                        sp.wait_ge(sem("other_free"), n + 1)
                        sp.dma_start(other[:, :], part_in.rearrange("n p s -> (n p) s")[bass.ds(n * P, P), :]).then_inc(sem("other"), 16)

                def store(n):
                    if part_out is not None:
                        sp.wait_ge(sem("sum"), n + 1)
                        sp.sem_inc(sem("store_asked"), 1)
                        sp.dma_start(part_out.rearrange("n p s -> (n p) s")[bass.ds(n * P, P), :], gate[0][:, :]).then_inc(sem("m_stored"), 16)

                load(0)
                with sp.Fori(1, KD) as n:
                    load(n)
                    store(n - 1)
                nxt.load(sp)
                store(KD - 1)
                if part_out is not None:
                    sp.wait_ge(sem("m_stored"), KD * 16)

            @block.gpsimd
            def _(pool):
                W.open_pool(pool)
                def turn(n):
                    for j, (_, _, nk, _) in enumerate(parts):
                        W.split_low(pool, 0, n * NP + j)
                        W.split_low(pool, 1, n * NP + j, nk)
                first_then_loop(pool, KD, turn)
                nxt.split_low(pool)

            @block.tensor
            def _(pe):
                W.open_pe(pe)
                with pe.Fori(0, KD) as n:
                    for j, (_, _, nk, y0) in enumerate(parts):
                        W.wait(pe, 0, n * NP + j)
                        pe.wait_ge(sem(f"pg_free{j}"), n + 1)
                        W.multiply(pe, 0, pG[j], AH, AL)
                        W.wait(pe, 1, n * NP + j)
                        pe.wait_ge(sem(f"py_free{j}"), n + 1)
                        W.multiply(pe, 1, pY[j], YH[:, y0:y0 + nk, :], YL[:, y0:y0 + nk, :], nk)

            @block.scalar
            def _(act):
                act.wait_ge(sem("gate_b"), 16 * NP)
                for j in range(NP):
                    act.sem_inc(sem(f"pg_free{j}"), 1)

                def chunk(n, more):
                    for j in range(NP):
                        turn = n * NP + j
                        act.wait_ge(W.s("used", 0), turn + 2)
                        act.wait_ge(sem(f"gate_free{j}"), n + 1)
                        act.activation(gate[j][:, :], flat(pG[j]), ACT.Sigmoid, bias=gate_b[:, j, bass.ds(n, 1)]).then_inc(sem(f"pg_free{j}"), 1)
                        if more or j < NP - 1:
                            W.split_high(act, 0, turn + 1)
                            W.split_high(act, 1, turn + 1, parts[(j + 1) % NP][2])
                over_loop(act, KD, chunk)
                nxt.split_high(act)

            @block.vector
            def _(dve):
                for j in range(NP):
                    dve.sem_inc(sem(f"py_free{j}"), 1)
                    dve.sem_inc(sem(f"gate_free{j}"), 1)
                dve.sem_inc(sem("other_free"), 1)
                with dve.Fori(0, KD) as n:
                    for j in range(NP):
                        dve.wait_ge(sem(f"pg_free{j}"), n + 2)
                        dve.wait_ge(W.s("used", 1), n * NP + j + 2)
                        dve.tensor_tensor(gate[j][:, :], gate[j][:, :], flat(pY[j]), ALU.mult).then_inc(sem(f"py_free{j}"), 1)
                        dve.wait_ge(sem(f"py_free{j}"), n + 2)
                    if part_out is not None:
                        dve.tensor_tensor(gate[0][:, :], gate[0][:, :], gate[1][:, :], ALU.add).then_inc(sem("sum"), 1)
                        dve.wait_ge(sem("sum"), n + 1)
                        dve.wait_ge(sem("m_stored"), (n + 1) * 16)
                    else:
                        dve.wait_ge(sem("other"), (n + 1) * 16)
                        dve.tensor_tensor(core.M[:, bass.ds(n, 1), :].squeeze(1), gate[0][:, :], other[:, :], ALU.add).then_inc(sem("sum"), 1)
                        dve.wait_ge(sem("sum"), n + 1)
                    for j in range(NP):
                        dve.sem_inc(sem(f"gate_free{j}"), 1)
                    dve.sem_inc(sem("other_free"), 1)


def rows_tiles(w, chunks):
    step = ROWS_K * P
    return [w[k * step:(k + 1) * step, half * HALF:(half + 1) * HALF] for half in range(2) for k in range(chunks // ROWS_K)]


def stage_rows(core, XH, XL, nk, w, acc, whole=None, load_acc=None, add=True):
    nc = core.nc
    G = ROWS_K
    NG = nk // G
    with stage(core) as (ctx, sem):
        W = WeightTiles(core, ctx, sem, G, HALF)
        out = psum(core, ctx, "rows", [P, NB, HALF])
        tiles = [(half, kg) for half in range(2) for kg in range(NG)]
        with nc.Block() as block:

            @block.sync
            def _(sp):
                if load_acc is not None:
                    sp.dma_start(acc[:, :, :], load_acc.rearrange("(b p) n -> p b n", p=P)).then_inc(sem("acc_loaded"), 16)
                for t, (half, kg) in enumerate(tiles):
                    W.load(sp, t % 2, t // 2, rows_tiles(w, nk)[t])

            @block.gpsimd
            def _(pool):
                W.open_pool(pool)
                for t in range(len(tiles)):
                    W.split_low(pool, t % 2, t // 2)

            @block.scalar
            def _(act):
                if whole is not None:
                    for k in range(nk):
                        act.activation(XH[:, k, :], whole[:, k, :], ACT.Copy).then_inc(sem("x_high"), 1)
                for t in range(len(tiles)):
                    W.split_high(act, t % 2, t // 2)

            @block.tensor
            def _(pe):
                W.open_pe(pe)
                for t, (half, kg) in enumerate(tiles):
                    W.wait(pe, t % 2, t // 2)
                    for b in range(NB):
                        if half and kg == 0:
                            pe.wait_ge(sem("added"), b + 1)
                        steps = slice(b * P, (b + 1) * P)
                        for k in range(G):
                            kk = kg * G + k
                            if whole is not None and b == 0 and half == 0:
                                pe.wait_ge(sem("x_low"), kk + 1)
                            for i, (x, v) in enumerate(((XH, W.high), (XL, W.high), (XH, W.low))):
                                last = pe.matmul(out[:, b, :], x[:, kk, steps], v[t % 2][:, k, :],
                                                 start=(kk == 0 and i == 0), stop=(kk == nk - 1 and i == 2))
                        if kg == NG - 1 and b < NB - 1:
                            last.then_inc(sem("out"), 1)
                    last.then_inc(W.s("used", t % 2), 1)

            @block.vector
            def _(dve):
                if whole is not None:
                    for k in range(nk):
                        dve.wait_ge(sem("x_high"), k + 1)
                        dve.tensor_tensor(XL[:, k, :], whole[:, k, :], XH[:, k, :].bitcast(F32), ALU.subtract).then_inc(sem("x_low"), 1)
                if load_acc is not None:
                    dve.wait_ge(sem("acc_loaded"), 16)
                for half in range(2):
                    cols = slice(half * HALF, (half + 1) * HALF)
                    for b in range(NB):
                        t = half * NG + NG - 1
                        if b < NB - 1:
                            dve.wait_ge(sem("out"), half * (NB - 1) + b + 1)
                        else:
                            dve.wait_ge(W.s("used", t % 2), t // 2 + 2)
                        if add:
                            dve.tensor_tensor(acc[:, b, cols], acc[:, b, cols], out[:, b, :], ALU.add).then_inc(sem("added"), 1)
                        else:
                            dve.tensor_copy(acc[:, b, cols], out[:, b, :]).then_inc(sem("added"), 1)


BUCKETS, MAX_DIST = 32, 128
LINE = SEQ + P


def bucket_edges():
    half = BUCKETS // 2
    n = np.arange(1, SEQ + 1, dtype=np.float64)
    large = half + np.floor(np.log(n / half) / np.log(MAX_DIST / half) * (BUCKETS - half) + 1e-9)
    of = np.concatenate([[0], np.where(n < half, n, np.minimum(large, BUCKETS - 1))])
    first = [int(np.argmax(of == b)) for b in range(BUCKETS)]
    return np.array([[a, b] for a, b in zip(first, first[1:] + [SEQ])], np.float32)


def stage_attention_tables(core, ahead):
    nc, io = core.nc, core.io
    AH, AL = core.AH, core.AL
    NH = 4
    with stage(core) as (ctx, sem):
        W = WeightTiles(core, ctx, sem, KD, slots=1)
        nxt = Ahead(core, sem, ahead, W, (1, 0))
        dist = sbuf(core, ctx, "dist", [BUCKETS, LINE])
        hot = sbuf(core, ctx, "hot", [BUCKETS, LINE])
        edges = sbuf(core, ctx, "edges", [BUCKETS, 2])
        rel = sbuf(core, ctx, "rel", [BUCKETS, NH])
        rel_wide = sbuf(core, ctx, "rel_wide", [BUCKETS, NH, P])
        line = sbuf(core, ctx, "line", [P, 2, LINE])
        bf = sbuf(core, ctx, "bf", [8, 1])
        z, t, f, c = (sbuf(core, ctx, n, [8, SEQ]) for n in ("z", "t", "f", "c"))
        pf = psum(core, ctx, "pf", [P, 2, HALF])
        pl = psum(core, ctx, "pl", [P, 3, HALF])
        with nc.Block() as block:

            @block.sync
            def _(sp):
                sp.dma_start(edges[:, :], io["bucket_edges"]).then_inc(sem("edges"), 16)
                sp.dma_start(rel[:, :], io["rel_bias"]).then_inc(sem("rel"), 16)
                sp.dma_start(bf[:, :], io["fox_b_f"].rearrange("a n -> n a")).then_inc(sem("bf"), 16)
                nxt.load(sp)
                for h in range(NH):
                    sp.wait_ge(sem("line"), h + 2)
                    sp.dma_start(core.lines[h], line[:, h % 2, :]).then_inc(sem("line_stored" if h % 2 == 0 else "line_stored1"), 16)
                sp.wait_ge(sem("c"), 1)
                sp.dma_start(core.neg_c, c[:, :]).then_inc(sem("c_stored"), 16)
                sp.wait_ge(sem("c_stored"), 16)
                sp.wait_ge(sem("line_stored"), 32)
                sp.wait_ge(sem("line_stored1"), 32)

            @block.gpsimd
            def _(pool):
                W.open_pool(pool)
                pool.iota(dist[:, :], pattern=[[-1, LINE]], base=SEQ - 1, channel_multiplier=0,
                          allow_small_or_imprecise_dtypes=True).then_inc(sem("dist"), 1)
                nxt.split_low(pool, 1)
                nxt.split_low(pool, 0)

            @block.scalar
            def _(act):
                nxt.split_high(act, 1)
                act.wait_ge(sem("z"), 1)
                act.activation(t[:, :], z[:, :], ACT.Abs).then_inc(sem("abs"), 1)
                act.wait_ge(sem("abs"), 1)
                act.activation(t[:, :], t[:, :], ACT.Exp, scale=-1.0).then_inc(sem("exp"), 1)
                act.wait_ge(sem("exp"), 1)
                act.activation(t[:, :], t[:, :], ACT.Ln, bias=1.0).then_inc(sem("ln"), 1)
                nxt.split_high(act, 0)

            @block.tensor
            def _(pe):
                W.open_pe(pe)
                pe.wait_ge(sem("hot"), 1)
                pe.wait_ge(sem("rel_wide"), 1)
                for h in range(NH):
                    pe.wait_ge(sem("line"), h + 1)
                    for j in range(3):
                        cols = slice(j * HALF, min((j + 1) * HALF, LINE))
                        last = pe.matmul(pl[:, j, 0:cols.stop - cols.start], rel_wide[:, h, :], hot[:, cols], start=True, stop=True)
                    last.then_inc(sem("pl"), 1)
                W.wait(pe, 0, 0)
                W.multiply(pe, 0, pf, AH, AL)

            @block.vector
            def _(dve):
                dve.wait_ge(sem("edges"), 16)
                dve.wait_ge(sem("dist"), 1)
                dve.tensor_scalar(hot[:, :], dist[:, :], edges[:, 0:1], None, ALU.is_ge).then_inc(sem("above"), 1)
                dve.wait_ge(sem("above"), 1)
                dve.scalar_tensor_tensor(out=hot[:, :], in0=dist[:, :], scalar=edges[:, 1:2], in1=hot[:, :],
                                         op0=ALU.is_lt, op1=ALU.mult).then_inc(sem("hot"), 1)
                dve.wait_ge(sem("rel"), 16)
                dve.tensor_copy(rel_wide[:, :, :], rel[:, :].unsqueeze(2).to_broadcast([BUCKETS, NH, P])).then_inc(sem("rel_wide"), 1)
                dve.sem_inc(sem("line"), 1)
                for h in range(NH):
                    dve.wait_ge(sem("pl"), h + 1)
                    if h >= 2:
                        dve.wait_ge(sem(("line_stored", "line_stored1")[h % 2]), 16)
                    dve.tensor_copy(line[:, h % 2, 0:SEQ], pl[:, :, :].rearrange("p a b -> p (a b)")[:, 0:SEQ]).then_inc(sem("line_low"), 1)
                    dve.wait_ge(sem("line_low"), h + 1)
                    dve.memset(line[:, h % 2, SEQ:LINE], NEG).then_inc(sem("line"), 1)
                dve.wait_ge(sem("bf"), 16)
                dve.wait_ge(W.s("used", 0), 2)
                dve.tensor_scalar(z[:, :], pf[0:8, :, :].rearrange("p a b -> p (a b)"), bf[:, 0:1], None, ALU.add).then_inc(sem("z"), 1)
                dve.wait_ge(sem("z"), 1)
                dve.memset(f[:, :], 1.0).then_inc(sem("f"), 1)
                dve.tensor_scalar(c[:, :], z[:, :], 0.0, None, ALU.min).then_inc(sem("min"), 1)
                dve.wait_ge(sem("ln"), 1)
                dve.wait_ge(sem("min"), 1)
                dve.tensor_tensor(z[:, :], t[:, :], c[:, :], ALU.subtract).then_inc(sem("nlf"), 1)
                dve.wait_ge(sem("nlf"), 1)
                dve.wait_ge(sem("f"), 1)
                dve.tensor_tensor_scan(c[:, :], f[:, :], z[:, :], 0.0, ALU.mult, ALU.add).then_inc(sem("c"), 1)


def stage_attention(core, kind, q_at, k_at, v_at, y0, ahead):
    nc, io = core.nc, core.io
    w_in = io["w_in"][0]
    AH, AL, YH, YL, ident = core.AH, core.AL, core.YH, core.YL, core.ident
    NH = 4
    U = 2 * NB
    diff = kind == "diff"
    with stage(core) as (ctx, sem):
        W = WeightTiles(core, ctx, sem, KD)
        nxt = Ahead(core, sem, ahead, W, (8, 4))
        Q = [sbuf(core, ctx, f"q{c}", [P, SEQ]) for c in range(2)]
        K = sbuf(core, ctx, "k", [P, SEQ])
        V = sbuf(core, ctx, "v", [P, NB, P])
        bias = sbuf(core, ctx, "bias", [P, 1 if diff else 2, SEQ])
        S = sbuf(core, ctx, "scores", [P, 2, SEQ])
        PR = sbuf(core, ctx, "probs", [P, 2, SEQ])
        PT = sbuf(core, ctx, "probs_t", [P, 2, SEQ])
        O = sbuf(core, ctx, "o", [P, NB, P]) if diff else None
        OS = sbuf(core, ctx, "o_scaled", [P, NB, P])
        VT = OS[:, :, :].rearrange("p b t -> p (b t)")
        mx = sbuf(core, ctx, "mx", [P, U])
        nmx = sbuf(core, ctx, "nmx", [P, U])
        total = sbuf(core, ctx, "total", [P, U])
        part = sbuf(core, ctx, "part", [P, U])
        mask = sbuf(core, ctx, "mask", [P, P])
        gain = sbuf(core, ctx, "gain", [P, 1])
        lq = sbuf(core, ctx, "lq", [P, 4, 64])
        lam = sbuf(core, ctx, "lam", [P, 4])
        blank = sbuf(core, ctx, "blank", [1, 2 * U])
        norm = sbuf(core, ctx, "norm", [P, 3, NB])
        pS = [psum(core, ctx, f"ps{c}", [P, 2, HALF]) for c in range(2)]
        pT = [psum(core, ctx, f"pt{c}", [P, 4, P]) for c in range(2)]
        pO = [psum(core, ctx, f"po{c}", [P, 4, P]) for c in range(2)]
        flat = lambda t: t[:, :, :].rearrange("p a b -> p (a b)")
        groups = [(u, g, min(4, u // 2 + 1 - g)) for u in range(U) for g in range(0, u // 2 + 1, 4)]
        GN = len(groups)
        last_group = {u: n for n, (u, _, _) in enumerate(groups)}

        with nc.Block() as block:

            @block.sync
            def _(sp):
                if diff:
                    for j, name in enumerate(("diff_lq1", "diff_lk1", "diff_lq2", "diff_lk2")):
                        sp.dma_start(lq[:, j, :], io[name][0].partition_broadcast(P)).then_inc(sem("lq"), 16)
                    sp.dma_start(gain[:, :], io["diff_subln_g"].rearrange("a n -> n a")).then_inc(sem("gain"), 16)
                def turn(h):
                    for slot, turn, at in ((0, h * 2, q_at), (1, h, k_at), (0, h * 2 + 1, v_at)):
                        W.load(sp, slot, turn, w_in[:, bass.ds(h * P + at, P)])
                    sp.wait_ge(sem("bias_free"), h + 1)
                    if diff:
                        src = core.lines.rearrange("h p y -> h (p y)")[bass.ds(h, 1), P - 1:P - 1 + P * (LINE - 1)]
                        sp.dma_start(bias[:, 0, :], src.rearrange("a (p y) -> (a p) y", p=P)[:, 0:SEQ]).then_inc(sem("bias"), 16)
                    else:
                        src = core.neg_c.rearrange("(h c) s -> h (c s)", c=2)[bass.ds(h, 1), :]
                        sp.dma_start(bias[:, :, :].rearrange("p c s -> p (c s)"), src.squeeze(0).partition_broadcast(P)).then_inc(sem("bias"), 16)
                first_then_loop(sp, NH, turn)
                nxt.load(sp)

            @block.gpsimd
            def _(pool):
                W.open_pool(pool)
                if not diff:
                    pool.memset(mask[:, :], 0.0).then_inc(sem("mask0"), 1)
                    pool.wait_ge(sem("mask0"), 1)
                    pool.affine_select(out=mask[:, :], in_=mask[:, :], compare_op=ALU.is_ge, fill=NEG, base=0,
                                       pattern=[[-1, P]], channel_multiplier=1).then_inc(sem("mask"), 1)
                    pool.wait_ge(sem("mask"), 1)
                for c in range(2):
                    pool.memset(Q[c][64 * (1 - c):64 * (2 - c), :], 0.0).then_inc(sem("q_zero"), 1)
                    pool.wait_ge(sem("q_zero"), c + 1)
                def turn(h):
                    W.split_low(pool, 0, h * 2)
                    W.split_low(pool, 1, h)
                    W.split_low(pool, 0, h * 2 + 1)
                first_then_loop(pool, NH, turn)
                nxt.split_low(pool, 1)
                nxt.split_low(pool, 0)

            @block.tensor
            def _(pe):
                W.open_pe(pe)
                pe.wait_ge(sem("q_zero"), 2)
                if not diff:
                    pe.wait_ge(sem("mask"), 1)
                def project_q(h):
                    W.wait(pe, 0, h * 2)
                    pe.wait_ge(sem("reduced"), h * U + U)
                    W.multiply(pe, 0, pS[0][:, :, :], AH, AL)

                def pair(h, more):
                    W.wait(pe, 1, h)
                    W.multiply(pe, 1, pS[1][:, :, :], AH, AL)

                    def scores(u):
                        b, c = u // 2, u % 2
                        n = (b + 1) * P
                        if u >= 2:
                            pe.wait_ge(sem("reduced"), h * U + u - 1 + U)
                        for a in range(0, n, HALF):
                            e = min(a + HALF, n)
                            masked = not diff and e == n
                            last = pe.matmul(pS[c][:, a // HALF, 0:e - a], Q[c][:, b * P:(b + 1) * P], K[:, a:e], start=True, stop=not masked)
                            if masked:
                                at = b * P - a
                                last = pe.matmul(pS[c][:, a // HALF, at:at + P], ident[:, :], mask[:, :], start=False, stop=True)
                        last.then_inc(sem("scores"), 1)

                    def turn(u):
                        for n, (uu, g, count) in enumerate(groups):
                            if uu != u:
                                continue
                            pe.wait_ge(sem("probs"), h * U + u + 1)
                            if n < 2:
                                pe.wait_ge(sem("v"), h * 2 + n + 1)
                            else:
                                pe.wait_ge(sem("probs_t"), h * GN + n - 1)
                            for j in range(count):
                                last = pe.transpose(pT[n % 2][:, j, :], PR[:, u % 2, (g + j) * P:(g + j + 1) * P], ident[:, :])
                            last.then_inc(sem("pt"), 1)

                    def values(u):
                        b, c = u // 2, u % 2
                        pe.wait_ge(sem("probs_t"), h * GN + last_group[u] + 1)
                        pe.wait_ge(sem("o_taken"), h * U + u + 1)
                        cols = slice(0, P) if diff else slice(c * 64, (c + 1) * 64)
                        for j in range(b + 1):
                            last = pe.matmul(pO[c][:, 0, 0:cols.stop - cols.start], PT[:, c, j * P:(j + 1) * P], V[:, j, cols],
                                             start=(j == 0), stop=(j == b))
                        last.then_inc(sem("o"), 1)

                    pe.wait_ge(sem("q"), h * 2 + 2)
                    pe.wait_ge(sem("k"), h + 1)
                    scores(0)
                    scores(1)
                    W.wait(pe, 0, h * 2 + 1)
                    W.multiply(pe, 0, [pS[0][:, 1, :], pS[1][:, 1, :]], AH, AL, halves=True)
                    pe.wait_ge(sem("vt"), h * 2 + 2)
                    for g in range(2):
                        pe.wait_ge(sem("yl"), h * 2 + 1)
                        for b in range(4):
                            blk = g * 4 + b
                            last = pe.transpose(pT[g][:, b, :], OS[:, blk, :], ident[:, :])
                        last.then_inc(sem("pt"), 1)
                    for u in range(U):
                        turn(u)
                        if u + 2 < U:
                            scores(u + 2)
                        values(u)
                    if more:
                        project_q(h + 1)
                    for g in range(2):
                        pe.wait_ge(sem("o_scaled"), h + 1)
                        pe.wait_ge(sem("probs_t"), h * GN + GN - 1 + g)
                        for b in range(4):
                            last = pe.transpose(pT[(GN + g) % 2][:, b, :], OS[:, g * 4 + b, :], ident[:, :])
                        last.then_inc(sem("pt"), 1)
                project_q(0)
                over_loop(pe, NH, pair)

            @block.scalar
            def _(act):
                if diff:
                    act.wait_ge(sem("lam_sums"), 2)
                    act.activation(lam[:, 2:4], lam[:, 0:2], ACT.Exp).then_inc(sem("lam_exp"), 1)

                def pair(h, more):
                    act.wait_ge(W.s("used", 0), h * 2 + 2)
                    W.split_high(act, 0, h * 2 + 1)
                    act.wait_ge(sem("scores"), h * U + U)
                    for c in range(2):
                        rows = slice(64 * c, 64 * (c + 1))
                        act.activation(Q[c][rows, :], flat(pS[0])[rows, :], ACT.Copy, scale=0.125).then_inc(sem("q"), 1)
                    act.wait_ge(W.s("used", 1), h + 2)
                    act.activation(K[:, :], flat(pS[1]), ACT.Copy).then_inc(sem("k"), 1)
                    if more:
                        W.split_high(act, 1, h + 1)
                    else:
                        nxt.split_high(act, 1)
                    for u in range(U):
                        if u == 2:
                            act.wait_ge(W.s("used", 0), h * 2 + 3)
                            for half in range(2):
                                act.activation(VT[:, half * HALF:(half + 1) * HALF], pS[half][:, 1, :], ACT.Copy).then_inc(sem("vt"), 1)
                            if more:
                                W.split_high(act, 0, h * 2 + 2)
                            else:
                                nxt.split_high(act, 0)
                        n = (u // 2 + 1) * P
                        act.wait_ge(sem("nmx"), h * U + u + 1)
                        act.wait_ge(sem("pt"), 4 + h * (GN + 4) + (last_group[u - 2] + 3 if u >= 2 else 0))
                        act.activation(PR[:, u % 2, 0:n], S[:, u % 2, 0:n], ACT.Exp, bias=nmx[:, u:u + 1],
                                       accum_out=total[:, u:u + 1]).then_inc(sem("probs"), 1)
                        if u >= 1:
                            evacuate(h, u - 1)
                    evacuate(h, U - 1)
                    if diff:
                        act.wait_ge(sem("mean"), h + 1)
                        act.activation(norm[:, 1, :], norm[:, 0, :], ACT.Sqrt, scale=1.0 / P, bias=core.eps[:, 0:1]).then_inc(sem("norm_root"), 1)
                    for g in range(2):
                        act.wait_ge(sem("pt"), 4 + h * (GN + 4) + 2 + GN + g + 1)
                        act.activation(YH[:, bass.ds(h + y0, 1), g * HALF:(g + 1) * HALF].squeeze(1), flat(pT[(GN + g) % 2]), ACT.Copy,
                                       scale=gain[:, 0:1] if diff else 1.0).then_inc(sem("yh"), 1)

                def evacuate(h, u):
                    for n, (uu, g, count) in enumerate(groups):
                        if uu != u or n % 2 == 0:
                            continue
                        act.wait_ge(sem("pt"), 4 + h * (GN + 4) + 2 + n + 1)
                        act.wait_ge(sem("probs_t"), h * GN + n)
                        if u >= 2:
                            act.wait_ge(sem("o"), h * U + u - 1)
                        act.activation(PT[:, u % 2, g * P:(g + count) * P], flat(pT[n % 2])[:, 0:count * P], ACT.Copy).then_inc(sem("probs_t"), 1)

                act.wait_ge(sem("opened"), 1)
                if diff:
                    act.wait_ge(sem("gain_scaled"), 1)
                over_loop(act, NH, pair)

            @block.vector
            def _(dve):
                dve.sem_inc(sem("bias_free"), 1)
                dve.sem_inc(sem("reduced"), U)
                dve.sem_inc(sem("yl"), 1)
                dve.sem_inc(sem("o_taken"), 2)
                dve.sem_inc(sem("scores"), U)
                dve.sem_inc(sem("pt"), 4)
                dve.sem_inc(sem("opened"), 1)
                if diff:
                    dve.wait_ge(sem("lq"), 64)
                    for j in range(2):
                        dve.tensor_tensor_reduce(lq[:, 2 * j, :], lq[:, 2 * j, :], lq[:, 2 * j + 1, :], 1.0, 0.0, ALU.mult, ALU.add,
                                                 lam[:, j:j + 1]).then_inc(sem("lam_sums"), 1)
                    dve.wait_ge(sem("lam_exp"), 1)
                    dve.tensor_tensor(lam[:, 0:1], lam[:, 3:4], lam[:, 2:3], ALU.subtract).then_inc(sem("lam"), 1)
                    dve.wait_ge(sem("lam"), 1)
                    dve.tensor_scalar(lam[:, 0:1], lam[:, 0:1], -LAM_INIT, None, ALU.add).then_inc(sem("lam"), 1)
                    dve.wait_ge(sem("gain"), 16)
                    dve.tensor_scalar(gain[:, :], gain[:, :], 1.0 - LAM_INIT, None, ALU.mult).then_inc(sem("gain_scaled"), 1)
                    dve.wait_ge(sem("lam"), 2)
                    dve.wait_ge(sem("gain_scaled"), 1)
                with dve.Fori(0, NH) as h:
                    dve.wait_ge(sem("bias"), (h + 1) * 16)

                    def reduce(u):
                        b, c = u // 2, u % 2
                        n = (b + 1) * P
                        dve.wait_ge(sem("scores"), h * U + U + u + 1)
                        if u >= 2:
                            dve.wait_ge(sem("probs"), h * U + u - 1)
                        dve.memset(blank[:, u:u + 1], 0.0)
                        table = bias[:, 0, SEQ - n:SEQ] if diff else bias[:, c, 0:n]
                        dve.tensor_tensor_reduce(S[:, c, 0:n], flat(pS[c])[:, 0:n], table, 1.0, NEG, ALU.add, ALU.max,
                                                 mx[:, u:u + 1]).then_inc(sem("reduced"), 1)
                        dve.wait_ge(sem("reduced"), h * U + U + u + 1)
                        dve.tensor_scalar(nmx[:, u:u + 1], mx[:, u:u + 1], -1.0, None, ALU.mult).then_inc(sem("nmx"), 1)

                    def evacuate(u):
                        for n, (uu, g, count) in enumerate(groups):
                            if uu != u or n % 2:
                                continue
                            dve.wait_ge(sem("pt"), 4 + h * (GN + 4) + 2 + n + 1)
                            if n:
                                dve.wait_ge(sem("probs_t"), h * GN + n)
                            if u >= 2:
                                dve.wait_ge(sem("o"), h * U + u - 1)
                            dve.tensor_copy(PT[:, u % 2, g * P:(g + count) * P], flat(pT[n % 2])[:, 0:count * P]).then_inc(sem("probs_t"), 1)

                    def take(u):
                        b, c = u // 2, u % 2
                        dve.wait_ge(sem("probs"), h * U + u + 1)
                        dve.reciprocal(part[:, u:u + 1], total[:, u:u + 1]).then_inc(sem("part"), 1)
                        dve.wait_ge(sem("part"), h * U + u + 1)
                        if diff and c == 1:
                            dve.tensor_scalar(part[:, u:u + 1], part[:, u:u + 1], lam[:, 0:1], None, ALU.mult).then_inc(sem("part_lam"), 1)
                            dve.wait_ge(sem("part_lam"), h * NB + b + 1)
                        dve.wait_ge(sem("o"), h * U + u + 1)
                        if diff:
                            if c == 0:
                                dve.tensor_scalar(O[:, b, :], pO[0][:, 0, :], part[:, u:u + 1], None, ALU.mult).then_inc(sem("o_taken"), 1)
                            else:
                                dve.wait_ge(sem("o_taken"), h * U + u + 2)
                                dve.scalar_tensor_tensor(out=O[:, b, :], in0=pO[1][:, 0, :], scalar=part[:, u:u + 1], in1=O[:, b, :],
                                                         op0=ALU.mult, op1=ALU.add).then_inc(sem("o_taken"), 1)
                                dve.wait_ge(sem("o_taken"), h * U + u + 3)
                                dve.memset(blank[:, U + u:U + u + 1], 0.0)
                                dve.tensor_tensor_reduce(OS[:, b, :], O[:, b, :], O[:, b, :], 1.0, 0.0, ALU.mult, ALU.add,
                                                         norm[:, 0, b:b + 1]).then_inc(sem("square"), 1)
                        else:
                            dve.tensor_scalar(OS[:, b, c * 64:(c + 1) * 64], pO[c][:, 0, 0:64], part[:, u:u + 1], None, ALU.mult).then_inc(sem("o_taken"), 1)

                    reduce(0)
                    reduce(1)
                    for g in range(2):
                        dve.wait_ge(sem("pt"), 4 + h * (GN + 4) + g + 1)
                        dve.tensor_copy(V[:, g * 4:(g + 1) * 4, :], pT[g][:, :, :]).then_inc(sem("v"), 1)
                    for u in range(U):
                        evacuate(u)
                        if u + 2 < U:
                            reduce(u + 2)
                        take(u)
                    dve.sem_inc(sem("bias_free"), 1)
                    if diff:
                        dve.wait_ge(sem("square"), (h + 1) * NB)
                        dve.sem_inc(sem("mean"), 1)
                        dve.wait_ge(sem("norm_root"), h + 1)
                        dve.reciprocal(norm[:, 2, :], norm[:, 1, :]).then_inc(sem("rstd"), 1)
                        dve.wait_ge(sem("rstd"), h + 1)
                        dve.tensor_tensor(OS[:, :, :], O[:, :, :], norm[:, 2, :].unsqueeze(2).to_broadcast([P, NB, P]), ALU.mult).then_inc(sem("o_scaled"), 1)
                    else:
                        dve.wait_ge(sem("o_taken"), h * U + U + 2)
                        dve.sem_inc(sem("o_scaled"), 1)
                    for g in range(2):
                        dve.wait_ge(sem("yh"), h * 2 + g + 1)
                        y = YL[:, bass.ds(h + y0, 1), g * HALF:(g + 1) * HALF].squeeze(1)
                        yh = YH[:, bass.ds(h + y0, 1), g * HALF:(g + 1) * HALF].squeeze(1).bitcast(F32)
                        if diff:
                            dve.scalar_tensor_tensor(out=y, in0=flat(pT[(GN + g) % 2]), scalar=gain[:, 0:1], in1=yh,
                                                     op0=ALU.mult, op1=ALU.subtract).then_inc(sem("yl"), 1)
                        else:
                            dve.tensor_tensor(y, flat(pT[(GN + g) % 2]), yh, ALU.subtract).then_inc(sem("yl"), 1)


LAM_INIT = 0.8 - 0.6 * 1.0


D_FF = 2816
FCH = D_FF // P


def stage_ffn(core, X):
    nc, io = core.nc, core.io
    AH, AL = core.AH, core.AL
    up, down = io["ffn_up"][0], io["ffn_down"][0]
    G = 2
    NG = FCH // G
    with stage(core) as (ctx, sem):
        W = WeightTiles(core, ctx, sem, KD)
        V = WeightTiles(core, ctx, sem, G, D, name="v", slots=1, ready=False)
        taps = sbuf(core, ctx, "taps", [P, 3, 2 * FCH])
        bias = sbuf(core, ctx, "bias", [P, 2 * FCH])
        UG = sbuf(core, ctx, "u_gate", [P, SEQ])
        UV = sbuf(core, ctx, "u_val", [P, SEQ])
        FH = sbuf(core, ctx, "f_high", [P, G, SEQ], F32R)
        FL = sbuf(core, ctx, "f_low", [P, G, SEQ], F32R)
        pU = [psum(core, ctx, f"pu{s}", [P, 2, HALF]) for s in range(2)]
        pD = psum(core, ctx, "pd", [P, 4, HALF])
        flat = lambda t: t[:, :, :].rearrange("p a b -> p (a b)")
        with nc.Block() as block:

            @block.sync
            def _(sp):
                for j in range(3):
                    sp.dma_start(taps[:, j, :], per_channel(io["ffn_conv_w"][0, j])).then_inc(sem("small"), 16)
                sp.dma_start(bias[:, :], per_channel(io["ffn_conv_b"][0])).then_inc(sem("small"), 16)
                def turn(i):
                    for j in range(G):
                        W.load(sp, 0, i * G + j, up[:, bass.ds((i * G + j) * P, P)])
                        W.load(sp, 1, i * G + j, up[:, bass.ds((i * G + j + FCH) * P, P)])
                        if j == 0:
                            V.load(sp, 0, i, down[bass.ds(i * (G * P), G * P), :])
                first_then_loop(sp, NG, turn)

            @block.gpsimd
            def _(pool):
                W.open_pool(pool)
                V.open_pool(pool)
                def turn(i):
                    for j in range(G):
                        W.split_low(pool, 0, i * G + j)
                        W.split_low(pool, 1, i * G + j)
                    V.split_low(pool, 0, i)
                first_then_loop(pool, NG, turn)

            @block.tensor
            def _(pe):
                W.open_pe(pe)
                V.open_pe(pe)

                def project(i, j, slot):
                    W.wait(pe, slot, i * G + j)
                    pe.wait_ge(sem(f"pu_free{slot}"), i * G + j + 1)
                    W.multiply(pe, slot, pU[slot], AH, AL)

                def output(i):
                    V.wait(pe, 0, i)
                    pe.wait_ge(sem("f_low"), i * G + G)
                    for q in range(2 * NB):
                        b, half = q // 2, q % 2
                        pe.wait_ge(sem("added"), i * 2 * NB + q + 1)
                        n = 0
                        for k in range(G):
                            for x, w in ((FH, V.high), (FL, V.high), (FH, V.low)):
                                last = pe.matmul(pD[:, q % 4, :], x[:, k, b * P:(b + 1) * P], w[0][:, k, half * HALF:(half + 1) * HALF],
                                                 start=(n == 0), stop=(n == 3 * G - 1))
                                n += 1
                        if q < 2 * NB - 1:
                            last.then_inc(sem("pd"), 1)
                    last.then_inc(V.s("used", 0), 1)

                def group(i, first):
                    project(i, 0, 0)
                    if not first:
                        output(i - 1)
                    project(i, 0, 1)
                    project(i, 1, 0)
                    project(i, 1, 1)

                group(0, True)
                with pe.Fori(1, NG) as i:
                    group(i, False)
                output(NG - 1)

            @block.scalar
            def _(act):
                act.wait_ge(sem("small"), 64)

                def group(i, more):
                    for j in range(G):
                        turn = i * G + j
                        for slot, U in ((0, UG), (1, UV)):
                            n = i * G + j + slot * FCH
                            act.wait_ge(W.s("used", slot), turn + 2)
                            act.wait_ge(sem(f"u_free{slot}"), turn + 1)
                            act.activation(U[:, :], flat(pU[slot]), ACT.Identity, scale=taps[:, 2, bass.ds(n, 1)],
                                           bias=bias[:, bass.ds(n, 1)]).then_inc(sem(f"tap2_{slot}"), 1)
                            if more or j < G - 1:
                                W.split_high(act, slot, turn + 1)
                            if slot == 0:
                                act.wait_ge(sem("pu_free0"), turn + 2)
                                act.activation(UG[:, :], UG[:, :], ACT.Gelu_apprx_tanh).then_inc(sem("gelu"), 1)
                        act.wait_ge(sem("product"), turn + 1)
                        act.wait_ge(V.s("used", 0), i + 1)
                        act.activation(FH[:, j, :], UV[:, :], ACT.Copy).then_inc(sem("f_high"), 1)
                        if j == 0:
                            V.split_high(act, 0, i)
                over_loop(act, NG, group)

            @block.vector
            def _(dve):
                for slot in range(2):
                    dve.sem_inc(sem(f"pu_free{slot}"), 1)
                    dve.sem_inc(sem(f"u_free{slot}"), 1)
                dve.sem_inc(sem("added"), 4)

                def add(i):
                    for q in range(2 * NB):
                        b, half = q // 2, q % 2
                        if q < 2 * NB - 1:
                            dve.wait_ge(sem("pd"), i * (2 * NB - 1) + q + 1)
                        else:
                            dve.wait_ge(V.s("used", 0), i + 2)
                        cols = slice(half * HALF, (half + 1) * HALF)
                        dve.tensor_tensor(X[:, b, cols], X[:, b, cols], pD[:, q % 4, :], ALU.add).then_inc(sem("added"), 1)

                def hidden(i, j, slot):
                    turn = i * G + j
                    U = (UG, UV)[slot]
                    n = i * G + j + slot * FCH
                    x = flat(pU[slot])
                    dve.wait_ge(sem(f"tap2_{slot}"), turn + 1)
                    dve.scalar_tensor_tensor(out=U[:, 1:], in0=x[:, :SEQ - 1], scalar=taps[:, 1, bass.ds(n, 1)], in1=U[:, 1:],
                                             op0=ALU.mult, op1=ALU.add).then_inc(sem(f"tap1_{slot}"), 1)
                    dve.wait_ge(sem(f"tap1_{slot}"), turn + 1)
                    dve.scalar_tensor_tensor(out=U[:, 2:], in0=x[:, :SEQ - 2], scalar=taps[:, 0, bass.ds(n, 1)], in1=U[:, 2:],
                                             op0=ALU.mult, op1=ALU.add).then_inc(sem(f"pu_free{slot}"), 1)
                    if slot == 1:
                        dve.wait_ge(sem("gelu"), turn + 1)
                        dve.wait_ge(sem("pu_free1"), turn + 2)
                        dve.tensor_tensor(UV[:, :], UV[:, :], UG[:, :], ALU.mult).then_inc(sem("product"), 1)
                        dve.wait_ge(sem("product"), turn + 1)
                        dve.sem_inc(sem("u_free0"), 1)
                        dve.wait_ge(sem("f_high"), turn + 1)
                        dve.tensor_tensor(FL[:, j, :], UV[:, :], FH[:, j, :].bitcast(F32), ALU.subtract).then_inc(sem("f_low"), 1)
                        dve.wait_ge(sem("f_low"), turn + 1)
                        dve.sem_inc(sem("u_free1"), 1)

                def group(i, first):
                    hidden(i, 0, 0)
                    if not first:
                        add(i - 1)
                    hidden(i, 0, 1)
                    hidden(i, 1, 0)
                    hidden(i, 1, 1)

                group(0, True)
                with dve.Fori(1, NG) as i:
                    group(i, False)
                add(NG - 1)


def stage_norm_time(core, X, gain, keep=None, residual=None, out=None):
    nc = core.nc
    with stage(core) as (ctx, sem):
        g = sbuf(core, ctx, "gain", [P, D])
        squares = sbuf(core, ctx, "squares", [P, 2, D])
        other = sbuf(core, ctx, "other", [P, NB, D]) if residual is not None else None
        stats = sbuf(core, ctx, "stats", [P, 3, NB])
        with nc.Block() as block:

            @block.sync
            def _(sp):
                sp.dma_start(g[:, :], gain.partition_broadcast(P)).then_inc(sem("gain"), 16)
                if residual is not None:
                    for b in range(NB):
                        sp.dma_start(other[:, b, :], residual[b * P:(b + 1) * P, :]).then_inc(sem(f"residual{b}"), 16)
                dst = keep if keep is not None else out
                for b in range(NB):
                    sp.wait_ge(sem("done"), b + 1)
                    sp.dma_start(dst[b * P:(b + 1) * P, :], X[:, b, :]).then_inc(sem("stored"), 16)
                sp.wait_ge(sem("stored"), 16 * NB)

            @block.scalar
            def _(act):
                for b in range(NB):
                    act.activation(squares[:, b % 2, :], X[:, b, :], ACT.Square, accum_out=stats[:, 0, b:b + 1]).then_inc(sem("squared"), 1)
                    act.wait_ge(sem("squared"), b + 1)
                    act.activation(stats[:, 1, b:b + 1], stats[:, 0, b:b + 1], ACT.Sqrt, scale=1.0 / D, bias=core.eps[:, 0:1]).then_inc(sem("root"), 1)

            @block.vector
            def _(dve):
                dve.wait_ge(sem("gain"), 16)
                for b in range(NB):
                    dve.wait_ge(sem("root"), b + 1)
                    dve.reciprocal(stats[:, 2, b:b + 1], stats[:, 1, b:b + 1]).then_inc(sem("rstd"), 1)
                    dve.wait_ge(sem("rstd"), b + 1)
                    dve.scalar_tensor_tensor(out=X[:, b, :], in0=X[:, b, :], scalar=stats[:, 2, b:b + 1], in1=g[:, :],
                                             op0=ALU.mult, op1=ALU.mult).then_inc(sem("done" if residual is None else "scaled"), 1)
                    if residual is not None:
                        dve.wait_ge(sem(f"residual{b}"), 16)
                        dve.wait_ge(sem("scaled"), b + 1)
                        dve.tensor_tensor(X[:, b, :], X[:, b, :], other[:, b, :], ALU.add).then_inc(sem("done"), 1)


def first_block(core):
    io, nc = core.io, core.nc
    w_in = io["w_in"][0]
    DQ, DK, DV, FQ, FK, FV = (2 * D + i * HALF for i in range(6))
    gate = lambda g: w_in[:, GATES_AT + g * D:GATES_AT + g * D + P]
    w_rnn, w_diff, w_fox, w_out = (io[n][0] for n in ("w_br_rnn", "w_br_diff", "w_br_fox", "w_out"))
    with ExitStack() as ctx:
        x0 = sbuf(core, ctx, "x0", [P, NB, D])
        stage_norm_to_channels(core, x0, io["norm1_g"][0], io["x"][0], ahead=columns(w_in, FOX_F_AT))
    core.M = nc.alloc_sbuf_tensor_at("m_top", [P, KD, SEQ], F32, offset=nc.sbuf_top - 4 * KD * SEQ)
    with ExitStack() as ctx:
        core.YH = sbuf(core, ctx, "y_high", [P, KD, SEQ], F32R)
        core.YL = sbuf(core, ctx, "y_low", [P, KD, SEQ], F32R)
        stage_attention_tables(core, columns(w_in, DQ, DK))
        stage_attention(core, "diff", DQ, DK, DV, 0, columns(w_in, FQ, FK))
        stage_attention(core, "fox", FQ, FK, FV, 4, [(0, gate(1)), (1, w_diff[:, 0:P])])
        stage_branches(core, [(1, w_diff, 4, 0), (2, w_fox, 4, 4)], columns(w_in, 0, D), part_out=core.m_part)
        stage_rnn(core, [(0, gate(0)), (1, w_rnn[:, 0:P])])
        stage_branches(core, [(0, w_rnn, KD, 0)], list(enumerate(rows_tiles(w_out, KD)[:2])), part_in=core.m_part)
    with ExitStack() as ctx:
        X = sbuf(core, ctx, "x", [P, NB, D])
        stage_rows(core, core.AH, core.AL, KD, w_out, X, whole=core.M, load_acc=io["x"][0])
        stage_norm_to_channels(core, X, io["norm2_g"][0], ahead=columns(io["ffn_up"][0], 0, D_FF))
        stage_ffn(core, X)
        stage_norm_time(core, X, io["final_g"], keep=core.x_mid)
        stage_norm_to_channels(core, X, io["pre_norm_w_2"][0], ahead=columns(io["w_in_2"][0], U_AT, U_AT + P))


Z_AT, XBC_AT, DT_AT = 0, 1024, 2560
Q_AT, F_AT, I_AT, G_AT = 2576, 3088, 3600, 4112
U_AT, S5G_AT = 4624, 5136
SSD_H = 16
GH = 8
SSD_CH = 12


class Overlay:

    def __init__(self, core, start, size):
        self.core, self.at, self.end = core, (start + 31) // 32 * 32, start + size

    def take(self, name, shape, dtype=F32):
        size = 4 * int(np.prod(shape[1:]))
        size = (size + 31) // 32 * 32
        assert self.at + size <= self.end, name
        self.core.serial += 1
        t = self.core.nc.alloc_sbuf_tensor_at(f"{name}_{self.core.serial}", shape, dtype, offset=self.at)
        self.at += size
        return t


def flat2(t):
    return t[:, :, :].rearrange("p a b -> p (a b)")


def stage_ssd_project(core, XBC, ZT, dtN, acN):
    nc, io = core.nc, core.io
    w_in = io["w_in_2"][0]
    AH, AL = core.AH, core.AL
    with stage(core) as (ctx, sem):
        W = WeightTiles(core, ctx, sem, KD)
        taps = sbuf(core, ctx, "taps", [P, 4, SSD_CH])
        bias = sbuf(core, ctx, "bias", [P, SSD_CH])
        vec = sbuf(core, ctx, "dt_bias_a", [P, 3, SSD_H])
        z = sbuf(core, ctx, "z_dt", [P, NB * SSD_H])
        before = sbuf(core, ctx, "before", [P, P])
        acR = sbuf(core, ctx, "acum_rows", [P, P])
        soft = Softplus(core, ctx, sem, "sp", [P, NB * SSD_H])
        pU = [psum(core, ctx, f"pu{s}", [P, 2, HALF]) for s in range(2)]
        pD = psum(core, ctx, "pd", [P, NB, SSD_H])
        pN = psum(core, ctx, "pn", [P, NB, SSD_H])
        pR = psum(core, ctx, "pr", [P, P])
        dt_rows = ZT[0:SSD_H, KD - 1, :]
        TAIL = SSD_CH - KD
        flat_dt = lambda t: t[:, :, :].rearrange("p c h -> p (c h)")

        def tail(j):
            return j % 2, KD + j // 2 + j % 2

        with nc.Block() as block:

            @block.sync
            def _(sp):
                sp.dma_start(vec[:, 0, :], io["ssd_dt_bias_2"][0].partition_broadcast(P)).then_inc(sem("vec"), 16)
                sp.dma_start(vec[:, 1, :], io["ssd_a_log_2"][0].partition_broadcast(P)).then_inc(sem("vec"), 16)
                for j in range(4):
                    sp.dma_start(taps[:, j, :], per_channel(io["ssd_conv_w_2"][0, j])).then_inc(sem("small"), 16)
                sp.dma_start(bias[:, :], per_channel(io["ssd_conv_b_2"][0])).then_inc(sem("small"), 16)
                def turn(n):
                    W.load(sp, 0, n, w_in[:, bass.ds(n * P + XBC_AT, P)])
                    W.load(sp, 1, n + 1, w_in[:, bass.ds(n * P + Z_AT, P)])
                first_then_loop(sp, KD, turn)
                for j in range(TAIL):
                    at = XBC_AT + (KD + j) * P
                    W.load(sp, *tail(j), w_in[:, at:at + P])
                sp.wait_ge(sem("acum_rows"), 1)
                sp.dma_start(core.acum.rearrange("c h t -> (c h) t"), acR[:, :]).then_inc(sem("stored"), 16)
                sp.wait_ge(sem("stored"), 16)

            @block.gpsimd
            def _(pool):
                W.open_pool(pool)
                pool.memset(before[:, :], 1.0).then_inc(sem("before0"), 1)
                pool.wait_ge(sem("before0"), 1)
                pool.affine_select(out=before[:, :], in_=before[:, :], compare_op=ALU.is_ge, fill=0.0, base=0,
                                   pattern=[[1, P]], channel_multiplier=-1).then_inc(sem("before"), 1)
                def turn(n):
                    W.split_low(pool, 0, n)
                    W.split_low(pool, 1, n + 1)
                first_then_loop(pool, KD, turn)
                for j in range(TAIL):
                    W.split_low(pool, *tail(j))

            @block.tensor
            def _(pe):
                W.open_pe(pe)
                W.wait(pe, 1, 0)
                W.multiply(pe, 1, pU[1], AH, AL)

                def project(s, turn, n):
                    W.wait(pe, s, turn)
                    pe.wait_ge(sem(f"pu_free{s}"), n + 1)
                    W.multiply(pe, s, pU[s], AH, AL)

                pe.wait_ge(sem("dt_rows"), 1)
                for c in range(NB):
                    last = pe.transpose(pD[:, c, :], dt_rows[:, c * P:(c + 1) * P], core.ident[0:SSD_H, 0:SSD_H])
                last.then_inc(sem("dt_turned"), 1)
                with pe.Fori(0, KD) as n:
                    project(0, n, n)
                    project(1, n + 1, n)
                pe.wait_ge(sem("before"), 1)
                pe.wait_ge(sem("dta"), 1)
                pe.matmul(flat_dt(pN), before[:, :], z[:, :], start=True, stop=True).then_inc(sem("cumulated"), 1)
                project(*tail(0), KD)
                pe.wait_ge(sem("acn"), 1)
                pe.transpose(pR[:, :], flat_dt(acN), core.ident[:, :]).then_inc(sem("rows"), 1)
                for j in range(1, TAIL):
                    project(*tail(j), KD + j // 2)

            @block.scalar
            def _(act):
                act.wait_ge(sem("vec"), 32)
                act.activation(vec[:, 2, :], vec[:, 1, :], ACT.Exp).then_inc(sem("ea"), 1)
                W.split_high(act, 1, 1)
                act.wait_ge(sem("z"), 1)
                soft.on_act(act, z[:, :])
                act.wait_ge(sem("small"), 80)

                def conv(s, turn, n, more):
                    tile = XBC[:, bass.ds(n, 1), :].squeeze(1)
                    act.wait_ge(W.s("used", s), turn + 2)
                    act.activation(tile, flat2(pU[s]), ACT.Identity, scale=taps[:, 3, bass.ds(n, 1)],
                                   bias=bias[:, bass.ds(n, 1)]).then_inc(sem("tap3"), 1)
                    if more:
                        W.split_high(act, s, turn + 1)

                def silu(n):
                    tile = XBC[:, bass.ds(n, 1), :].squeeze(1)
                    act.wait_ge(sem("conv"), n + 1)
                    act.sem_inc(sem("act_asked"), 1)
                    act.activation(tile, tile, ACT.Silu).then_inc(sem("silu"), 1)

                with act.Fori(0, KD) as n:
                    conv(0, n, n, True)
                    act.wait_ge(W.s("used", 1), n + 3)
                    act.activation(ZT[:, bass.ds(n, 1), :].squeeze(1), flat2(pU[1]), ACT.Silu).then_inc(sem("z_out"), 1)
                    W.split_high(act, 1, n + 2)
                    silu(n)
                for j in range(TAIL):
                    conv(*tail(j), KD + j, j < TAIL - 2)
                    silu(KD + j)

            @block.vector
            def _(dve):
                dve.sem_inc(sem("pu_free0"), 1)
                dve.wait_ge(W.s("used", 1), 2)
                dve.tensor_copy(dt_rows, pU[1][0:SSD_H, :, :].rearrange("p a b -> p (a b)")).then_inc(sem("dt_rows"), 1)
                dve.wait_ge(sem("dt_rows"), 1)
                dve.sem_inc(sem("pu_free1"), 1)
                over_chunks = lambda v: v.unsqueeze(1).to_broadcast([P, NB, SSD_H])
                zc = z[:, :].rearrange("p (c h) -> p c h", h=SSD_H)
                dve.wait_ge(sem("vec"), 32)
                dve.wait_ge(sem("dt_turned"), 1)
                dve.tensor_tensor(zc, pD[:, :, :], over_chunks(vec[:, 0, :]), ALU.add).then_inc(sem("z"), 1)
                dve.wait_ge(sem("z"), 1)
                soft.on_dve(dve, z[:, :], flat_dt(dtN))
                dve.wait_ge(sem("ea"), 1)
                dve.tensor_scalar(vec[:, 2, :], vec[:, 2, :], -1.0, None, ALU.mult).then_inc(sem("a"), 1)
                dve.wait_ge(sem("a"), 1)
                dve.wait_ge(soft.s("out"), 1)
                dve.tensor_tensor(zc, dtN[:, :, :], over_chunks(vec[:, 2, :]), ALU.mult).then_inc(sem("dta"), 1)

                def conv(s, n):
                    tile, x = XBC[:, bass.ds(n, 1), :].squeeze(1), flat2(pU[s])
                    dve.wait_ge(sem("tap3"), n + 1)
                    for back in (1, 2, 3):
                        ins = dve.scalar_tensor_tensor(out=tile[:, back:], in0=x[:, :SEQ - back], scalar=taps[:, 3 - back, bass.ds(n, 1)],
                                                       in1=tile[:, back:], op0=ALU.mult, op1=ALU.add)
                        if back < 3:
                            ins.then_inc(sem("taps"), 1)
                            dve.wait_ge(sem("taps"), n * 2 + back)
                    ins.then_inc(sem("conv"), 1)
                    dve.wait_ge(sem("conv"), n + 1)
                    dve.sem_inc(sem(f"pu_free{s}"), 1)

                with dve.Fori(0, KD) as n:
                    conv(0, n)
                    dve.wait_ge(sem("z_out"), n + 1)
                    dve.sem_inc(sem("pu_free1"), 1)
                dve.wait_ge(sem("cumulated"), 1)
                dve.tensor_copy(acN[:, :, :], pN[:, :, :]).then_inc(sem("acn"), 1)
                for j in range(TAIL):
                    conv(j % 2, KD + j)
                    if j == 0:
                        dve.wait_ge(sem("rows"), 1)
                        dve.tensor_copy(acR[:, :], pR[:, :]).then_inc(sem("acum_rows"), 1)


def stage_ssd_chunks(core, XBC, ZT, dtN, acN, ahead):
    nc, io = core.nc, core.io
    with stage(core) as (ctx, sem):
        nxt = Ahead(core, sem, ahead)
        lay = Overlay(core, core.act_at, 2 * 4 * KD * SEQ)
        two = range(2)
        acB = [lay.take(f"acum_rows{s}", [P, GH, P]) for s in two]
        E = [lay.take(f"decay{s}", [P, GH, P]) for s in two]
        XS = [lay.take(f"x_chunk{s}", [P, 4, P]) for s in two]
        BS = [lay.take(f"b_chunk{s}", [P, P]) for s in two]
        CS = [lay.take(f"c_chunk{s}", [P, P]) for s in two]
        XD = [lay.take(f"x_skip{s}", [P, 4, P]) for s in two]
        xdt = [lay.take(f"x_dt{s}", [P, GH, 64]) for s in two]
        xde = [lay.take(f"x_dt_end{s}", [P, GH, 64]) for s in two]
        BN = [lay.take(f"b_time{s}", [P, P]) for s in two]
        small = [lay.take(f"small{s}", [P, 4, GH]) for s in two]
        Y = [lay.take(f"y{s}", [P, GH, 64]) for s in two]
        T = [lay.take(f"y_skip{s}", [P, 4, P]) for s in two]
        ST = lay.take("state", [P, GH, 64])
        skip = lay.take("skip", [P, KD])
        pX = psum(core, ctx, "px", [P, 4, P])
        pB = psum(core, ctx, "pb", [P, P])
        pC = psum(core, ctx, "pc", [P, P])
        pYD = psum(core, ctx, "pyd", [P, GH, 64])
        pYO = psum(core, ctx, "pyo", [P, GH, 64])
        pS = psum(core, ctx, "pst", [P, GH, 64])
        pT = [psum(core, ctx, f"pty{s}", [P, 4, P]) for s in two]

        def loops(engine, prepare, finish=None, before=None, late=None):
            for g in range(2):
                if before is not None:
                    before(g)

                def at(body, pair, c):
                    if body is not None:
                        body(g, pair * 2 + c, pair * 2 + (c + g * NB), c % 2, pair + (c // 2 + g * (NB // 2)))

                at(prepare, 0, 0)
                at(late, 0, 0)
                with engine.Fori(0, NB // 2 - 1) as pair:
                    for c in two:
                        at(prepare, pair, c + 1)
                        at(finish, pair, c)
                        at(late, pair, c + 1)
                at(prepare, NB // 2 - 1, 1)
                at(finish, NB // 2 - 1, 0)
                at(late, NB // 2 - 1, 1)
                at(finish, NB // 2 - 1, 1)

        with nc.Block() as block:

            @block.sync
            def _(sp):
                nxt.load(sp)
                for k in range(KD):
                    for j in range(2):
                        sp.dma_start(skip[j * 64:(j + 1) * 64, k:k + 1], io["ssd_d_2"][0, 2 * k + j:2 * k + j + 1].partition_broadcast(64)).then_inc(sem("skip"), 16)

                def prepare(g, c, it, s, turn):
                    sp.wait_ge(sem("seg"), it + 1)
                    sp.wait_ge(sem("small"), it + 1)
                    src = core.acum[bass.ds(c, 1), g * GH:(g + 1) * GH, :].squeeze(0)
                    sp.sem_inc(sem("asked"), 1)
                    sp.dma_start(acB[s][:, :, :], src.partition_broadcast(P)).then_inc(sem(f"rows{s}"), 16)
                loops(sp, prepare)

            @block.gpsimd
            def _(pool):
                pool.wait_ge(sem("skip"), 16 * 2 * KD)
                fill = pool.to_reg(NEG)
                pool.sem_inc(sem("xd"), 2)
                pool.sem_inc(sem("gated"), 2)

                def prepare(g, c, it, s, turn):
                    pool.wait_ge(sem("skipped"), it + 1)
                    pool.wait_ge(sem("xs"), it + 1)
                    pool.tensor_tensor(XD[s][:, :, :], XS[s][:, :, :], skip[:, g * 4:(g + 1) * 4].unsqueeze(2).to_broadcast([P, 4, P]),
                                       ALU.mult).then_inc(sem("xd"), 1)
                    pool.wait_ge(sem("seg"), it + 3)
                    pool.sem_inc(sem("pool_asked"), 1)
                    pool.affine_select(out=E[s][:, :, :], in_=E[s][:, :, :], compare_op=ALU.is_ge, fill=fill, base=0,
                                       pattern=[[0, GH], [1, P]], channel_multiplier=-1).then_inc(sem("masked"), 1)
                    pool.wait_ge(sem("x_dt"), it + 2)
                    pool.wait_ge(sem("dte"), it + 1)
                    pool.wait_ge(sem("pst"), it + 1)
                    pool.tensor_tensor(xde[s][:, :, :], xdt[s][:, :, :], small[s][:, 1, :].unsqueeze(2).to_broadcast([P, GH, 64]),
                                       ALU.mult).then_inc(sem("x_dte"), 1)

                def finish(g, c, it, s, turn):
                    zt = ZT[:, g * 4:(g + 1) * 4, bass.ds(c * P, P)]
                    pool.wait_ge(sem("skipped"), it + 3)
                    pool.sem_inc(sem("pool_asked"), 1)
                    pool.tensor_tensor(zt, zt, T[s][:, :, :], ALU.mult).then_inc(sem("gated"), 1)
                loops(pool, prepare, finish, lambda g: nxt.split_low(pool, g))

            @block.scalar
            def _(act):
                act.sem_inc(sem("small"), 2)

                def prepare(g, c, it, s, turn):
                    steps = bass.ds(c * P, P)
                    act.wait_ge(sem("scores"), it + 1)
                    act.wait_ge(sem("xd"), it + 1)
                    act.sem_inc(sem("act_asked"), 1)
                    act.activation(XS[s][:, :, :], XBC[:, g * 4:(g + 1) * 4, steps], ACT.Copy).then_inc(sem("xs"), 1)
                    act.activation(BS[s][:, :], XBC[:, KD + g, steps], ACT.Copy).then_inc(sem("bs"), 1)
                    act.wait_ge(sem("pyo"), it + 1)
                    act.sem_inc(sem("act_asked"), 1)
                    act.activation(CS[s][:, :], XBC[:, KD + 2 + g, steps], ACT.Copy).then_inc(sem("cs"), 1)
                    act.wait_ge(sem(f"rows{s}"), turn * 16 + 16)
                    act.wait_ge(sem("state"), it + 1)
                    act.sem_inc(sem("act_asked"), 1)
                    act.activation(small[s][:, 2, :], acN[:, bass.ds(c, 1), g * GH:(g + 1) * GH].squeeze(1), ACT.Exp).then_inc(sem("ea"), 1)
                    act.activation(small[s][:, 3, :], acB[s][:, :, P - 1], ACT.Exp).then_inc(sem("small"), 1)
                    act.wait_ge(sem("to_end"), it + 1)
                    act.activation(small[s][:, 1, :], small[s][:, 0, :], ACT.Exp).then_inc(sem("dte"), 1)
                    act.wait_ge(sem("masked"), it + 1)
                    act.activation(E[s][:, :, :], E[s][:, :, :], ACT.Exp).then_inc(sem("decay"), 1)
                    act.wait_ge(sem("b_turned"), it + 1)
                    act.activation(BN[s][:, :], pB[:, :], ACT.Copy).then_inc(sem("bn"), 1)
                loops(act, prepare, None, lambda g: nxt.split_high(act, g))

            @block.tensor
            def _(pe):
                ident = core.ident
                pe.sem_inc(sem("y_turned"), 2)
                pe.sem_inc(sem("ydiag"), 2)
                pe.sem_inc(sem("scores"), 2)
                pe.sem_inc(sem("pyo"), 2)
                pe.sem_inc(sem("pst"), 2)

                def prepare(g, c, it, s, turn):
                    pe.wait_ge(sem("xs"), it + 1)
                    pe.wait_ge(sem("cs"), it + 1)
                    pe.wait_ge(sem("bs"), it + 1)
                    pe.wait_ge(sem("x_dt"), it + 1)
                    for j in range(4):
                        last = pe.transpose(pX[:, j, :], XS[s][:, j, :], ident[:, :])
                    last.then_inc(sem("x_turned"), 1)
                    pe.wait_ge(sem("bn"), it + 1)
                    pe.wait_ge(sem("mt"), it + 1)
                    pe.transpose(pB[:, :], BS[s][:, :], ident[:, :]).then_inc(sem("b_turned"), 1)
                    pe.matmul(pC[:, :], BS[s][:, :], CS[s][:, :], start=True, stop=True).then_inc(sem("scores"), 1)

                def finish(g, c, it, s, turn):
                    pe.wait_ge(sem("state"), it + 2)
                    pe.wait_ge(sem("y_off"), it + 1)
                    pe.matmul(pYO[:, :, :].rearrange("p a b -> p (a b)"), CS[s][:, :], ST[:, :, :].rearrange("p a b -> p (a b)"), start=True, stop=True).then_inc(sem("pyo"), 1)
                    pe.wait_ge(sem("bn"), it + 2)
                    pe.wait_ge(sem("x_dte"), it + 1)
                    pe.matmul(pS[:, :, :].rearrange("p a b -> p (a b)"), BN[s][:, :], xde[s][:, :, :].rearrange("p a b -> p (a b)"), start=True, stop=True).then_inc(sem("pst"), 1)
                    pe.wait_ge(sem("mt"), it + 2)
                    pe.wait_ge(sem("y"), it + 2)
                    for h in range(GH):
                        last = pe.matmul(pYD[:, h, :], E[s][:, h, :], xdt[s][:, h, :], start=True, stop=True)
                    last.then_inc(sem("ydiag"), 1)
                    pe.wait_ge(sem("y"), it + 3)
                    pe.wait_ge(sem("skipped"), it + 1)
                    yv = Y[s][:, :, :].rearrange("p (j a) b -> p j (a b)", j=4)
                    for j in range(4):
                        last = pe.transpose(pT[s][:, j, :], yv[:, j, :], ident[:, :])
                    last.then_inc(sem("y_turned"), 1)
                loops(pe, prepare, finish, lambda g: pe.wait_ge(sem("cleared"), g + 1))

            @block.vector
            def _(dve):
                for name, n in (("seg", 2), ("skipped", 2), ("state", 2), ("x_dt", 1), ("mt", 1), ("y_off", 1), ("y", 2)):
                    dve.sem_inc(sem(name), n)
                dve.sem_inc(sem("bn"), 1)
                wide = lambda t: t.unsqueeze(2).to_broadcast([P, GH, 64])

                def prepare(g, c, it, s, turn):
                    heads = slice(g * GH, (g + 1) * GH)
                    ac_c = acN[:, bass.ds(c, 1), heads].squeeze(1)
                    dve.wait_ge(sem(f"rows{s}"), turn * 16 + 16)
                    dve.wait_ge(sem("ydiag"), it + 1)
                    dve.tensor_tensor(small[s][:, 0, :], acB[s][:, :, P - 1], ac_c, ALU.subtract).then_inc(sem("to_end"), 1)
                    dve.tensor_tensor(E[s][:, :, :], acB[s][:, :, :], ac_c.unsqueeze(2).to_broadcast([P, GH, P]), ALU.subtract).then_inc(sem("seg"), 1)
                    dve.wait_ge(sem("x_turned"), it + 1)
                    dve.tensor_tensor(xdt[s][:, :, :], pX[:, :, :].rearrange("p a b -> p (a b)").rearrange("p (h d) -> p h d", d=64),
                                      wide(dtN[:, bass.ds(c, 1), heads].squeeze(1)), ALU.mult).then_inc(sem("x_dt"), 1)

                def decays(g, c, it, s, turn):
                    dve.wait_ge(sem("decay"), it + 1)
                    dve.wait_ge(sem("scores"), it + 3)
                    dve.tensor_tensor(E[s][:, :, :], E[s][:, :, :], pC[:, :].unsqueeze(1).to_broadcast([P, GH, P]), ALU.mult).then_inc(sem("mt"), 1)

                def finish(g, c, it, s, turn):
                    dve.wait_ge(sem("ea"), it + 1)
                    dve.wait_ge(sem("pyo"), it + 3)
                    dve.tensor_tensor(Y[s][:, :, :], pYO[:, :, :], wide(small[s][:, 2, :]), ALU.mult).then_inc(sem("y_off"), 1)
                    dve.wait_ge(sem("small"), it + 3)
                    dve.tensor_tensor(ST[:, :, :], ST[:, :, :], wide(small[s][:, 3, :]), ALU.mult).then_inc(sem("decayed"), 1)
                    dve.wait_ge(sem("decayed"), it + 1)
                    dve.wait_ge(sem("pst"), it + 3)
                    dve.tensor_tensor(ST[:, :, :], ST[:, :, :], pS[:, :, :], ALU.add).then_inc(sem("state"), 1)
                    dve.wait_ge(sem("y_off"), it + 2)
                    dve.wait_ge(sem("ydiag"), it + 3)
                    dve.tensor_tensor(Y[s][:, :, :], Y[s][:, :, :], pYD[:, :, :], ALU.add).then_inc(sem("y"), 1)
                    dve.wait_ge(sem("y_turned"), it + 3)
                    dve.wait_ge(sem("gated"), it + 1)
                    dve.wait_ge(sem("xd"), it + 3)
                    dve.tensor_tensor(T[s][:, :, :], pT[s][:, :, :], XD[s][:, :, :], ALU.add).then_inc(sem("skipped"), 1)

                def clear(g):
                    if g:
                        dve.wait_ge(sem("state"), NB * g + 2)
                        dve.wait_ge(sem("pyo"), NB * g + 2)
                    dve.memset(ST[:, :, :], 0.0).then_inc(sem("cleared"), 1)
                    dve.wait_ge(sem("cleared"), g + 1)
                loops(dve, prepare, finish, clear, decays)


def stage_mix_rows(core, src, chunks, per_group, gain, high, low, w, acc, ahead=(), factor=None, add=True):
    nc = core.nc
    NG = chunks // per_group
    KT = ROWS_K
    NK = chunks // KT
    tiles = [(half, kt) for half in range(2) for kt in range(NK)]
    with stage(core) as (ctx, sem):
        W = WeightTiles(core, ctx, sem, KT, HALF)
        nxt = Ahead(core, sem, ahead, W, (NK, NK))
        sq = [sbuf(core, ctx, f"sq{s}", [P, SEQ]) for s in range(2)]
        diag = sbuf(core, ctx, "diag", [P, NB, P])
        gains = sbuf(core, ctx, "gains", [P, chunks])
        stats = sbuf(core, ctx, "stats", [P, 3, NG, NB])
        out = psum(core, ctx, "rows", [P, NB, HALF])
        sums = out[:, 0, 0:chunks * NB].rearrange("p (k b) -> p k b", b=NB)
        spread = [out[:, 2 * s + 4:2 * s + 6, :] for s in range(2)]

        with nc.Block() as block:

            @block.sync
            def _(sp):
                sp.dma_start(gains[:, :], per_channel(gain)).then_inc(sem("gains"), 16)
                for t, (half, kt) in enumerate(tiles):
                    W.load(sp, t % 2, t // 2, rows_tiles(w, chunks)[t])
                nxt.load(sp)

            @block.gpsimd
            def _(pool):
                W.open_pool(pool)
                for k in range(1, chunks, 2):
                    pool.wait_ge(sem("high"), k + 1)
                    pool.tensor_tensor(low[:, k, :], src[:, k, :], high[:, k, :].bitcast(F32), ALU.subtract).then_inc(sem("low1"), 1)
                for t in range(len(tiles)):
                    W.split_low(pool, t % 2, t // 2)
                nxt.split_low(pool)

            @block.tensor
            def _(pe):
                W.open_pe(pe)
                for k in range(chunks):
                    pe.wait_ge(sem(f"squared{k % 2}"), k // 2 + 1)
                    for b in range(NB):
                        last = pe.matmul(sums[:, k, b:b + 1], sq[k % 2][:, b * P:(b + 1) * P], core.ones[:, 0:1], start=True, stop=True)
                    last.then_inc(sem("summed"), 1)
                for g in range(NG):
                    pe.wait_ge(sem("diag"), g + 1)
                    if g >= 2:
                        pe.wait_ge(sem("scaled"), (g - 1) * per_group)
                    for h in range(2):
                        last = pe.matmul(spread[g % 2][:, h, :], core.ones[:, :], flat2(diag)[:, h * HALF:(h + 1) * HALF], start=True, stop=True)
                    last.then_inc(sem("spread"), 1)
                for t, (half, kt) in enumerate(tiles):
                    W.wait(pe, t % 2, t // 2)
                    for b in range(NB):
                        if half and kt == 0:
                            pe.wait_ge(sem("added"), b + 1)
                        if t == 0 and b == 4:
                            pe.wait_ge(sem("scaled"), chunks)
                        for k in range(KT):
                            kk = kt * KT + k
                            if b == 0 and half == 0:
                                pe.wait_ge(sem(f"low{kk % 2}"), kk // 2 + 1)
                            for i, (x, v) in enumerate(((high, W.high), (low, W.high), (high, W.low))):
                                last = pe.matmul(out[:, b, :], x[:, kk, b * P:(b + 1) * P], v[t % 2][:, k, :],
                                                 start=(kk == 0 and i == 0), stop=(kk == chunks - 1 and i == 2))
                        if kt == NK - 1 and b < NB - 1:
                            last.then_inc(sem("out"), 1)
                    last.then_inc(W.s("used", t % 2), 1)

            @block.scalar
            def _(act):
                for k in range(0, chunks, 2):
                    if k:
                        act.wait_ge(sem("summed"), k - 1)
                    act.activation(sq[0][:, :], src[:, k, :], ACT.Square).then_inc(sem("squared0"), 1)
                act.wait_ge(sem("total"), NG)
                act.activation(stats[:, 1, :, :], stats[:, 0, :, :], ACT.Sqrt, scale=1.0 / (per_group * P),
                               bias=core.eps[:, 0:1]).then_inc(sem("root"), 1)
                for k in range(chunks):
                    act.wait_ge(sem("result"), k + 1)
                    act.activation(high[:, k, :], src[:, k, :], ACT.Copy).then_inc(sem("high"), 1)
                for t in range(len(tiles)):
                    W.split_high(act, t % 2, t // 2)
                nxt.split_high(act)

            @block.vector
            def _(dve):
                for k in range(1, chunks, 2):
                    if k > 1:
                        dve.wait_ge(sem("summed"), k - 1)
                    dve.tensor_tensor(sq[1][:, :], src[:, k, :], src[:, k, :], ALU.mult).then_inc(sem("squared1"), 1)
                dve.wait_ge(sem("summed"), chunks)
                for g in range(NG):
                    dve.tensor_reduce(stats[:, 0, g, :], sums[:, g * per_group:(g + 1) * per_group, :].rearrange("p k b -> p b k"),
                                      AX.X, ALU.add).then_inc(sem("total"), 1)
                dve.wait_ge(sem("root"), 1)
                dve.reciprocal(stats[:, 2, :, :], stats[:, 1, :, :]).then_inc(sem("rstd"), 1)
                dve.wait_ge(sem("rstd"), 1)
                dve.wait_ge(sem("gains"), 16)

                def spread_out(g):
                    if g:
                        dve.wait_ge(sem("spread"), g)
                    dve.tensor_tensor(diag[:, :, :], core.ident[:, :].unsqueeze(1).to_broadcast([P, NB, P]),
                                      stats[:, 2, g, :].unsqueeze(2).to_broadcast([P, NB, P]), ALU.mult).then_inc(sem("diag"), 1)

                def split_low(k):
                    if k % 2 == 0:
                        dve.wait_ge(sem("high"), k + 1)
                        dve.tensor_tensor(low[:, k, :], src[:, k, :], high[:, k, :].bitcast(F32), ALU.subtract).then_inc(sem("low0"), 1)

                spread_out(0)
                for k in range(chunks):
                    g = k // per_group
                    if k % per_group == 0:
                        if g + 1 < NG:
                            spread_out(g + 1)
                        dve.wait_ge(sem("spread"), g + 1)
                    dve.scalar_tensor_tensor(out=src[:, k, :], in0=src[:, k, :], scalar=gains[:, k:k + 1], in1=flat2(spread[g % 2]),
                                             op0=ALU.mult, op1=ALU.mult).then_inc(sem("scaled"), 1)
                    dve.wait_ge(sem("scaled"), k + 1)
                    if factor is not None:
                        dve.tensor_tensor(src[:, k, :], src[:, k, :], factor[:, k, :], ALU.mult).then_inc(sem("result"), 1)
                    else:
                        dve.sem_inc(sem("result"), 1)
                    if k:
                        split_low(k - 1)
                split_low(chunks - 1)
                for half in range(2):
                    cols = slice(half * HALF, (half + 1) * HALF)
                    for b in range(NB):
                        t = half * NK + NK - 1
                        if b < NB - 1:
                            dve.wait_ge(sem("out"), half * (NB - 1) + b + 1)
                        else:
                            dve.wait_ge(W.s("used", t % 2), t // 2 + 2)
                        if add:
                            dve.tensor_tensor(acc[:, b, cols], acc[:, b, cols], out[:, b, :], ALU.add).then_inc(sem("added"), 1)
                        else:
                            dve.tensor_copy(acc[:, b, cols], out[:, b, :]).then_inc(sem("added"), 1)


HG_H = 4
LEVELS = 7


def level_masks():
    s, l = np.arange(P)[:, None], np.arange(P)[None, :]
    out = [s == l]
    for v in range(LEVELS):
        m = 1 << v
        out.append((s // (2 * m) == l // (2 * m)) & (s % (2 * m) < m) & (l % (2 * m) >= m))
    return np.ascontiguousarray(np.stack(out, 1).astype(np.int32))


def stage_hgrn(core, O, SG, ahead):
    nc, io = core.nc, core.io
    w_in = io["w_in_2"][0]
    with stage(core) as (ctx, sem):
        W = WeightTiles(core, ctx, sem, KD)
        nxt = Ahead(core, sem, ahead, W, (2 * HG_H, 2 * HG_H))
        Qt, Kt, CU, VT, A, TF = (sbuf(core, ctx, n, [P, SEQ]) for n in ("q", "k", "cum", "vt", "attn", "tf"))
        Dc = [sbuf(core, ctx, f"d{s}", [P, SEQ]) for s in range(2)]
        X = [sbuf(core, ctx, f"x{s}", [P, SEQ]) for s in range(2)]
        V = sbuf(core, ctx, "v", [P, NB, P])
        keep = sbuf(core, ctx, "keep", [P, SEQ])
        masks = sbuf(core, ctx, "masks", [P, LEVELS + 1, P], I32)
        blank = sbuf(core, ctx, "blank", [1, LEVELS + 1])
        el = sbuf(core, ctx, "el", [P, NB])
        pp = [psum(core, ctx, f"pp{s}", [P, 2, HALF]) for s in range(4)]
        KE, KN, ST = VT, VT, TF
        blocks = lambda t: t[:, :].rearrange("p (c t) -> p c t", t=P)
        pblocks = lambda t: flat2(t).rearrange("p (c t) -> p c t", t=P)
        NL = LEVELS + 1

        def halves(t, v):
            m = 1 << v
            r = t[:, :].rearrange("p (n two m) -> p n two m", two=2, m=m)
            return r[:, :, 0, :], r[:, :, 1, :]

        def middle(v):
            m = 1 << v
            r = CU[:, :].rearrange("p (n two m) -> p n two m", two=2, m=m)
            return r[:, :, 0, m - 1:m].to_broadcast([P, SEQ // (2 * m), m])

        with nc.Block() as block:

            @block.sync
            def _(sp):
                sp.dma_start(masks[:, :, :], io["level_masks"]).then_inc(sem("masks"), 16)
                def turn(h):
                    for j, at in enumerate((F_AT, Q_AT, I_AT, G_AT)):
                        W.load(sp, j % 2, h * 2 + j // 2, w_in[:, bass.ds(h * P + at, P)])
                first_then_loop(sp, HG_H, turn)
                nxt.load(sp)

            @block.gpsimd
            def _(pool):
                W.open_pool(pool)
                pool.memset(keep[:, :], 1.0).then_inc(sem("keep0"), 1)
                pool.wait_ge(sem("keep0"), 1)
                pool.memset(blocks(keep)[:, :, 0:1], 0.0).then_inc(sem("keep"), 1)
                pool.memset(A[:, :], 0.0).then_inc(sem("keep"), 1)
                def turn(h):
                    for j in range(4):
                        W.split_low(pool, j % 2, h * 2 + j // 2)
                    for v in range(LEVELS):
                        s = v % 2
                        pool.wait_ge(sem("level_exp"), h * LEVELS + v + 1)
                        pool.wait_ge(sem("level_done"), h * NL + v + 2)
                        pool.tensor_tensor(halves(X[s], v)[0], halves(Kt, v)[0], halves(Dc[s], v)[0], ALU.mult).then_inc(sem("left"), 1)
                first_then_loop(pool, HG_H, turn)
                nxt.split_low(pool)

            @block.tensor
            def _(pe):
                W.open_pe(pe)
                pe.sem_inc(sem("level_done"), 2)
                ident = core.ident
                with pe.Fori(0, HG_H) as h:
                    for j in range(4):
                        s, turn = j % 2, h * 2 + j // 2
                        W.wait(pe, s, turn)
                        pe.wait_ge(sem("banks_free"), h + 1)
                        W.multiply(pe, s, pp[j], core.AH, core.AL)
                    pe.wait_ge(sem("vt"), h + 1)
                    pe.wait_ge(sem("lf"), h + 1)
                    pe.wait_ge(sem("k"), h + 1)
                    for c in range(NB):
                        last = pe.transpose(pblocks(pp[0])[:, c, :], blocks(VT)[:, c, :], ident[:, :])
                    last.then_inc(sem("v_turned"), 1)
                    pe.wait_ge(sem("q"), h + 1)
                    for c in range(NB):
                        last = pe.matmul(pblocks(pp[1])[:, c, :], blocks(Kt)[:, c, :], blocks(Qt)[:, c, :], start=True, stop=True)
                    last.then_inc(sem("level_done"), 1)
                    pe.wait_ge(sem("k_end"), h + 1)
                    pe.wait_ge(sem("sg"), h + 1)
                    for c in range(NB):
                        last = pe.transpose(pblocks(pp[3])[:, c, :], blocks(KE)[:, c, :], ident[:, :])
                    last.then_inc(sem("k_turned"), 1)
                    for v in range(LEVELS):
                        if v == 2:
                            pe.wait_ge(sem("kn"), h + 1)
                            pe.wait_ge(sem("v"), h + 1)
                            for c in range(NB):
                                last = pe.matmul(pblocks(pp[0])[:, c, :], blocks(KN)[:, c, :], V[:, c, :], start=True, stop=True)
                            last.then_inc(sem("added"), 1)
                        pe.wait_ge(sem("left"), h * LEVELS + v + 1)
                        pe.wait_ge(sem("right"), h * LEVELS + v + 1)
                        if v >= 1:
                            pe.wait_ge(sem("placed"), h * NL + v)
                        x = blocks(X[v % 2])
                        out = pblocks(pp[1 + (v + 1) % 2])
                        for c in range(NB):
                            last = pe.matmul(out[:, c, :], x[:, c, :], x[:, c, :], start=True, stop=True)
                        last.then_inc(sem("level_done"), 1)
                    pe.wait_ge(sem("placed"), h * NL + NL)
                    pe.wait_ge(sem("q_start"), h + 1)
                    for c in range(NB):
                        if c:
                            pe.wait_ge(sem("state"), h * (NB - 1) + c)
                        out = pblocks(pp[1])[:, c, :]
                        last = pe.matmul(out, V[:, c, :], blocks(A)[:, c, :], start=True, stop=(c == 0))
                        if c:
                            last = pe.matmul(out, blocks(ST)[:, c, :], blocks(X[1])[:, c, :], start=False, stop=True)
                    last.then_inc(sem("o"), 1)

            @block.scalar
            def _(act):

                def level(h, v):
                    act.wait_ge(sem("level_diff"), h * LEVELS + v + 1)
                    act.activation(Dc[v % 2][:, :], Dc[v % 2][:, :], ACT.Exp).then_inc(sem("level_exp"), 1)

                def head(h, more):
                    act.wait_ge(W.s("used", 0), h * 2 + 2)
                    W.split_high(act, 0, h * 2 + 1)
                    act.activation(TF[:, :], flat2(pp[0]), ACT.Abs).then_inc(sem("abs"), 1)
                    act.wait_ge(sem("abs"), h + 1)
                    act.activation(TF[:, :], TF[:, :], ACT.Exp, scale=-1.0).then_inc(sem("exp_f"), 1)
                    act.wait_ge(sem("exp_f"), h + 1)
                    act.activation(TF[:, :], TF[:, :], ACT.Ln, bias=1.0).then_inc(sem("ln_f"), 1)
                    act.activation(Kt[:, :], flat2(pp[0]), ACT.Sigmoid, scale=-1.0).then_inc(sem("k"), 1)
                    act.wait_ge(W.s("used", 1), h * 2 + 2)
                    W.split_high(act, 1, h * 2 + 1)
                    act.activation(Qt[:, :], flat2(pp[1]), ACT.Silu).then_inc(sem("q"), 1)
                    level(h, 0)
                    level(h, 1)
                    act.activation(el[:, :], blocks(CU)[:, :, P - 1], ACT.Exp).then_inc(sem("el"), 1)
                    act.wait_ge(W.s("used", 0), h * 2 + 3)
                    if more:
                        W.split_high(act, 0, h * 2 + 2)
                    else:
                        nxt.split_high(act, 0)
                    act.activation(VT[:, :], flat2(pp[2]), ACT.Copy).then_inc(sem("vt"), 1)
                    act.wait_ge(W.s("used", 1), h * 2 + 3)
                    if more:
                        W.split_high(act, 1, h * 2 + 2)
                    else:
                        nxt.split_high(act, 1)
                    act.activation(SG[:, bass.ds(h, 1), :].squeeze(1), flat2(pp[3]), ACT.Silu).then_inc(sem("sg"), 1)
                    act.wait_ge(sem("v_turned"), h + 1)
                    act.activation(flat2(V), flat2(pp[0]), ACT.Copy).then_inc(sem("v"), 1)
                    act.wait_ge(sem("end_diff"), h + 1)
                    act.activation(KE[:, :], KE[:, :], ACT.Exp).then_inc(sem("end_exp"), 1)
                    level(h, 2)
                    act.wait_ge(sem("k_turned"), h + 1)
                    act.activation(KN[:, :], flat2(pp[3]), ACT.Copy).then_inc(sem("kn"), 1)
                    for v in range(3, LEVELS):
                        level(h, v)
                    act.wait_ge(sem("left"), h * LEVELS + LEVELS - 1)
                    act.wait_ge(sem("right"), h * LEVELS + LEVELS - 1)
                    act.activation(Dc[1][:, :], CU[:, :], ACT.Exp).then_inc(sem("exp_cum"), 1)
                    act.wait_ge(sem("o"), h + 1)
                    act.activation(O[:, bass.ds(h, 1), :].squeeze(1), flat2(pp[1]), ACT.Copy).then_inc(sem("o_out"), 1)
                over_loop(act, HG_H, head)

            @block.vector
            def _(dve):
                dve.sem_inc(sem("banks_free"), 1)
                dve.wait_ge(sem("keep"), 2)
                dve.wait_ge(sem("masks"), 16)
                with dve.Fori(0, HG_H) as h:
                    dve.wait_ge(sem("ln_f"), h + 1)
                    dve.wait_ge(sem("k"), h + 1)
                    dve.scalar_tensor_tensor(out=TF[:, :], in0=flat2(pp[0]), scalar=0.0, in1=TF[:, :], op0=ALU.min, op1=ALU.subtract).then_inc(sem("lf"), 1)
                    dve.wait_ge(sem("lf"), h + 1)
                    dve.tensor_tensor_scan(CU[:, :], keep[:, :], TF[:, :], 0.0, ALU.mult, ALU.add).then_inc(sem("cum"), 1)
                    dve.wait_ge(sem("cum"), h + 1)

                    def differences(v):
                        s = v % 2
                        if v >= 2:
                            dve.wait_ge(sem("left"), h * LEVELS + v - 1)
                            dve.wait_ge(sem("right"), h * LEVELS + v - 1)
                        l, r = halves(Dc[s], v)
                        cl, cr = halves(CU, v)
                        dve.tensor_tensor(l, middle(v), cl, ALU.subtract)
                        dve.tensor_tensor(r, cr, middle(v), ALU.subtract).then_inc(sem("level_diff"), 1)

                    def place(level):
                        dve.wait_ge(sem("level_done"), h * NL + level + 3)
                        dve.memset(blank[:, level:level + 1], 0.0)
                        m = masks[:, level, :].unsqueeze(1).to_broadcast([P, NB, P])
                        dve.copy_predicated(blocks(A), m, pblocks(pp[1 + level % 2])).then_inc(sem("placed"), 1)

                    def right(v):
                        s = v % 2
                        dve.wait_ge(sem("level_exp"), h * LEVELS + v + 1)
                        dve.wait_ge(sem("q"), h + 1)
                        dve.wait_ge(sem("level_done"), h * NL + v + 2)
                        dve.tensor_tensor(halves(X[s], v)[1], halves(Qt, v)[1], halves(Dc[s], v)[1], ALU.mult).then_inc(sem("right"), 1)

                    def states():
                        dve.wait_ge(sem("added"), h + 1)
                        dve.wait_ge(sem("el"), h + 1)
                        st, add = blocks(ST), pblocks(pp[0])
                        dve.tensor_copy(st[:, 1, :], add[:, 0, :]).then_inc(sem("state"), 1)
                        for c in range(1, NB - 1):
                            dve.wait_ge(sem("state"), h * (NB - 1) + c)
                            dve.scalar_tensor_tensor(out=st[:, c + 1, :], in0=st[:, c, :], scalar=el[:, c:c + 1], in1=add[:, c, :],
                                                     op0=ALU.mult, op1=ALU.add).then_inc(sem("state"), 1)

                    differences(0)
                    differences(1)
                    for v in range(LEVELS):
                        right(v)
                        if v == 0:
                            dve.wait_ge(sem("v_turned"), h + 1)
                            dve.tensor_tensor(blocks(KE), blocks(CU)[:, :, P - 1:P].to_broadcast([P, NB, P]), blocks(CU), ALU.subtract).then_inc(sem("end_diff"), 1)
                            dve.wait_ge(sem("end_exp"), h + 1)
                            dve.tensor_tensor(KE[:, :], Kt[:, :], KE[:, :], ALU.mult).then_inc(sem("k_end"), 1)
                        if v:
                            dve.wait_ge(sem("placed"), h * NL + v)
                        place(v)
                        if v + 2 < LEVELS:
                            differences(v + 2)
                        if v == 3:
                            states()
                    dve.wait_ge(sem("exp_cum"), h + 1)
                    dve.wait_ge(sem("level_done"), h * NL + LEVELS + 2)
                    dve.tensor_tensor(X[1][:, :], Qt[:, :], Dc[1][:, :], ALU.mult).then_inc(sem("q_start"), 1)
                    dve.wait_ge(sem("placed"), h * NL + LEVELS)
                    place(LEVELS)
                    dve.wait_ge(sem("state"), h * (NB - 1) + NB - 1)
                    dve.wait_ge(sem("o_out"), h + 1)
                    dve.sem_inc(sem("banks_free"), 1)


S5_CH = 4
S5_G = 32
S5_PAIRS = S5_G // 2
S5_P, S5_N = 64, 16
ST = 8
TWO_PI = 2 * np.pi
ROUND = 1.5 * 2.0 ** 23
FINE = 1.5 * 2.0 ** 7


def two_pi_parts():
    first = 6.28125
    second = float(np.floor((TWO_PI - first) * 2.0 ** 21) / 2.0 ** 21)
    return first, second, TWO_PI - first - second


class Chain:

    def __init__(self, engine, sem):
        self.engine, self.sem, self.count = engine, sem, 0

    def __call__(self, instruction):
        instruction.then_inc(self.sem, 1)
        self.count += 1
        self.engine.wait_ge(self.sem, self.count)


class S5Tables:

    def __init__(self, core, ctx):
        take = lambda name, shape: sbuf(core, ctx, name, [P] + shape)
        self.rot = take("rot", [2, S5_PAIRS, P])
        self.keep = take("keep", [S5_PAIRS, P])
        self.AB = take("ab", [2, S5_PAIRS, ST, S5_N])
        self.BB = take("bb", [2, S5_PAIRS, S5_N])
        self.CA = take("ca", [2, S5_PAIRS, ST + 2, S5_N])
        self.UT = take("ut", [S5_G, P])


def stage_s5_tables(core, T):
    nc, io = core.nc, core.io
    w_in = io["w_in_2"][0]
    with stage(core) as (ctx, sem):
        W = WeightTiles(core, ctx, sem, KD)
        lam = sbuf(core, ctx, "lam", [P, 3, S5_PAIRS])
        B = sbuf(core, ctx, "b", [P, 2, S5_PAIRS, S5_N])
        cn = sbuf(core, ctx, "c_rows", [P, 2, 4, 2, S5_P])
        C = sbuf(core, ctx, "c", [P, 2, S5_PAIRS, S5_N])
        v = sbuf(core, ctx, "values", [P, 12, S5_PAIRS])
        count = sbuf(core, ctx, "count", [P, P])
        pw = sbuf(core, ctx, "powers", [P, 6, ST + 1, S5_PAIRS])
        half_pi = sbuf(core, ctx, "half_pi", [P, 1])
        tmp = T.AB[:, :, :, :, :].rearrange("p i q j h -> p i (q j h)")
        scratch_b = sbuf(core, ctx, "scratch_b", [P, 2, S5_PAIRS, S5_N])
        scratch_c = sbuf(core, ctx, "scratch", [P, S5_PAIRS, S5_N])
        ub = [sbuf(core, ctx, f"u_blocks{s}", [P, ST, P]) for s in range(2)]
        pU = [psum(core, ctx, f"pu{s}", [P, 2, HALF]) for s in range(2)]
        pC = psum(core, ctx, "pc", [P, 2, 4, P])
        NQ = S5_PAIRS

        def fill(t, a):
            return a.unsqueeze(2).to_broadcast([P, NQ, t])

        with nc.Block() as block:

            @block.sync
            def _(sp):
                two = lambda name: io[name][0].rearrange("(q r) p -> r p q", r=2)
                for r in range(2):
                    half = slice(r * S5_P, (r + 1) * S5_P)
                    sp.dma_start(lam[half, 0, :], two("s5_lambda_re_2")[r]).then_inc(sem("lam"), 16)
                    sp.dma_start(lam[half, 1, :], two("s5_lambda_im_2")[r]).then_inc(sem("lam"), 16)
                    sp.dma_start(lam[half, 2, :], io["s5_log_step_2"][0].rearrange("(q r) -> r q", r=2)[r].partition_broadcast(S5_P)).then_inc(sem("lam"), 16)
                for i, name in enumerate(("s5_b_re_2", "s5_b_im_2")):
                    for r in range(2):
                        sp.dma_start(B[r * S5_P:(r + 1) * S5_P, i, :, :], io[name][0].rearrange("(q r) p h -> r p q h", r=2)[r]).then_inc(sem("b"), 16)
                for i, name in enumerate(("s5_c_re_2", "s5_c_im_2")):
                    for r in range(2):
                        sp.dma_start(cn[:, i, :, r, :], io[name][0].rearrange("(n g) h p -> (g h) n p", g=8)).then_inc(sem("c"), 16)
                for n in range(2, S5_CH):
                    W.load(sp, n % 2, n // 2, w_in[:, U_AT + n * P:U_AT + (n + 1) * P])
                for n in range(S5_CH):
                    sp.wait_ge(sem("u_blocks"), n + 1)
                    sp.dma_start(core.s5_u[n * P:(n + 1) * P, :, :], ub[n % 2][:, :, :]).then_inc(sem(f"u_stored{n % 2}"), 16)
                for s in range(2):
                    sp.wait_ge(sem(f"u_stored{s}"), 16 * S5_CH // 2)
                for j in range(ST):
                    sp.dma_start(T.UT[j * S5_N:(j + 1) * S5_N, :, :], core.s5_u[:, j, :].rearrange("(g h) b -> h g b", h=S5_N)).then_inc(sem("ut"), 16)
                sp.wait_ge(sem("ut"), 16 * ST)

            @block.gpsimd
            def _(pool):
                W.open_pool(pool)
                pool.memset(half_pi[:, :], np.pi / 2).then_inc(sem("half_pi"), 1)
                for n in range(S5_CH):
                    W.split_low(pool, n % 2, n // 2)
                pool.wait_ge(sem("bb"), 1)
                pool.wait_ge(sem("big_sin"), 1)
                pool.wait_ge(sem("big_cos"), 1)
                done = Chain(pool, sem("pool"))
                re, im = T.BB[:, 0, :, :], T.BB[:, 1, :, :]
                for tau in range(ST):
                    ar, ai = fill(S5_N, pw[:, 2, tau, :]), fill(S5_N, pw[:, 3, tau, :])
                    for i, (b1, b2, op) in enumerate(((re, im, ALU.subtract), (im, re, ALU.add))):
                        out = T.AB[:, i, :, ST - 1 - tau, :]
                        pool.tensor_tensor(scratch_b[:, i, :, :], b1, ar, ALU.mult).then_inc(sem("pool_part"), 1)
                        done(pool.tensor_tensor(out, b2, ai, ALU.mult))
                        pool.wait_ge(sem("pool_part"), 2 * tau + i + 1)
                        done(pool.tensor_tensor(out, scratch_b[:, i, :, :], out, op))

            @block.tensor
            def _(pe):
                W.open_pe(pe)
                pe.wait_ge(sem("c"), 64)
                for i in range(2):
                    for n in range(4):
                        last = pe.transpose(pC[:, i, n, :], cn[:, i, n, :, :].rearrange("x r p -> x (r p)"), core.ident[:, :])
                last.then_inc(sem("c_turned"), 1)
                for n in range(S5_CH):
                    W.wait(pe, n % 2, n // 2)
                    if n >= 2:
                        pe.wait_ge(sem("u_blocks"), n - 1)
                    W.multiply(pe, n % 2, pU[n % 2], core.AH, core.AL)

            @block.scalar
            def _(act):
                act.wait_ge(sem("lam"), 96)
                act.activation(v[:, 0, :], lam[:, 2, :], ACT.Exp).then_inc(sem("step"), 1)
                act.wait_ge(sem("half_pi"), 1)
                act.wait_ge(sem("log_powers"), 1)
                act.activation(pw[:, 1, :, :], pw[:, 0, :, :], ACT.Exp).then_inc(sem("mags"), 1)
                act.activation(v[:, 9, :], pw[:, 0, ST, :], ACT.Exp).then_inc(sem("mags"), 1)
                act.wait_ge(sem("turns"), 1)
                act.activation(pw[:, 3, :, :], pw[:, 2, :, :], ACT.Sin, scale=6.283185).then_inc(sem("sin"), 1)
                act.activation(pw[:, 4, :, :], pw[:, 2, :, :], ACT.Abs).then_inc(sem("abs"), 1)
                act.wait_ge(sem("abs"), 1)
                act.activation(pw[:, 4, :, :], pw[:, 4, :, :], ACT.Sin, scale=-6.283185, bias=half_pi[:, 0:1]).then_inc(sem("cos"), 1)

                def blocks(n):
                    act.wait_ge(W.s("used", n % 2), n // 2 + 2)
                    if n >= 2:
                        act.wait_ge(sem(f"u_stored{n % 2}"), 16 * (n // 2))
                    act.activation(ub[n % 2][:, :, :], flat2(pU[n % 2]).rearrange("p (b j) -> p j b", j=ST), ACT.Copy).then_inc(sem("u_blocks"), 1)
                    if n < 2:
                        W.split_high(act, n, 1)
                blocks(0)
                blocks(1)
                act.wait_ge(sem("big_turns"), 1)
                flat = lambda t: t.rearrange("p q b -> p (q b)")
                act.activation(flat(T.rot[:, 1, :, :]), tmp[:, 0, :], ACT.Sin, scale=6.283185).then_inc(sem("big_sin"), 1)
                act.activation(tmp[:, 1, :], tmp[:, 0, :], ACT.Abs).then_inc(sem("abs"), 1)
                act.wait_ge(sem("abs"), 2)
                act.activation(flat(T.rot[:, 0, :, :]), tmp[:, 1, :], ACT.Sin, scale=-6.283185, bias=half_pi[:, 0:1]).then_inc(sem("big_cos"), 1)
                blocks(2)
                blocks(3)

            @block.vector
            def _(dve):
                done = Chain(dve, sem("dve"))
                c1, c2, c3 = two_pi_parts()
                done(dve.tensor_tensor_scan(count[:, :], core.ones[:, :], core.ones[:, :], -1.0, ALU.mult, ALU.add))
                dve.wait_ge(sem("lam"), 96)
                lr, li = v[:, 1, :], lam[:, 1, :]
                done(dve.tensor_scalar(lr, lam[:, 0, :], -1e-4, None, ALU.min))
                dve.wait_ge(sem("step"), 1)
                step, ls, ang, k, f = (v[:, i, :] for i in (0, 2, 3, 4, 5))
                done(dve.tensor_tensor(ls, lr, step, ALU.mult))
                taus = count[:, 0:ST + 1].unsqueeze(2).to_broadcast([P, ST + 1, NQ])
                over_taus = lambda a: a.unsqueeze(1).to_broadcast([P, ST + 1, NQ])
                done(dve.tensor_tensor(pw[:, 0, :, :], taus, over_taus(ls), ALU.mult))
                dve.sem_inc(sem("log_powers"), 1)
                done(dve.tensor_tensor(ang, li, step, ALU.mult))
                done(dve.tensor_scalar(k, ang, 1.0 / TWO_PI, ROUND, ALU.mult, ALU.add))
                done(dve.tensor_scalar(k, k, ROUND, None, ALU.subtract))
                for c in (c1, c2, c3):
                    done(dve.scalar_tensor_tensor(out=ang, in0=k, scalar=-c, in1=ang, op0=ALU.mult, op1=ALU.add))
                done(dve.tensor_scalar(f, ang, 1.0 / TWO_PI, None, ALU.mult))

                def split(f, high, low):
                    done(dve.tensor_scalar(high, f, FINE, None, ALU.add))
                    done(dve.tensor_scalar(high, high, FINE, None, ALU.subtract))
                    done(dve.tensor_tensor(low, f, high, ALU.subtract))

                def turns(out, scratch, mult, high, low):
                    done(dve.tensor_tensor(out, mult, high, ALU.mult))
                    done(dve.tensor_scalar(scratch, out, ROUND, None, ALU.add))
                    done(dve.tensor_scalar(scratch, scratch, ROUND, None, ALU.subtract))
                    done(dve.tensor_tensor(out, out, scratch, ALU.subtract))
                    done(dve.tensor_tensor(scratch, mult, low, ALU.mult))
                    done(dve.tensor_tensor(out, out, scratch, ALU.add))
                    done(dve.tensor_scalar(out, out, 0.5, -0.5, ALU.min, ALU.max))

                high, low = v[:, 6, :], v[:, 7, :]
                split(f, high, low)
                turns(pw[:, 2, :, :], pw[:, 5, :, :], taus, over_taus(high), over_taus(low))
                dve.sem_inc(sem("turns"), 1)
                done(dve.tensor_scalar(f, f, float(ST), None, ALU.mult))
                done(dve.tensor_scalar(k, f, ROUND, None, ALU.add))
                done(dve.tensor_scalar(k, k, ROUND, None, ALU.subtract))
                done(dve.tensor_tensor(f, f, k, ALU.subtract))
                split(f, high, low)
                big = [tmp[:, i, :].rearrange("p (q b) -> p q b", b=P) for i in range(2)]
                turns(big[0], big[1], count[:, :].unsqueeze(1).to_broadcast([P, NQ, P]), fill(P, high), fill(P, low))
                dve.sem_inc(sem("big_turns"), 1)

                dve.wait_ge(sem("mags"), 2)
                done(dve.tensor_copy(T.keep[:, :, :], fill(P, v[:, 9, :])))
                done(dve.memset(T.keep[:, :, 0:1], 0.0))
                dve.wait_ge(sem("sin"), 1)
                dve.wait_ge(sem("cos"), 1)
                are, aim = pw[:, 2, :, :], pw[:, 3, :, :]
                done(dve.tensor_tensor(are, pw[:, 1, :, :], pw[:, 4, :, :], ALU.mult))
                done(dve.tensor_tensor(aim, pw[:, 1, :, :], aim, ALU.mult))
                nr, ni, den, t1, t2 = (v[:, i, :] for i in (6, 7, 8, 10, 11))
                cr, ci = v[:, 2, :], v[:, 3, :]
                done(dve.tensor_scalar(nr, pw[:, 2, 1, :], 1.0, None, ALU.subtract))
                done(dve.tensor_copy(ni, pw[:, 3, 1, :]))
                done(dve.tensor_tensor(t1, lr, lr, ALU.mult))
                done(dve.tensor_tensor(t2, li, li, ALU.mult))
                done(dve.tensor_tensor(t1, t1, t2, ALU.add))
                done(dve.reciprocal(den, t1))
                done(dve.tensor_tensor(t1, nr, lr, ALU.mult))
                done(dve.tensor_tensor(t2, ni, li, ALU.mult))
                done(dve.tensor_tensor(t1, t1, t2, ALU.add))
                done(dve.tensor_tensor(cr, t1, den, ALU.mult))
                done(dve.tensor_tensor(t1, ni, lr, ALU.mult))
                done(dve.tensor_tensor(t2, nr, li, ALU.mult))
                done(dve.tensor_tensor(t1, t1, t2, ALU.subtract))
                done(dve.tensor_tensor(ci, t1, den, ALU.mult))

                def times(out, sign, a1, b1, a2, b2, scratch):
                    done(dve.tensor_tensor(scratch, a1, b1, ALU.mult))
                    done(dve.tensor_tensor(out, a2, b2, ALU.mult))
                    done(dve.tensor_tensor(out, scratch, out, ALU.add if sign > 0 else ALU.subtract))

                dve.wait_ge(sem("b"), 64)
                small = scratch_c[:, :, :]
                times(T.BB[:, 0, :, :], -1, B[:, 0, :, :], fill(S5_N, cr), B[:, 1, :, :], fill(S5_N, ci), small)
                times(T.BB[:, 1, :, :], +1, B[:, 1, :, :], fill(S5_N, cr), B[:, 0, :, :], fill(S5_N, ci), small)
                dve.sem_inc(sem("bb"), 1)
                dve.wait_ge(sem("c_turned"), 1)
                for i in range(2):
                    for r in range(2):
                        half = slice(r * S5_P, (r + 1) * S5_P)
                        src = pC[half, i, :, :].rearrange("p n (q r h) -> p (n q) r h", r=2, h=S5_N)[:, :, r, :]
                        done(dve.tensor_copy(C[half, i, :, :], src))
                for i in range(2):
                    done(dve.memset(T.CA[:, i, :, 0, :], 0.0))
                for tau in range(ST + 1):
                    ar, ai = fill(S5_N, pw[:, 2, tau, :]), fill(S5_N, pw[:, 3, tau, :])
                    sc = scratch_c[:, :, :]
                    times(T.CA[:, 0, :, tau + 1, :], -1, C[:, 0, :, :], ar, C[:, 1, :, :], ai, sc)
                    done(dve.tensor_tensor(sc, C[:, 0, :, :], ai, ALU.mult))
                    done(dve.tensor_tensor(T.CA[:, 1, :, tau + 1, :], C[:, 1, :, :], ar, ALU.mult))
                    done(dve.scalar_tensor_tensor(out=T.CA[:, 1, :, tau + 1, :], in0=sc, scalar=-1.0, in1=T.CA[:, 1, :, tau + 1, :],
                                                  op0=ALU.mult, op1=ALU.subtract))


def stage_s5_states(core, T):
    nc = core.nc
    NQ = S5_PAIRS
    with stage(core) as (ctx, sem):
        Z = sbuf(core, ctx, "z", [P, 2, NQ, P])
        R = T.AB[:, :, :, :, :].rearrange("p i q j h -> p i q (j h)")
        Y = Z[:, :, :, :].rearrange("p i q b -> p (i q) b")
        two = range(2)
        lay = Overlay(core, core.w_at, 6 * 4 * D)
        ab = [lay.take(f"ab{s}", [P, 2, P]) for s in two]
        abt = [lay.take(f"abt{s}", [P, 2, 2, P]) for s in two]
        t1 = [lay.take(f"tc{s}", [P, 2, P]) for s in two]
        t2 = [lay.take(f"ts{s}", [P, 2, P]) for s in two]
        be = [lay.take(f"b_even_odd{s}", [P, 2, 2, 2, ST, S5_N]) for s in two]
        cs = [lay.take(f"c_next{s}", [P, 2, 2, P]) for s in two]
        M = [sbuf(core, ctx, f"m{s}", [P, 2, P]) for s in two]
        SX = [sbuf(core, ctx, f"sx{s}", [P, 2, P]) for s in two]
        pT = [psum(core, ctx, f"pt{s}", [P, 4, P]) for s in two]
        pS = [psum(core, ctx, f"ps{s}", [P, 4, P]) for s in two]
        pM = [psum(core, ctx, f"pm{s}", [P, 4, P]) for s in two]
        pY = [psum(core, ctx, f"py{s}", [P, 4, P]) for s in two]

        def pairs(engine, body):
            with engine.Fori(0, NQ // 2) as i:
                for s in two:
                    body(i * 2 + s, s)

        def pairs_ahead(engine, prepare, finish):
            prepare(0, 0)
            with engine.Fori(0, NQ // 2 - 1) as i:
                for s in two:
                    prepare(i * 2 + (s + 1), 1 - s)
                    finish(i * 2 + s, s)
            prepare(NQ - 1, 1)
            finish(NQ - 2, 0)
            finish(NQ - 1, 1)

        def one(t, q):
            return t[:, :, bass.ds(q, 1), :].rearrange("p i q b -> p (i q) b")

        with nc.Block() as block:

            @block.gpsimd
            def _(pool):
                for s in two:
                    pool.memset(abt[s][:, :, :, :], 0.0).then_inc(sem("zero"), 1)
                    pool.memset(be[s][:, :, :, :, :, :], 0.0).then_inc(sem("zero"), 1)
                    pool.memset(cs[s][:, :, :, :], 0.0).then_inc(sem("zero"), 1)
                    pool.memset(M[s][:, :, :], 0.0).then_inc(sem("zero"), 1)
                    pool.memset(SX[s][:, :, 0:1], 0.0).then_inc(sem("zero"), 1)
                pool.wait_ge(sem("zero"), 10)

                def to_ab(q, s):
                    pool.wait_ge(sem("ab_turned"), q + 1)
                    pool.sem_inc(sem("pool_asked"), 1)
                    pool.tensor_copy(ab[s][:, :, :], T.AB[:, :, bass.ds(q, 1), :, :].rearrange("p i q j h -> p (i q) (j h)")).then_inc(sem("ab"), 1)
                pairs(pool, to_ab)
                pool.wait_ge(sem("ab"), NQ)

                def to_bc(q, s):
                    rows = [slice(r * S5_P, (r + 1) * S5_P) for r in two]
                    pool.wait_ge(sem("pm"), q + 1)
                    pool.sem_inc(sem("pool_asked"), 1)
                    for r in two:
                        b = T.BB[rows[r], :, bass.ds(q, 1), :].to_broadcast([S5_P, 2, ST // 2, S5_N])
                        for odd in two:
                            pool.tensor_copy(be[s][rows[r], r, :, odd, odd::2, :], b).then_inc(sem("be"), 1)
                        pool.wait_ge(sem("be"), q * 4 + 2 * r + 2)
                    pool.wait_ge(sem("y"), q + 1)
                    pool.sem_inc(sem("pool_asked"), 1)
                    for r in two:
                        pool.tensor_copy(cs[s][rows[r], r, :, :], T.CA[rows[r], :, bass.ds(q, 1), 2:, :].rearrange("p i q j h -> p (i q) (j h)")).then_inc(sem("cs"), 1)
                        pool.wait_ge(sem("cs"), q * 2 + r + 1)
                pairs(pool, to_bc)

            @block.tensor
            def _(pe):
                pe.sem_inc(sem("ab_turned"), 2)
                pe.sem_inc(sem("y"), 2)
                pe.sem_inc(sem("pm"), 2)

                def inputs(q, s):
                    pe.wait_ge(sem("ab"), q + 1)
                    for i in two:
                        last = pe.transpose(pT[s][:, i, :], ab[s][:, i, :], core.ident[:, :])
                    last.then_inc(sem("ab_turned"), 1)
                    pe.wait_ge(sem("abt"), 2 * q + 2)
                    pe.wait_ge(sem("z"), q + 1)
                    for i in two:
                        for r in two:
                            last = pe.matmul(pS[s][:, i, :], abt[s][:, i, r, :], T.UT[:, bass.ds(q * 2 + r, 1), :].squeeze(1),
                                             start=(r == 0), stop=(r == 1))
                    last.then_inc(sem("inputs"), 1)
                pairs(pe, inputs)

                def kernels(q, s):
                    pe.wait_ge(sem("be"), 4 * q + 4)
                    pe.wait_ge(sem("m"), q * 4 + 4)
                    for r in two:
                        n = 0
                        for i in two:
                            for odd in two:
                                last = pe.matmul(pM[s][:, r, :], be[s][:, r, i, odd, :, :].rearrange("p j h -> p (j h)"),
                                                 T.CA[:, i, bass.ds(q, 1), 1 - odd:ST + 1 - odd, :].rearrange("p q j h -> p (q j h)"),
                                                 start=(n == 0), stop=(n == 3))
                                n += 1
                    last.then_inc(sem("pm"), 1)

                def outputs(q, s):
                    pe.wait_ge(sem("cs"), 2 * q + 2)
                    pe.wait_ge(sem("m"), q * 4 + 12)
                    pe.wait_ge(sem("sx"), q * 2 + 2)
                    pe.wait_ge(sem("y_kept"), q + 1)
                    for r in two:
                        pe.matmul(pY[s][:, r, :], M[s][:, r, :], T.UT[:, bass.ds(q * 2 + r, 1), :].squeeze(1), start=True, stop=False)
                        for i in two:
                            last = pe.matmul(pY[s][:, r, :], cs[s][:, r, i, :], SX[s][:, i, :], start=False, stop=(i == 1))
                    last.then_inc(sem("y"), 1)
                pairs_ahead(pe, kernels, outputs)

            @block.scalar
            def _(act):
                def turned(q, s):
                    act.wait_ge(sem("ab_turned"), q + 3)
                    act.wait_ge(sem("inputs_credit"), q + 1)
                    for r in two:
                        cols = slice(r * S5_P, (r + 1) * S5_P)
                        act.activation(abt[s][:, :, r, cols], pT[s][:, 0:2, cols], ACT.Copy).then_inc(sem("abt"), 1)
                act.wait_ge(sem("zero"), 10)
                pairs(act, turned)
                act.sem_inc(sem("m"), 8)

                def bands(q, s):
                    act.wait_ge(sem("pm"), q + 3)
                    act.wait_ge(sem("y"), q + 1)
                    for band in range(4):
                        at = band * 2 * S5_N
                        act.activation(M[s][at:at + 32, :, at:P], pM[s][at:at + 32, 0:2, 0:P - at], ACT.Copy).then_inc(sem("m"), 1)

                def keep(q, s):
                    act.wait_ge(sem("y"), q + 3)
                    act.activation(Y[:, bass.ds(q * 2, 2), :], pY[s][:, 0:2, :], ACT.Copy).then_inc(sem("y_kept"), 1)
                act.sem_inc(sem("y_kept"), 2)
                pairs_ahead(act, bands, keep)

            @block.vector
            def _(dve):
                dve.sem_inc(sem("z"), 2)
                dve.sem_inc(sem("inputs_credit"), 2)

                def rotate(q, s):
                    cos, sin = (T.rot[:, i, bass.ds(q, 1), :].to_broadcast([P, 2, P]) for i in two)
                    dve.wait_ge(sem("inputs"), q + 1)
                    dve.sem_inc(sem("inputs_credit"), 1)
                    dve.tensor_tensor(t1[s][:, :, :], pS[s][:, 0:2, :], cos, ALU.mult).then_inc(sem("t1"), 1)
                    dve.tensor_tensor(t2[s][:, :, :], pS[s][:, 0:2, :], sin, ALU.mult).then_inc(sem("z"), 1)
                    dve.wait_ge(sem("t1"), q + 1)
                    dve.wait_ge(sem("z"), q + 3)
                    dve.tensor_tensor(Z[:, 0, bass.ds(q, 1), :].squeeze(1), t1[s][:, 0, :], t2[s][:, 1, :], ALU.add).then_inc(sem("zz"), 1)
                    dve.tensor_tensor(Z[:, 1, bass.ds(q, 1), :].squeeze(1), t1[s][:, 1, :], t2[s][:, 0, :], ALU.subtract).then_inc(sem("zz"), 1)
                    dve.wait_ge(sem("zz"), q * 2 + 2)
                pairs(dve, rotate)
                for i in two:
                    dve.tensor_tensor_scan(R[:, i, :, :].rearrange("p q b -> p (q b)"), T.keep[:, :, :].rearrange("p q b -> p (q b)"),
                                           Z[:, i, :, :].rearrange("p q b -> p (q b)"), 0.0, ALU.mult, ALU.add).then_inc(sem("scan"), 1)
                dve.wait_ge(sem("scan"), 2)
                dve.wait_ge(sem("zero"), 10)

                def back(q, s):
                    cos, sin = (T.rot[:, i, bass.ds(q, 1), :].to_broadcast([P, 2, P]) for i in two)
                    dve.tensor_tensor(t1[s][:, :, :], one(R, q), cos, ALU.mult).then_inc(sem("u1"), 1)
                    dve.tensor_tensor(t2[s][:, :, :], one(R, q), sin, ALU.mult).then_inc(sem("u2"), 1)
                    dve.wait_ge(sem("u1"), q + 1)
                    dve.wait_ge(sem("u2"), q + 1)
                    dve.wait_ge(sem("y"), q + 1)
                    dve.tensor_tensor(SX[s][:, 0, 1:], t1[s][:, 0, :P - 1], t2[s][:, 1, :P - 1], ALU.subtract).then_inc(sem("sx"), 1)
                    dve.tensor_tensor(SX[s][:, 1, 1:], t1[s][:, 1, :P - 1], t2[s][:, 0, :P - 1], ALU.add).then_inc(sem("sx"), 1)
                    dve.wait_ge(sem("sx"), q * 2 + 2)
                pairs(dve, back)

            @block.sync
            def _(sp):
                sp.wait_ge(sem("y_kept"), NQ + 2)
                for j in range(ST):
                    sp.dma_start(core.s5_y[:, j, :].rearrange("(g h) b -> h g b", h=S5_N), Y[j * S5_N:(j + 1) * S5_N, :, :]).then_inc(sem("stored"), 16)
                sp.wait_ge(sem("stored"), 16 * ST)


def stage_s5_glu(core, O, ahead):
    nc, io = core.nc, core.io
    w_in, glu = io["w_in_2"][0], io["s5_glu_w_2"][0]
    with stage(core) as (ctx, sem):
        W = WeightTiles(core, ctx, sem, KD, ready=False)
        nxt = Ahead(core, sem, ahead, W, (3 * S5_CH // 2, 3 * S5_CH // 2))
        yb = sbuf(core, ctx, "y_blocks", [P, S5_CH, SEQ])
        ub = sbuf(core, ctx, "u_blocks", [P, S5_CH, SEQ])
        H = sbuf(core, ctx, "y_high", [P, S5_CH, SEQ], F32R)
        L = sbuf(core, ctx, "y_low", [P, S5_CH, SEQ], F32R)
        skip = sbuf(core, ctx, "skip", [P, S5_CH])
        bias = sbuf(core, ctx, "bias", [P, 2 * S5_CH])
        sig = sbuf(core, ctx, "sig", [P, SEQ])
        gate = sbuf(core, ctx, "gate", [P, SEQ])
        pV, pS, pG = (psum(core, ctx, n, [P, 2, HALF]) for n in ("pv", "ps", "pg"))

        def tile(n, j):
            t = 3 * n + j
            return t % 2, t // 2

        def multiplied(engine, n, j):
            slot, turn = tile(n, j)
            engine.wait_ge(W.s("used", slot), turn + 2)

        with nc.Block() as block:

            @block.sync
            def _(sp):
                def load(n):
                    W.load(sp, *tile(n, 0), w_in[:, S5G_AT + n * P:S5G_AT + (n + 1) * P])
                    W.load(sp, *tile(n, 1), glu[:, n * P:(n + 1) * P], S5_CH)
                    W.load(sp, *tile(n, 2), glu[:, (S5_CH + n) * P:(S5_CH + n + 1) * P], S5_CH)
                load(0)
                sp.dma_start(skip[:, :], per_channel(io["s5_d_2"][0])).then_inc(sem("small"), 16)
                sp.dma_start(bias[:, :], per_channel(io["s5_glu_b_2"][0])).then_inc(sem("small"), 16)
                for n in range(S5_CH):
                    sp.dma_start(yb[:, n, :], core.s5_y[n * P:(n + 1) * P, :, :].rearrange("p j b -> p (j b)")).then_inc(sem(f"y{n}"), 16)
                    sp.dma_start(ub[:, n, :], core.s5_u[n * P:(n + 1) * P, :, :].rearrange("p j b -> p (j b)")).then_inc(sem(f"y{n}"), 16)
                for n in range(1, S5_CH):
                    load(n)
                nxt.load(sp)

            @block.gpsimd
            def _(pool):
                W.open_pool(pool)
                for n in range(S5_CH):
                    W.split_low(pool, *tile(n, 0))
                    W.split_low(pool, *tile(n, 1), S5_CH)
                    W.split_low(pool, *tile(n, 2), S5_CH)
                nxt.split_low(pool)

            @block.tensor
            def _(pe):
                W.open_pe(pe)
                for n in range(S5_CH):
                    W.wait(pe, *tile(n, 0))
                    if n:
                        pe.wait_ge(sem("silu"), n)
                    W.multiply(pe, tile(n, 0)[0], pG, core.AH, core.AL)
                    if n == 0:
                        pe.wait_ge(sem("low"), S5_CH)
                    W.wait(pe, *tile(n, 1))
                    if n:
                        pe.wait_ge(sem("val"), n)
                    W.multiply(pe, tile(n, 1)[0], pV, H, L, S5_CH)
                    W.wait(pe, *tile(n, 2))
                    if n:
                        pe.wait_ge(sem("sig"), n)
                    W.multiply(pe, tile(n, 2)[0], pS, H, L, S5_CH)

            @block.scalar
            def _(act):
                W.split_high(act, *tile(0, 0))
                W.split_high(act, *tile(0, 1), S5_CH)
                for n in range(S5_CH):
                    act.wait_ge(sem("sum"), n + 1)
                    act.activation(ub[:, n, :], ub[:, n, :], ACT.Gelu_apprx_tanh).then_inc(sem("gelu"), 1)
                for n in range(S5_CH):
                    act.wait_ge(sem("gelu"), n + 1)
                    act.activation(H[:, n, :], ub[:, n, :], ACT.Copy).then_inc(sem("high"), 1)
                act.wait_ge(sem("small"), 32)
                for n in range(S5_CH):
                    multiplied(act, n, 0)
                    if n:
                        act.wait_ge(sem("out"), n)
                    act.activation(gate[:, :], flat2(pG), ACT.Silu).then_inc(sem("silu"), 1)
                    W.split_high(act, *tile(n, 2), S5_CH)
                    if n < S5_CH - 1:
                        W.split_high(act, *tile(n + 1, 0))
                    else:
                        nxt.split_high(act, 0)
                    multiplied(act, n, 2)
                    act.activation(sig[:, :], flat2(pS), ACT.Sigmoid, bias=bias[:, S5_CH + n:S5_CH + n + 1]).then_inc(sem("sig"), 1)
                    if n < S5_CH - 1:
                        W.split_high(act, *tile(n + 1, 1), S5_CH)
                nxt.split_high(act, 1)

            @block.vector
            def _(dve):
                dve.wait_ge(sem("small"), 32)
                for n in range(S5_CH):
                    dve.wait_ge(sem(f"y{n}"), 32)
                    dve.scalar_tensor_tensor(out=yb[:, n, :], in0=ub[:, n, :], scalar=skip[:, n:n + 1], in1=yb[:, n, :],
                                             op0=ALU.mult, op1=ALU.add).then_inc(sem("plus"), 1)
                    dve.wait_ge(sem("plus"), n + 1)
                    dve.tensor_copy(ub[:, n, :].rearrange("p (b j) -> p j b", j=ST), yb[:, n, :].rearrange("p (j b) -> p j b", j=ST)).then_inc(sem("sum"), 1)
                for n in range(S5_CH):
                    dve.wait_ge(sem("high"), n + 1)
                    dve.tensor_tensor(L[:, n, :], ub[:, n, :], H[:, n, :].bitcast(F32), ALU.subtract).then_inc(sem("low"), 1)
                for n in range(S5_CH):
                    dve.wait_ge(sem("sig"), n + 1)
                    dve.scalar_tensor_tensor(out=O[:, n, :], in0=flat2(pV), scalar=bias[:, n:n + 1], in1=sig[:, :],
                                             op0=ALU.add, op1=ALU.mult).then_inc(sem("val"), 1)
                    dve.wait_ge(sem("val"), n + 1)
                    dve.tensor_tensor(O[:, n, :], O[:, n, :], gate[:, :], ALU.mult).then_inc(sem("out"), 1)


def second_block(core):
    io, nc = core.io, core.nc
    w_in, w_out = io["w_in_2"][0], io["w_out_2"][0]
    w_ssd, w_hgrn, w_s5 = w_out[0:D, :], w_out[D:D + HALF, :], w_out[D + HALF:2 * D, :]
    first_rows = lambda w, chunks: list(enumerate(rows_tiles(w, chunks)[:2]))
    SIZE = 4 * 4 * SEQ
    at = lambda name, n, dtype=F32: nc.alloc_sbuf_tensor_at(name, [P, 4, SEQ], dtype, offset=nc.sbuf_top - n * SIZE)
    O, OL, SG, OH = at("part_out", 1), at("part_low", 1, F32R), at("hgrn_gate", 2), at("part_high", 3, F32R)
    core.limit = nc.sbuf_top - SIZE
    with ExitStack() as ctx:
        T = S5Tables(core, ctx)
        stage_s5_tables(core, T)
        stage_s5_states(core, T)
    stage_s5_glu(core, O, first_rows(w_s5, S5_CH))
    X = sbuf(core, core.ctx, "mixed", [P, NB, D])
    core.limit = nc.sbuf_top - 3 * SIZE
    stage_mix_rows(core, O, S5_CH, S5_CH, io["s5_norm_w_2"][0], OH, OL, w_s5, X,
                   ahead=columns(w_in, F_AT, Q_AT), add=False)
    core.limit = nc.sbuf_top - 2 * SIZE
    stage_hgrn(core, O, SG, first_rows(w_hgrn, 4))
    core.limit = nc.sbuf_top - 3 * SIZE
    stage_mix_rows(core, O, 4, 1, io["hgrn_norm_w_2"][0], OH, OL, w_hgrn, X,
                   ahead=columns(w_in, XBC_AT, DT_AT), factor=SG)
    core.limit = nc.sbuf_top
    with ExitStack() as ctx:
        ZT = sbuf(core, ctx, "z", [P, KD, SEQ])
        with ExitStack() as inner:
            dtN = sbuf(core, inner, "dt", [P, NB, SSD_H])
            acN = sbuf(core, inner, "acum", [P, NB, SSD_H])
            XBC = sbuf(core, inner, "xbc", [P, SSD_CH, SEQ])
            stage_ssd_project(core, XBC, ZT, dtN, acN)
            stage_ssd_chunks(core, XBC, ZT, dtN, acN, first_rows(w_ssd, KD))
        stage_mix_rows(core, ZT, KD, 4, io["ssd_norm_w_2"][0], core.AH, core.AL, w_ssd, X)
    stage_norm_time(core, X, io["post_norm_w_2"][0], residual=core.x_mid, out=io["out"])


def program(nc, io):
    with ExitStack() as ctx:
        ctx.enter_context(nc.allow_non_contiguous_dma(reason="small vectors and the S5 part's blocks"))
        core = make_core(nc, io, ctx)
        core.ctx = ctx
        scratch = lambda name, shape: nc.dram_tensor(name, shape, F32).ap()
        core.lines = scratch("lines", [4, P, LINE])
        core.neg_c = scratch("neg_c", [8, SEQ])
        core.m_part = scratch("m_part", [KD, P, SEQ])
        core.x_mid = scratch("x_mid", [SEQ, D])
        core.acum = scratch("acum_rows", [NB, SSD_H, P])
        core.s5_u = scratch("s5_u", [S5_CH * P, ST, P])
        core.s5_y = scratch("s5_y", [S5_CH * P, ST, P])
        setup(core)
        first_block(core)
        second_block(core)


def kernel(**inputs):
    import concourse.bacc as bacc
    from concourse.bass_utils import run_bass_kernel_spmd

    nc = bacc.Bacc("TRN2", target_bir_lowering=False, num_devices=1)
    data = dict(inputs, bucket_edges=bucket_edges(), level_masks=level_masks())
    arrays, io = {}, {}
    for name, value in data.items():
        value = np.ascontiguousarray(value)
        arrays[f"in_{name}"] = value
        io[name] = nc.dram_tensor(f"in_{name}", value.shape, mybir.dt.from_np(value.dtype), kind="ExternalInput").ap()
    io["out"] = nc.dram_tensor("out", (SEQ, D), F32, kind="ExternalOutput").ap()
    program(nc, io)
    result = run_bass_kernel_spmd(nc, [arrays], core_ids=[0])
    return result.results[0]["out"].reshape(1, SEQ, D)
```
